# Optimizing a Trainium2 kernel written in Bass

```python
import math
import jax, jax.numpy as jnp
from jax import lax
import numpy as np

D_MODEL = 2048
BATCH = 1
SEQ = 256
DEPTH = 1

EPS = 1e-6
D_MIX = D_MODEL
RET_HEADS = 8
RET_DV = D_MIX // (2 * RET_HEADS)
RET_DK = RET_DV // 2
RET_CHUNK = 128
RET_W = RET_HEADS * RET_DV
NSA_HEADS = 8
NSA_GROUPS = 2
NSA_HPG = NSA_HEADS // NSA_GROUPS
NSA_DH = D_MIX // (2 * NSA_HEADS)
NSA_W = NSA_HEADS * NSA_DH
KV_W = NSA_GROUPS * NSA_DH
CMP_LEN = 32
CMP_STRIDE = 16
CMP_HIDDEN = 2 * NSA_DH
SEL_BLOCK = 64
SEL_TOPK = 16
SEL_QCHUNK = 32
WINDOW = 512
WIN_QBLOCK = 128
N_BUCKETS = 32
MAX_DISTANCE = 128
PEER_HEADS = 8
PEER_NKEYS = 128
PEER_N = PEER_NKEYS * PEER_NKEYS
PEER_DQ = 256
PEER_TOPK = 16
PEER_TOKCHUNK = 128
SPLITS = (RET_HEADS * RET_DK, RET_HEADS * RET_DK, RET_W, RET_W, NSA_W, 6 * KV_W, 3 * NSA_HEADS)
IN_COLS = 2 * RET_HEADS * RET_DK + 2 * RET_W + NSA_W + 6 * KV_W + 3 * NSA_HEADS

kernel_name = 'hybrid_retnet_nsa_peer'

def rms_normalize(x):
    xf = x.astype(jnp.float32)
    return (xf * lax.rsqrt(jnp.mean(xf * xf, axis=-1, keepdims=True) + EPS)).astype(x.dtype)

def rmsnorm(x, g):
    return rms_normalize(x) * g

def masked_softmax(s, mask):
    s = jnp.where(mask, s.astype(jnp.float32), -1e30)
    m = jnp.max(s, axis=-1, keepdims=True)
    e = jnp.exp(s - m) * mask
    return e / jnp.maximum(jnp.sum(e, axis=-1, keepdims=True), 1e-30)

def t5_bucket(dist):
    dist = jnp.maximum(dist, 0)
    max_exact = N_BUCKETS // 2
    log_ratio = jnp.log(jnp.maximum(dist, 1).astype(jnp.float32) / max_exact) / math.log(MAX_DISTANCE / max_exact)
    large = jnp.minimum(max_exact + (log_ratio * (N_BUCKETS - max_exact)).astype(jnp.int32), N_BUCKETS - 1)
    return jnp.where(dist < max_exact, dist, large)

def rotary(x, pos):
    half = x.shape[-1] // 2
    inv = 1.0 / (10000.0 ** (jnp.arange(half, dtype=jnp.float32) / half))
    ang = pos.astype(jnp.float32)[:, None] * inv[None, :]
    cos = jnp.cos(ang)[None, :, None, :].astype(x.dtype)
    sin = jnp.sin(ang)[None, :, None, :].astype(x.dtype)
    x1, x2 = x[..., :half], x[..., half:]
    return jnp.concatenate([x1 * cos - x2 * sin, x1 * sin + x2 * cos], axis=-1)

def retention_chunkwise(q, k, v):
    B, T, H, dk = q.shape
    dv = v.shape[-1]
    C = RET_CHUNK
    nc = T // C
    q = q.astype(jnp.float32) * dk ** -0.5
    k = k.astype(jnp.float32)
    v = v.astype(jnp.float32)
    log_g = jnp.log(1.0 - 2.0 ** (-5.0 - jnp.arange(H, dtype=jnp.float32)))
    qc = q.reshape(B, nc, C, H, dk)
    kc = k.reshape(B, nc, C, H, dk)
    vc = v.reshape(B, nc, C, H, dv)
    idx = jnp.arange(C, dtype=jnp.float32)
    diff = idx[:, None] - idx[None, :]
    dmask = jnp.where(diff >= 0, jnp.exp(log_g[:, None, None] * jnp.maximum(diff, 0.0)), 0.0)
    s = jnp.einsum('bcnhd,bcmhd->bchnm', qc, kc) * dmask
    intra = jnp.einsum('bchnm,bcmhe->bcnhe', s, vc)
    zeta = jnp.exp(log_g[:, None] * (C - 1 - idx)[None, :])
    xi = jnp.exp(log_g[:, None] * (idx + 1.0)[None, :])
    kv = jnp.einsum('bcmhd,hm,bcmhe->bchde', kc, zeta, vc)
    decay_c = jnp.exp(log_g * C)[None, :, None, None]

    def step(state, kv_c):
        return state * decay_c + kv_c, state

    _, r_prev = lax.scan(step, jnp.zeros((B, H, dk, dv), jnp.float32), jnp.moveaxis(kv, 1, 0))
    r_prev = jnp.moveaxis(r_prev, 0, 1)
    cross = jnp.einsum('bcnhd,bchde,hn->bcnhe', qc, r_prev, xi)
    return (intra + cross).reshape(B, T, H, dv)

def retention_group(rq, rk, rv, rg, gn_g, pos):
    B, T, _ = rq.shape
    q = rotary(rq.reshape(B, T, RET_HEADS, RET_DK), pos)
    k = rotary(rk.reshape(B, T, RET_HEADS, RET_DK), pos)
    v = rv.reshape(B, T, RET_HEADS, RET_DV)
    y = retention_chunkwise(q, k, v)
    mu = jnp.mean(y, axis=-1, keepdims=True)
    var = jnp.mean(jnp.square(y - mu), axis=-1, keepdims=True)
    y = ((y - mu) * lax.rsqrt(var + EPS)).reshape(B, T, RET_W).astype(rg.dtype) * gn_g
    return jax.nn.silu(rg) * y

def compress(a, pe, w1, w2):
    B, T, G, dh = a.shape
    nc = (T - CMP_LEN) // CMP_STRIDE + 1
    idx = jnp.arange(nc)[:, None] * CMP_STRIDE + jnp.arange(CMP_LEN)[None, :]
    blk = a[:, idx] + pe[:, None, :]
    blk = jnp.moveaxis(blk, 3, 2).reshape(B, nc, G, CMP_LEN * dh)
    return jax.nn.gelu(blk @ w1) @ w2

def cmp_attention(q, kc, vc, rb):
    T = q.shape[1]
    nc = kc.shape[1]
    s = jnp.einsum('btghd,bcgd->bghtc', q, kc)
    end = jnp.arange(nc) * CMP_STRIDE + CMP_LEN - 1
    dist = jnp.arange(T)[:, None] - end[None, :]
    bias = jnp.moveaxis(rb[t5_bucket(dist)], (2, 3), (0, 1))
    p = masked_softmax(s + bias, dist >= 0)
    o = jnp.einsum('bghtc,bcgd->btghd', p.astype(vc.dtype), vc)
    return o, p

def sel_attention(q, k, v, p_cmp, rb):
    B, T = q.shape[:2]
    nsel = T // SEL_BLOCK
    nc = p_cmp.shape[-1]
    topk = min(SEL_TOPK, nsel)
    cs = jnp.arange(nc) * CMP_STRIDE
    js = jnp.arange(nsel) * SEL_BLOCK
    overlap = jnp.clip(jnp.minimum(cs[:, None] + CMP_LEN, js[None, :] + SEL_BLOCK) - jnp.maximum(cs[:, None], js[None, :]), 0, None).astype(jnp.float32) / CMP_LEN
    imp = jnp.einsum('bghtc,cj->bgtj', p_cmp, overlap)
    t = jnp.arange(T)
    j = jnp.arange(nsel)
    cur = t // SEL_BLOCK
    causal = j[None, :] * SEL_BLOCK <= t[:, None]
    forced = (j[None, :] == 0) | (j[None, :] == cur[:, None]) | (j[None, :] == cur[:, None] - 1)
    imp = jnp.where(forced, 1e9, imp)
    imp = jnp.where(causal, imp, -1e9)
    vals, idx = lax.top_k(imp, topk)
    sel_ok = vals > -1e8
    kb = jnp.moveaxis(k.reshape(B, nsel, SEL_BLOCK, NSA_GROUPS, NSA_DH), 3, 1)
    vb = jnp.moveaxis(v.reshape(B, nsel, SEL_BLOCK, NSA_GROUPS, NSA_DH), 3, 1)
    nq = T // SEL_QCHUNK
    qs = jnp.moveaxis(q.reshape(B, nq, SEL_QCHUNK, NSA_GROUPS, NSA_HPG, NSA_DH), 1, 0)
    idx_s = jnp.moveaxis(idx.reshape(B, NSA_GROUPS, nq, SEL_QCHUNK, topk), 2, 0)
    ok_s = jnp.moveaxis(sel_ok.reshape(B, NSA_GROUPS, nq, SEL_QCHUNK, topk), 2, 0)
    bi = jnp.arange(B)[:, None, None, None]
    gi = jnp.arange(NSA_GROUPS)[None, :, None, None]
    gi5 = gi[..., None]
    sb = jnp.arange(SEL_BLOCK)
    n_keys = topk * SEL_BLOCK

    def chunk(args):
        qc, ic, okc, t0 = args
        kg = kb[bi, gi, ic]
        vg = vb[bi, gi, ic]
        tq = t0 + jnp.arange(SEL_QCHUNK)
        kpos = ic[..., None] * SEL_BLOCK + sb
        dist = tq[:, None, None] - kpos
        mask = okc[..., None] & (dist >= 0)
        bias = jnp.moveaxis(rb[t5_bucket(dist), gi5], -1, 2)
        s = jnp.einsum('btghd,bgtksd->bghtks', qc, kg) + bias
        p = masked_softmax(s.reshape(B, NSA_GROUPS, NSA_HPG, SEL_QCHUNK, n_keys), mask.reshape(B, NSA_GROUPS, 1, SEL_QCHUNK, n_keys))
        return jnp.einsum('bghtn,bgtnd->btghd', p.astype(vg.dtype), vg.reshape(B, NSA_GROUPS, SEL_QCHUNK, n_keys, NSA_DH))

    o = lax.map(chunk, (qs, idx_s, ok_s, jnp.arange(nq) * SEL_QCHUNK))
    return jnp.moveaxis(o, 0, 1).reshape(B, T, NSA_GROUPS, NSA_HPG, NSA_DH)

def win_attention(q, k, v, rb):
    B, T = q.shape[:2]
    nb = T // WIN_QBLOCK
    nwin = WINDOW // WIN_QBLOCK + 1
    K = nwin * WIN_QBLOCK
    widx = jnp.arange(nb)[:, None] + jnp.arange(nwin)[None, :]

    def band(a):
        ap = jnp.pad(a, ((0, 0), (WINDOW, 0), (0, 0), (0, 0))).reshape(B, nb + nwin - 1, WIN_QBLOCK, NSA_GROUPS, NSA_DH)
        return jnp.moveaxis(ap[:, widx].reshape(B, nb, K, NSA_GROUPS, NSA_DH), 1, 0)

    kw, vw = band(k), band(v)
    qb = jnp.moveaxis(q.reshape(B, nb, WIN_QBLOCK, NSA_GROUPS, NSA_HPG, NSA_DH), 1, 0)
    ki = jnp.arange(K)
    dist = WINDOW + jnp.arange(WIN_QBLOCK)[:, None] - ki[None, :]
    in_band = (dist >= 0) & (dist < WINDOW)
    bias = jnp.moveaxis(rb[t5_bucket(dist)], (2, 3), (0, 1))

    def block(args):
        qn, kn, vn, n = args
        kpos = n * WIN_QBLOCK - WINDOW + ki
        mask = in_band & (kpos >= 0)[None, :]
        s = jnp.einsum('bqghd,bkgd->bghqk', qn, kn) + bias
        p = masked_softmax(s, mask)
        return jnp.einsum('bghqk,bkgd->bqghd', p.astype(vn.dtype), vn)

    o = lax.map(block, (qb, kw, vw, jnp.arange(nb)))
    return jnp.moveaxis(o, 0, 1).reshape(B, T, NSA_GROUPS, NSA_HPG, NSA_DH)

def nsa_group(nq, nkv, ngate, rel_bias, cmp_pe, cmp_w1, cmp_w2, out_g):
    B, T, _ = nq.shape
    q = nq.reshape(B, T, NSA_GROUPS, NSA_HPG, NSA_DH) * NSA_DH ** -0.5
    kv = nkv.reshape(B, T, 6, NSA_GROUPS, NSA_DH)
    rb = rel_bias.reshape(N_BUCKETS, NSA_GROUPS, NSA_HPG)
    k_cmp = compress(kv[:, :, 0], cmp_pe[0], cmp_w1[0], cmp_w2[0])
    v_cmp = compress(kv[:, :, 1], cmp_pe[1], cmp_w1[1], cmp_w2[1])
    o_cmp, p_cmp = cmp_attention(q, k_cmp, v_cmp, rb)
    o_sel = sel_attention(q, kv[:, :, 2], kv[:, :, 3], p_cmp, rb)
    o_win = win_attention(q, kv[:, :, 4], kv[:, :, 5], rb)
    gate = jax.nn.sigmoid(ngate.reshape(B, T, NSA_GROUPS, NSA_HPG, 3))
    o = gate[..., 0:1] * o_cmp + gate[..., 1:2] * o_sel + gate[..., 2:3] * o_win
    return rms_normalize(o).reshape(B, T, NSA_W) * out_g

def peer_ffn(x, wq, subkeys, u, v):
    B, T, D = x.shape
    n = B * T
    xt = x.reshape(n, D)
    q = (xt @ wq).reshape(n, PEER_HEADS, 2, PEER_DQ // 2)
    s = jnp.einsum('nhpd,pkd->nhpk', q, subkeys)
    sv, si = lax.top_k(s, PEER_TOPK)
    cand = sv[:, :, 0, :, None] + sv[:, :, 1, None, :]
    cidx = si[:, :, 0, :, None] * PEER_NKEYS + si[:, :, 1, None, :]
    cs, ci = lax.top_k(cand.reshape(n, PEER_HEADS, PEER_TOPK * PEER_TOPK), PEER_TOPK)
    eidx = jnp.take_along_axis(cidx.reshape(n, PEER_HEADS, PEER_TOPK * PEER_TOPK), ci, axis=-1)
    gate = jax.nn.softmax(cs.astype(jnp.float32), axis=-1).astype(x.dtype)
    nch = n // PEER_TOKCHUNK

    def chunk(args):
        xc, ec, gc = args
        hid = jax.nn.gelu(jnp.einsum('cd,chkd->chk', xc, u[ec]))
        return jnp.einsum('chk,chkd->cd', gc * hid, v[ec])

    out = lax.map(chunk, (xt.reshape(nch, PEER_TOKCHUNK, D), eidx.reshape(nch, PEER_TOKCHUNK, PEER_HEADS, PEER_TOPK), gate.reshape(nch, PEER_TOKCHUNK, PEER_HEADS, PEER_TOPK)))
    return out.reshape(B, T, D)

def setup_inputs(seed: int = 0) -> dict:
    key = jax.random.key(seed)
    ks = jax.random.split(key, 16)
    nrm = jax.random.normal
    f32 = jnp.float32
    return {
        'x': nrm(ks[0], (BATCH, SEQ, D_MODEL), f32),
        'norm1_g': 1.0 + 0.02 * nrm(ks[1], (DEPTH, D_MODEL), f32),
        'w_in': nrm(ks[2], (DEPTH, D_MODEL, IN_COLS), f32) * D_MODEL ** -0.5,
        'rel_bias': 0.5 * nrm(ks[3], (N_BUCKETS, NSA_HEADS), f32),
        'ret_gn_g': 1.0 + 0.02 * nrm(ks[4], (DEPTH, RET_W), f32),
        'cmp_pe': 0.2 * nrm(ks[5], (DEPTH, 2, CMP_LEN, NSA_DH), f32),
        'cmp_w1': nrm(ks[6], (DEPTH, 2, CMP_LEN * NSA_DH, CMP_HIDDEN), f32) * (CMP_LEN * NSA_DH) ** -0.5,
        'cmp_w2': nrm(ks[7], (DEPTH, 2, CMP_HIDDEN, NSA_DH), f32) * CMP_HIDDEN ** -0.5,
        'nsa_out_g': 1.0 + 0.02 * nrm(ks[8], (DEPTH, NSA_W), f32),
        'w_out': nrm(ks[9], (DEPTH, D_MIX, D_MODEL), f32) * D_MIX ** -0.5,
        'norm2_g': 1.0 + 0.02 * nrm(ks[10], (DEPTH, D_MODEL), f32),
        'peer_wq': nrm(ks[11], (DEPTH, D_MODEL, PEER_HEADS * PEER_DQ), f32) * D_MODEL ** -0.5,
        'peer_subkeys': nrm(ks[12], (DEPTH, 2, PEER_NKEYS, PEER_DQ // 2), f32) * (PEER_DQ // 2) ** -0.5,
        'peer_u': nrm(ks[13], (DEPTH, PEER_N, D_MODEL), f32) * D_MODEL ** -0.5,
        'peer_v': 0.5 * nrm(ks[14], (DEPTH, PEER_N, D_MODEL), f32),
        'norm_f_g': 1.0 + 0.02 * nrm(ks[15], (D_MODEL,), f32),
    }

def reference(x, norm1_g, w_in, rel_bias, ret_gn_g, cmp_pe, cmp_w1, cmp_w2, nsa_out_g, w_out, norm2_g, peer_wq, peer_subkeys, peer_u, peer_v, norm_f_g):
    T = x.shape[1]
    pos = jnp.arange(T)
    offsets = [int(o) for o in np.cumsum(SPLITS)[:-1]]
    h = x
    for l in range(DEPTH):
        xn = rmsnorm(h, norm1_g[l])
        proj = xn @ w_in[l]
        rq, rk, rv, rg, nq, nkv, ngate = jnp.split(proj, offsets, axis=-1)
        ret = retention_group(rq, rk, rv, rg, ret_gn_g[l], pos)
        nsa = nsa_group(nq, nkv, ngate, rel_bias, cmp_pe[l], cmp_w1[l], cmp_w2[l], nsa_out_g[l])
        h = h + jnp.concatenate([ret, nsa], axis=-1) @ w_out[l]
        h = h + peer_ffn(rmsnorm(h, norm2_g[l]), peer_wq[l], peer_subkeys[l], peer_u[l], peer_v[l])
    return rmsnorm(h, norm_f_g)


_drawn_inputs = setup_inputs


def setup_inputs(seed=0):
    import zlib

    import numpy as np

    out = dict(_drawn_inputs(seed))
    spreads = {}
    factors = {}
    for name, (base, spread) in spreads.items():
        noise = np.random.default_rng([zlib.crc32(name.encode()), seed]).standard_normal(out[name].shape)
        drawn = base * np.exp(spread * noise) if base else spread * noise
        out[name] = __import__('jax').numpy.asarray(drawn.astype(out[name].dtype))
    for name, factor in factors.items():
        out[name] = (out[name] * factor).astype(out[name].dtype)
    return out
```

```python
import math
from contextlib import ExitStack

import concourse.bass as bass
import numpy as np
from concourse import mybir

F32 = mybir.dt.float32
F32R = mybir.dt.float32r
U32 = mybir.dt.uint32
ALU = mybir.AluOpType
ACT = mybir.ActivationFunctionType
AX = mybir.AxisListType

P = 128
T = 256
D = 2048
KT = D // P
EPS = 1e-6
RET_HEADS, RET_DK = 8, 64
NSA_HEADS, GROUPS, DH = 8, 2, 128
HPG = NSA_HEADS // GROUPS
CMP_LEN, CMP_STRIDE = 32, 16
NCMP = (T - CMP_LEN) // CMP_STRIDE + 1
CPAD = 16
N_BUCKETS, MAX_DISTANCE = 32, 128
NEG = -1e30
PH, PK, NKEYS = 8, 16, 128
GROUP_J = 8

RQ, RK, RV, RG, NQ, KV = 0, 4, 8, 16, 24, 32
W_IN_TILES = 44
KC, VC, KS, VS, KW, VW = KV, KV + 2, KV + 4, KV + 6, KV + 8, KV + 10

RAW = 4
N_IN = 0
N_CMP = N_IN + W_IN_TILES
N_OUT = N_CMP + 8
N_WQ = N_OUT + KT
N_PEER = N_WQ + KT
HALF = NKEYS // 2
def n_u(half): return N_PEER + 2 * HALF * half
def n_v(half): return n_u(half) + HALF

BIAS_W = 384
ONEHOT_F = 512
SCALE = float(DH) ** -0.5
LOWEST = -3.4e38
ROUTE_GATE = 5 * 32 + 3 + 5 * 16 + 1


def buckets(dist):
    d = np.maximum(dist, 0)
    exact = N_BUCKETS // 2
    ratio = np.log(np.maximum(d, 1).astype(np.float32) / np.float32(exact)) / np.float32(math.log(MAX_DISTANCE / exact))
    large = np.minimum(exact + (ratio * np.float32(N_BUCKETS - exact)).astype(np.int32), N_BUCKETS - 1)
    return np.where(d < exact, d, large)


def onehot_of(dist):
    out = np.zeros((N_BUCKETS + 1, len(dist)), np.float32)
    out[np.where(dist >= 0, buckets(dist), N_BUCKETS), np.arange(len(dist))] = 1.0
    return out


def constants():
    eye = np.eye(P, dtype=np.float32)
    base = np.concatenate([eye, np.ones((P, P), np.float32), np.tile(np.arange(P, dtype=np.float32), (P, 1))], 1)
    center = eye - 1.0 / P
    swap = np.zeros((P, P), np.float32)
    half = RET_DK // 2
    for m in range(P):
        if m % RET_DK < half:
            swap[m + half, m] = -1.0
        else:
            swap[m - half, m] = 1.0
    inv = (1.0 / (np.float32(10000.0) ** (np.arange(half, dtype=np.float32) / np.float32(half)))).astype(np.float32)
    ang = np.arange(T, dtype=np.float32)[None, :] * inv[np.arange(P) % half][:, None]
    hm = np.zeros((P, NSA_HEADS), np.float32)
    for p in range(P):
        if p % CPAD < NCMP:
            hm[p, p // CPAD] = 1.0
    t = np.arange(T).reshape(2, P)
    seen = np.zeros((P, 2, CPAD), np.float32)
    for c in range(NCMP):
        seen[:, :, c] = (t >= c * CMP_STRIDE + CMP_LEN - 1).T
    mid = np.concatenate([center, swap, np.cos(ang), np.sin(ang), hm, seen.reshape(P, 2 * CPAD)], 1).astype(np.float32)
    log_g = np.log(1.0 - 2.0 ** (-5.0 - np.arange(RET_HEADS, dtype=np.float64)))
    diff = np.arange(T)[None, :] - np.arange(P)[:, None]
    decay = np.where(diff >= 0, np.exp(log_g[:, None, None] * np.maximum(diff, 0)), 0.0) * RET_DK ** -0.5
    decay = decay.transpose(1, 0, 2).reshape(P, RET_HEADS * T).astype(np.float32)
    onehots = np.concatenate([onehot_of(T - 1 - np.arange(BIAS_W)), onehot_of(np.arange(ONEHOT_F) - 256)], 1)
    return base, mid, decay, onehots


MID_W = 2 * P + 2 * T + NSA_HEADS + 2 * CPAD


def build(nc, a, out):
    with ExitStack() as ctx:
        def sb(name, shape, dt=F32):
            return ctx.enter_context(nc.sbuf_tensor(name, shape, dt))

        def sem(name):
            return ctx.enter_context(nc.semaphore(name))

        bank = [ctx.enter_context(nc.psum_tensor(f"bank{b}", [P, 512], F32)) for b in range(8)]

        raw = sb("raw", [P, RAW, D])
        hi = sb("hi", [P, 2, D], F32R)
        lo = sb("lo", [P, 2, D], F32R)
        act = sb("act", [P, KT, 2 * T], F32R)
        hT = sb("hT", [P, 4096])
        arena = sb("arena", [P, 16384])
        gs = sb("gs", [P, 2, 2048])
        wm = sb("wm", [P, 2, 2, T], F32R)
        wmt = sb("wmt", [P, 2, T])
        base = sb("base", [P, 3 * P])
        subk = sb("subk", [P, 2, NKEYS])
        gains = sb("gains", [P, 2 * KT + 16])
        gate = sb("gate", [P, 2, 3 * NSA_HEADS])
        small = sb("small", [P, 64])
        rstd = sb("rstd", [P, T])
        ident, ones, iota = base[:, 0:P], base[:, P:2 * P], base[:, 2 * P:3 * P]
        g1, g2 = gains[:, 0:KT], gains[:, KT:2 * KT]
        gn_g, out_g = gains[:, 2 * KT:2 * KT + 8], gains[:, 2 * KT + 8:2 * KT + 16]

        proj = arena[:, 0:W_IN_TILES * T]
        def tile(f, n=1): return proj[:, f * T:(f + n) * T]
        rv_tok = arena[:, 11264:13312].rearrange("p (t n) -> p t n", t=2)
        v_tok = arena[:, 13312:14336].rearrange("p (t n) -> p t n", t=2)
        decay = arena[:, 14336:16384]
        onehots = arena[:, 11264:11264 + BIAS_W + ONEHOT_F]
        rb_wide = arena[:, 12288:13312].rearrange("p (h m) -> p h m", h=NSA_HEADS)
        rb = small[:, 40:48]
        bias = gs[:, :, :].rearrange("p a n -> p (a n)")[:, 0:8 * BIAS_W].rearrange("p (h n) -> p h n", h=8)
        vch = gs[:, :, :].rearrange("p a n -> p (a n)")[:, 3072:4096].rearrange("p (h n) -> p h n", h=8)
        mid = hT[:, 0:MID_W]
        center, swap = mid[:, 0:P], mid[:, P:2 * P]
        cos, sin = mid[:, 2 * P:2 * P + T], mid[:, 2 * P + T:2 * P + 2 * T]
        head_mask = mid[:, 2 * P + 2 * T:2 * P + 2 * T + 8]
        seen = mid[:, MID_W - 2 * CPAD:MID_W].rearrange("p (t c) -> p t c", t=2)
        w2 = hT[:, 832:1344].rearrange("p (k f n) -> p k f n", k=2, f=2)
        hid = hT[:, 1344:1464].rearrange("p (k f n) -> p k f n", k=2, f=2)
        hid_wide = hT[:, 1472:1728].rearrange("p (f n) -> p f n", f=2)
        cbias = hT[:, 1728:1984].rearrange("p (t c h) -> p t c h", t=2, c=CPAD)
        pc = hT[:, 1984:2240].rearrange("p (t h c) -> p t h c", t=2, h=8)
        pcT = hT[:, 2240:2496]
        kc = hT[:, 2496:2528]
        pw = hT[:, 2560:3328].rearrange("p (s n) -> p s n", s=2)
        ptw = hT[:, 3328:4096].rearrange("p (s n) -> p s n", s=2)
        wg = arena[:, 4096:4096 + KT * 24].rearrange("p (k n) -> p k n", k=KT)
        wg_r = wm[:, :, :, :].rearrange("p a b n -> p (a b n)")[:, 0:KT * 48].rearrange("p (k n) -> p k n", k=KT)
        act_flat = act[:, :, :].rearrange("p k n -> p (k n)")
        blk_r = act_flat[:, 0:3840].rearrange("p (k l n) -> p k l n", k=2, l=CMP_LEN)
        blk = arena[:, RV * T:RV * T + 1920].rearrange("p (k l n) -> p k l n", k=2, l=CMP_LEN)

        rows_dram = nc.dram_tensor("bias_rows", (NSA_HEADS, P, BIAS_W), F32, kind="Internal").ap()
        gate_dram = nc.dram_tensor("gate_matrix", (NKEYS // GROUP_J, P, T, GROUP_J), F32, kind="Internal").ap()

        xn = arena[:, 0:4096].rearrange("p (k t) -> p k t", k=KT)
        qT = arena[:, 4096:8192]
        cand = arena[:, 4096:8192].rearrange("p (t h a b) -> p t h a b", t=2, h=PH, a=PK)
        pick = arena[:, 0:4096].rearrange("p (t n a) -> p t n a", t=2, a=PK)
        sc = arena[:, 8192:12288].rearrange("p (t g k) -> p t g k", t=2, g=2 * PH)
        top = arena[:, 12288:12800].rearrange("p (t g k) -> p t g k", t=2, g=2 * PH)
        top_i = arena[:, 12800:13312].bitcast(U32).rearrange("p (t g k) -> p t g k", t=2, g=2 * PH)
        top_f = arena[:, 13312:13824].rearrange("p (t h s k) -> p t h s k", t=2, h=PH, s=2)
        cs = arena[:, 13824:14080].rearrange("p (t h k) -> p t h k", t=2, h=PH)
        ci = arena[:, 14080:14336].bitcast(U32)
        cab = arena[:, 14336:14848].rearrange("p (s n) -> p s n", s=2)
        cab_u = arena[:, 14336:14848].bitcast(U32).rearrange("p (s n) -> p s n", s=2)
        choice = arena[:, 14848:15616].rearrange("p (s t n) -> p s t n", s=3, t=2)
        choiceT = arena[:, 15616:16384].rearrange("p (s n) -> p s n", s=3)
        onehot = arena[:, 0:4096].rearrange("p (b s n j) -> p b s n j", b=2, s=2, n=8)

        raw_loaded = [sem(f"raw_loaded{s}") for s in range(RAW)]
        hi_ready, lo_ready, block_done = sem("hi_ready"), sem("lo_ready"), sem("block_done")
        acc_evacuated = sem("acc_evacuated")
        x_loaded, base_loaded, small_loaded = sem("x_loaded"), sem("base_loaded"), sem("small_loaded")
        onehots_loaded, mid_loaded, decay_loaded = sem("onehots_loaded"), sem("mid_loaded"), sem("decay_loaded")
        xres_loaded = sem("xres_loaded")
        sq_ready, ss_ready, std_ready, rstd_ready = sem("sq_ready"), sem("ss_ready"), sem("std_ready"), sem("rstd_ready")
        xn_ready, act_hi_ready, act_lo_ready = sem("xn_ready"), sem("act_hi_ready"), sem("act_lo_ready")
        rb_ready, rb_wide_ready, rows_ready, rows_copied = sem("rb_ready"), sem("rb_wide_ready"), sem("rows_ready"), sem("rows_copied")
        rows_stored, bias_loaded, cbias_ready, cbias_copied = sem("rows_stored"), sem("bias_loaded"), sem("cbias_ready"), sem("cbias_copied")
        wg_hi_ready, wg_lo_ready, gate_acc, gate_exp, gate_step, gate_ready = (
            sem(s) for s in ("wg_hi_ready", "wg_lo_ready", "gate_acc", "gate_exp", "gate_step", "gate_ready"))
        v_turned, v_copied = sem("v_turned"), sem("v_copied")
        swapped, rot_sin, rot_cos, rotated = sem("swapped"), sem("rot_sin"), sem("rot_cos"), sem("rotated")
        blk_ready, blk_hi, blk_lo, hid_ready = sem("blk_ready"), sem("blk_hi"), sem("blk_lo"), sem("hid_ready")
        kc_acc, kc_copied, wide_zero, wide_ready, vc_acc, vch_ready = (
            sem(s) for s in ("kc_acc", "kc_copied", "wide_zero", "wide_ready", "vc_acc", "vch_ready"))
        cs_acc, cstep, cexp, pc_ready, pcT_acc, pcT_copied = (
            sem(s) for s in ("cs_acc", "cstep", "cexp", "pc_ready", "pcT_acc", "pcT_copied"))
        s_acc, s_biased, s_max, s_nmax, p_exp, p_rec, p_coef, p_ready = (
            sem(s) for s in ("s_acc", "s_biased", "s_max", "s_nmax", "p_exp", "p_rec", "p_coef", "p_ready"))
        pT_acc, pT_copied, pv_done, o_copied = sem("pT_acc"), sem("pT_copied"), sem("pv_done"), sem("o_copied")
        r_acc, r_decayed, y_acc, y_copied = sem("r_acc"), sem("r_decayed"), sem("y_acc"), sem("y_copied")
        osq_ready, oss_acc, ostd, orstd, mixed = (sem(s) for s in ("osq_ready", "oss_acc", "ostd", "orstd", "mixed"))
        yc_acc, ysq_ready, yss_acc, ystd, yrstd = (sem(s) for s in ("yc_acc", "ysq_ready", "yss_acc", "ystd", "yrstd"))
        silu_exp, silu_step, ynorm = sem("silu_exp"), sem("silu_step"), sem("ynorm")
        q_scores, q_copied, route, route_exp, choices_ready = (
            sem(s) for s in ("q_scores", "q_copied", "route", "route_exp", "choices_ready"))
        ch_turned, ch_copied, onehot_ready, gate_rows, gate_evac, choice_step = (
            sem(s) for s in ("ch_turned", "ch_copied", "onehot_ready", "gate_rows", "gate_evac", "choice_step"))
        gate_stored = [sem(f"gate_stored{s}") for s in range(2)]
        gate_loaded = [sem(f"gate_loaded{s}") for s in range(2)]
        seeded, gated, wm_hi, wm_lo = sem("seeded"), sem("gated"), sem("wm_hi"), sem("wm_lo")
        half_kept, fin_sq, fin_std, fin_rstd, fin_ready, gf_loaded, out_stored = (
            sem(s) for s in ("half_kept", "fin_sq", "fin_std", "fin_rstd", "fin_ready", "gf_loaded", "out_stored"))

        eps_ready = sem("eps_ready")
        eps = small[:, 32:33]
        silu_e = arena[:, 11264:13312]

        def stats(u):
            return small[:, 48 + 8 * (u % 2):56 + 8 * (u % 2)]

        block = ctx.enter_context(nc.Block())

        def raw_count(n):
            return 4 * n + 16

        @block.sync
        def _(sp):
            x_src = a["xT"]
            sp.dma_start(hT[:, :], x_src).then_inc(x_loaded, 16)
            sp.dma_start(base[:, :], a["base"]).then_inc(base_loaded, 16)
            sp.dma_start(gains[:, :], a["gains"]).then_inc(small_loaded, 16)
            sp.dma_start(wg, a["w_gate"]).then_inc(small_loaded, 16)
            sp.dma_start(rb[0:N_BUCKETS, :], a["rel_bias"]).then_inc(small_loaded, 16)
            sp.dma_start(onehots[0:N_BUCKETS + 1, :], a["onehots"]).then_inc(onehots_loaded, 16)
            sp.dma_start(subk[:, :, :], a["subkeys"]).then_inc(small_loaded, 16)
            sp.dma_start(decay, a["decay"]).then_inc(decay_loaded, 16)

            def load(src, n, s):
                sp.wait_ge(hi_ready, n - RAW + 1)
                sp.wait_ge(lo_ready, n - RAW + 1)
                sp.dma_start(raw[:, s, :], src).then_inc(raw_loaded[s], 16)

            for n in range(RAW):
                sp.dma_start(raw[:, n, :], a["w_in"][n]).then_inc(raw_loaded[n], 16)
            with sp.Fori(1, W_IN_TILES // RAW) as lap:
                i = lap * RAW
                for s in range(RAW):
                    load(a["w_in"][i + s], N_IN + i + s, s)
            sp.wait_ge(xn_ready, KT)
            sp.dma_start(mid, a["mid"]).then_inc(mid_loaded, 16)
            sp.dma_start(hT[:, 832:1344], a["cmp_w2"]).then_inc(mid_loaded, 16)
            sp.dma_start(wmt[:, :, :].rearrange("p a n -> p (a n)")[:, 0:2 * CMP_LEN], a["cmp_pe"]).then_inc(mid_loaded, 16)
            sp.wait_ge(rows_copied, NSA_HEADS)
            sp.dma_start(rows_dram.rearrange("h p n -> p h n"), bias).then_inc(rows_stored, 16)
            sp.wait_ge(rows_stored, 16)
            for part in range(2):
                first = P * (1 - part)
                skew = bass.AP(tensor=rows_dram.tensor, offset=P - 1 + first,
                               ap=[[BIAS_W - 1, P], [P * BIAS_W, NSA_HEADS], [1, P * (part + 1)]])
                sp.dma_start(bias[:, :, P * part:P * part + P * (part + 1)], skew).then_inc(bias_loaded, 16)
            with sp.Fori(0, 8 // RAW) as lap:
                i = lap * RAW
                for s in range(RAW):
                    load(a["cmp_w1"][i + s], N_CMP + i + s, s)
            for s in range(RAW):
                load(a["w_out"][s], N_OUT + s, s)
            sp.wait_ge(mixed, 16)
            sp.wait_ge(y_acc, RET_HEADS)
            sp.dma_start(hT[:, :], x_src).then_inc(xres_loaded, 16)
            with sp.Fori(1, KT // RAW) as lap:
                i = lap * RAW
                for s in range(RAW):
                    load(a["w_out"][i + s], N_OUT + i + s, s)
            with sp.Fori(0, KT // RAW) as lap:
                i = lap * RAW
                for s in range(RAW):
                    load(a["wq"][i + s], N_WQ + i + s, s)
            for half in range(2):
                with sp.Fori(0, HALF // RAW) as lap:
                    i = lap * RAW
                    for s in range(RAW):
                        load(a["u"][i + (HALF * half + s)], n_u(half) + i + s, s)

                def v_group(q, g):
                    if half or not isinstance(q, int):
                        sp.wait_ge(gated, GROUP_J * q + (HALF * half - GROUP_J))
                    sp.dma_start(gs[:, g, :], gate_dram[q + (HALF // GROUP_J * half)].rearrange("i t j -> i (t j)")
                                 ).then_inc(gate_loaded[g], 16)
                    for r in range(GROUP_J):
                        load(a["v"][:, GROUP_J * q + (HALF * half + r), :], n_v(half) + r + GROUP_J * q, r % RAW)

                if half == 0:
                    for s in range(2):
                        sp.wait_ge(gate_stored[s], 16 * (T // 32))
                    for g in range(2):
                        v_group(g, g)
                with sp.Fori(1 if half == 0 else 0, (HALF // GROUP_J) // 2) as lap:
                    q = lap * 2
                    for g in range(2):
                        v_group(q + g, g)
            sp.wait_ge(seeded, 2)
            sp.dma_start(hT[:, 0:D], a["norm_f"]).then_inc(gf_loaded, 16)
            for tt in range(2):
                sp.wait_ge(fin_ready, 4 * (tt + 1))
                sp.dma_start(out[tt * P:(tt + 1) * P, :], arena[:, tt * D:(tt + 1) * D]).then_inc(out_stored, 16)
            sp.wait_ge(out_stored, 32)

        @block.gpsimd
        def _(pool):
            with pool.Fori(0, T // 32) as lap:
                for s in range(2):
                    pool.wait_ge(gate_evac, 4 * lap + (2 * s + 2))
                    pool.dma_start(gate_dram.rearrange("g i t j -> i g (t j)")[:, :, bass.ds((32 * lap + 16 * s) * GROUP_J, 16 * GROUP_J)],
                                   gs[:, s, :].rearrange("p (g n) -> p g n", g=NKEYS // GROUP_J)).then_inc(gate_stored[s], 16)

        @block.tensor
        def _(pe):
            def product(dst, s, k, mh, ml, first, last):
                wh, wl = hi[:, s, k * P:(k + 1) * P], lo[:, s, k * P:(k + 1) * P]
                nc.tensor.matmul(dst, wh, mh, start=first, stop=False)
                nc.tensor.matmul(dst, wh, ml, start=False, stop=False)
                return nc.tensor.matmul(dst, wl, mh, start=False, stop=last)

            def weights_block(n, s, e):
                pe.wait_ge(hi_ready, n + 1)
                pe.wait_ge(lo_ready, n + 1)
                if not (isinstance(e, int) and e < 2):
                    pe.wait_ge(acc_evacuated, e - 1)
                for k in range(KT):
                    last = product(bank[s % 2][:, 0:T], s % 2, k, act[:, k, 0:T], act[:, k, T:2 * T], k == 0, k == KT - 1)
                last.then_inc(block_done, 1)

            def square_sums(count):
                pe.wait_ge(sq_ready, count)
                for k in range(KT):
                    last = nc.tensor.matmul(bank[7][:, 0:T], ones, xn[:, k, :], start=(k == 0), stop=(k == KT - 1))
                last.then_inc(ss_ready, 1)

            pe.wait_ge(base_loaded, 16)
            square_sums(1)
            pe.wait_ge(rb_wide_ready, 1)
            pe.wait_ge(onehots_loaded, 16)
            rows = N_BUCKETS + 1
            for h in range(NSA_HEADS):
                if h >= 4:
                    pe.wait_ge(rows_copied, h - 3)
                nc.tensor.matmul(bank[2 + h % 4][:, 0:BIAS_W], rb_wide[0:rows, h, :], onehots[0:rows, 0:BIAS_W],
                                 start=True, stop=True).then_inc(rows_ready, 1)
            for tt in range(2):
                for c in range(NCMP):
                    z = BIAS_W + 256 + tt * P - CMP_STRIDE * c - (CMP_LEN - 1)
                    at = (tt * CPAD + c) * 8
                    last = nc.tensor.matmul(bank[6][:, at:at + 8], onehots[0:rows, z:z + P], rb[0:rows, :],
                                            start=True, stop=True)
            last.then_inc(cbias_ready, 1)

            pe.wait_ge(act_hi_ready, 1)
            pe.wait_ge(act_lo_ready, 1)
            for n in range(RAW):
                weights_block(n, n, n)
            with pe.Fori(1, W_IN_TILES // RAW) as lap:
                i = lap * RAW
                for s in range(RAW):
                    weights_block(i + s, s, i + s)
            pe.wait_ge(wg_hi_ready, 1)
            pe.wait_ge(wg_lo_ready, 1)
            pe.wait_ge(cbias_copied, 1)
            for tt in range(2):
                dst = bank[6][:, tt * 24:(tt + 1) * 24]
                for k in range(KT):
                    xh, xl = act[:, k, tt * P:(tt + 1) * P], act[:, k, T + tt * P:T + (tt + 1) * P]
                    nc.tensor.matmul(dst, xh, wg_r[:, k, 0:24], start=(k == 0), stop=False)
                    nc.tensor.matmul(dst, xh, wg_r[:, k, 24:48], start=False, stop=False)
                    last = nc.tensor.matmul(dst, xl, wg_r[:, k, 0:24], start=False, stop=(k == KT - 1))
            last.then_inc(gate_acc, 1)

            pe.wait_ge(acc_evacuated, W_IN_TILES)
            pe.wait_ge(rows_copied, NSA_HEADS)
            pe.wait_ge(std_ready, 1)
            for x in range(6):
                tt = (x // 2 if x < 4 else x - 4)
                tiles = [RV + 4 * (x % 2) + j for j in range(4)] if x < 4 else [VS, VS + 1, VW, VW + 1]
                if x == 4:
                    pe.wait_ge(gate_exp, 1)
                for j, f in enumerate(tiles):
                    last = nc.tensor.transpose(bank[2 + x][:, j * P:(j + 1) * P], tile(f)[:, tt * P:(tt + 1) * P], ident)
                last.then_inc(v_turned, 1)
            pe.wait_ge(mid_loaded, 48)
            for i in range(4):
                pe.wait_ge(v_copied, i + 1)
                nc.tensor.matmul(bank[2 + i][:, :], swap, tile(2 * i, 2), start=True, stop=True).then_inc(swapped, 1)

            pe.wait_ge(blk_hi, 1)
            pe.wait_ge(blk_lo, 1)
            for b in range(8):
                kind, lh, e = b // 4, b % 2, b // 2
                pe.wait_ge(hi_ready, N_CMP + b + 1)
                pe.wait_ge(lo_ready, N_CMP + b + 1)
                if lh == 0 and e >= 2:
                    pe.wait_ge(acc_evacuated, W_IN_TILES + e - 1)
                for k in range(16):
                    m = blk_r[:, kind, lh * 16 + k, :]
                    last = product(bank[e % 2][:, 0:2 * NCMP], b % 2, k, m[:, 0:30], m[:, 30:60],
                                   lh == 0 and k == 0, lh == 1 and k == 15)
                last.then_inc(block_done, 1)
            pe.wait_ge(acc_evacuated, W_IN_TILES + 4)
            pe.wait_ge(rot_sin, 4)
            for f in range(2):
                last = nc.tensor.matmul(bank[4][:, 0:30], w2[:, 0, f, :], hid[:, 0, f, :], start=(f == 0), stop=(f == 1))
            last.then_inc(kc_acc, 1)
            pe.wait_ge(wide_ready, 2)
            for f in range(2):
                last = nc.tensor.matmul(bank[5][:, 0:DH], hid_wide[:, f, :], w2[:, 1, f, :], start=(f == 0), stop=(f == 1))
            last.then_inc(vc_acc, 1)
            pe.wait_ge(kc_copied, 1)
            pe.wait_ge(v_copied, 6)
            for tt in range(2):
                for h in range(NSA_HEADS):
                    at, g = (tt * 8 + h) * CPAD, h // HPG
                    last = nc.tensor.matmul(bank[6][:, at:at + NCMP], tile(NQ + h)[:, tt * P:(tt + 1) * P],
                                            kc[:, g * NCMP:(g + 1) * NCMP], start=True, stop=True)
            last.then_inc(cs_acc, 1)

            def scores(u):
                h, kt = u // 2, (KS, KW)[u % 2] + u // 2 // HPG
                if u >= 2:
                    pe.wait_ge(s_biased, u - 1)
                q, dst = tile(NQ + h), bank[2 + u % 2]
                nc.tensor.matmul(dst[:, 0:P], q[:, 0:P], tile(kt)[:, 0:P], start=True, stop=True)
                nc.tensor.matmul(dst[:, P:3 * P], q[:, P:T], tile(kt), start=True, stop=True).then_inc(s_acc, 1)

            def turn(u):
                pe.wait_ge(p_ready, u + 1)
                if u >= 2:
                    pe.wait_ge(pT_copied, u - 1)
                for j in range(3):
                    last = nc.tensor.transpose(bank[4 + u % 2][:, j * P:(j + 1) * P], pw[:, u % 2, j * P:(j + 1) * P], ident)
                last.then_inc(pT_acc, 1)

            def weigh(u):
                h, branch = u // 2, u % 2
                g, dst = h // HPG, bank[6 + h % 2]
                at = branch * T + g * DH
                if branch == 0:
                    if h >= 2:
                        pe.wait_ge(o_copied, h - 1)
                    nc.tensor.matmul(dst[:, 0:T], vch[:, h, :], pcT, start=True, stop=False)
                pe.wait_ge(pT_copied, u + 1)
                nc.tensor.matmul(dst[:, 0:T], v_tok[:, 0, at:at + DH], ptw[:, u % 2, 0:T], start=False, stop=False)
                nc.tensor.matmul(dst[:, P:T], v_tok[:, 1, at:at + DH], ptw[:, u % 2, T:3 * P],
                                 start=False, stop=(branch == 1)).then_inc(pv_done, 1)

            pe.wait_ge(kc_copied, 1)
            scores(0)
            scores(1)
            pe.wait_ge(pc_ready, 1)
            for tt in range(2):
                last = nc.tensor.transpose(bank[7][:, tt * P:(tt + 1) * P], pc[:, tt, :, :].rearrange("p h c -> p (h c)"), ident)
            last.then_inc(pcT_acc, 1)
            pe.wait_ge(pcT_copied, 1)
            pe.wait_ge(vch_ready, NSA_HEADS)
            units = 2 * NSA_HEADS
            for u in range(units):
                turn(u)
                if u >= 1:
                    weigh(u - 1)
                if u + 2 < units:
                    scores(u + 2)
            weigh(units - 1)

            pe.wait_ge(rotated, 4)
            pe.wait_ge(s_biased, units)
            pe.wait_ge(pT_copied, units)

            def r_scores(h):
                part = slice(RET_DK * (h % 2), RET_DK * (h % 2 + 1))
                q, k, dst = tile(RQ + h // 2)[part, :], tile(RK + h // 2)[part, :], bank[2 + h % 2]
                if h >= 2:
                    pe.wait_ge(r_decayed, h - 1)
                nc.tensor.matmul(dst[:, 0:T], k[:, 0:P], q, start=True, stop=True)
                nc.tensor.matmul(dst[:, T:3 * P], k[:, P:T], q[:, P:T], start=True, stop=True).then_inc(r_acc, 1)

            r_scores(0)
            for h in range(RET_HEADS):
                if h + 1 < RET_HEADS:
                    r_scores(h + 1)
                pe.wait_ge(r_decayed, h + 1)
                if h >= 2:
                    pe.wait_ge(y_copied, h - 1)
                dst = bank[4 + h % 2]
                nc.tensor.matmul(dst[:, 0:T], rv_tok[:, 0, h * P:(h + 1) * P], pw[:, h % 2, 0:T], start=True, stop=False)
                nc.tensor.matmul(dst[:, P:T], rv_tok[:, 1, h * P:(h + 1) * P], pw[:, h % 2, T:3 * P],
                                 start=False, stop=True).then_inc(y_acc, 1)

            pe.wait_ge(osq_ready, 1)
            pe.wait_ge(y_copied, RET_HEADS)
            for c in range(4):
                nc.tensor.matmul(bank[2 + c][:, :], ones, tile(KV + 2 * c, 2), start=True, stop=True).then_inc(oss_acc, 1)
            pe.wait_ge(o_copied, NSA_HEADS)
            for c in range(4):
                nc.tensor.matmul(bank[(6 + c) % 8][:, :], center, tile(RV + 2 * c, 2), start=True, stop=True).then_inc(yc_acc, 1)
            for c in range(4):
                pe.wait_ge(ysq_ready, c + 1)
                pe.wait_ge(ostd, c + 1)
                nc.tensor.matmul(bank[2 + c][:, :], ones, tile(2 * c, 2), start=True, stop=True).then_inc(yss_acc, 1)

            pe.wait_ge(act_hi_ready, 3)
            pe.wait_ge(act_lo_ready, 3)
            with pe.Fori(0, KT // RAW) as lap:
                i = lap * RAW
                for s in range(RAW):
                    weights_block(N_OUT + i + s, s, W_IN_TILES + 4 + i + s)
            pe.wait_ge(ystd, 4)
            square_sums(2)
            pe.wait_ge(act_hi_ready, 4)
            pe.wait_ge(act_lo_ready, 4)
            with pe.Fori(0, KT // RAW) as lap:
                i = lap * RAW
                for s in range(RAW):
                    weights_block(N_WQ + i + s, s, W_IN_TILES + 4 + KT + i + s)
            pe.wait_ge(acc_evacuated, W_IN_TILES + 4 + 2 * KT)
            pe.wait_ge(small_loaded, 64)
            for tt in range(2):
                for g in range(2 * PH):
                    last = nc.tensor.matmul(bank[tt * 4 + g // 4][:, (g % 4) * P:(g % 4 + 1) * P],
                                            qT[:, g * T + tt * P:g * T + (tt + 1) * P], subk[:, g % 2, :], start=True, stop=True)
                    if g % 4 == 3:
                        last.then_inc(q_scores, 1)

            pe.wait_ge(choices_ready, 3)
            pe.wait_ge(q_copied, 8)
            for x in range(6):
                last = nc.tensor.transpose(bank[x // 4][:, (x % 4) * P:(x % 4 + 1) * P], choice[:, x // 2, x % 2, :], ident)
            last.then_inc(ch_turned, 1)
            pe.wait_ge(ch_copied, 2)

            def gate_batch(b, r):
                pe.wait_ge(onehot_ready, b + 1)
                if not (isinstance(b, int) and b < 2):
                    pe.wait_ge(gate_evac, b - 1)
                for t in range(8):
                    last = nc.tensor.matmul(bank[2 * (r % 2) + t // 4][:, (t % 4) * P:(t % 4 + 1) * P],
                                            onehot[:, r % 2, 0, t, :], onehot[:, r % 2, 1, t, :], start=True, stop=True)
                last.then_inc(gate_rows, 1)

            for b in range(4):
                gate_batch(b, b)
            with pe.Fori(1, (T // 8) // 4) as lap:
                i = lap * 4
                for r in range(4):
                    gate_batch(i + r, r)
            pe.wait_ge(gate_evac, T // 8)

            e_peer = W_IN_TILES + 4 + 2 * KT
            for half in range(2):
                if half:
                    pe.wait_ge(half_kept, 8)
                with pe.Fori(0, HALF // RAW) as lap:
                    i = lap * RAW
                    for s in range(RAW):
                        weights_block(n_u(half) + i + s, s, e_peer + HALF * half + i + s)
                pe.wait_ge(acc_evacuated, e_peer + HALF * (half + 1))
                for b in range(8):
                    tt, dc = b // 4, b % 4
                    if half == 0:
                        for j in range(4):
                            last = nc.tensor.matmul(bank[b][:, j * P:(j + 1) * P],
                                                    hT[:, (4 * dc + j) * T + tt * P:(4 * dc + j) * T + (tt + 1) * P], ident,
                                                    start=(j == 0), stop=False, skip_group_check=True)
                    else:
                        last = nc.tensor.matmul(bank[b][:, :], ident, hT[:, tt * D + dc * 512:tt * D + (dc + 1) * 512],
                                                start=True, stop=False, skip_group_check=True)
                last.then_inc(seeded, 1)

                def v_block(n, m, s, closing=False):
                    pe.wait_ge(hi_ready, n + 1)
                    pe.wait_ge(lo_ready, n + 1)
                    pe.wait_ge(wm_hi, m + 1)
                    pe.wait_ge(wm_lo, m + 1)
                    w, vh, vl = wm[:, s % 2, :, :], hi[:, s % 2, :], lo[:, s % 2, :]
                    for tt in range(2):
                        for part, moving in ((0, vl), (0, vh), (1, vh)):
                            for dc in range(4):
                                last = nc.tensor.matmul(bank[tt * 4 + dc][:, :], w[:, part, tt * P:(tt + 1) * P],
                                                        moving[:, dc * 512:(dc + 1) * 512], start=False,
                                                        stop=closing and part == 1, skip_group_check=True)
                    last.then_inc(block_done, 1)

                with pe.Fori(0, (HALF - RAW) // RAW) as lap:
                    i = lap * RAW
                    for s in range(RAW):
                        v_block(n_v(half) + i + s, HALF * half + i + s, s)
                for s in range(RAW):
                    m = HALF - RAW + s
                    v_block(n_v(half) + m, HALF * half + m, s, closing=(s == RAW - 1))

        @block.scalar
        def _(ac):
            def round_block(n, s):
                ac.wait_ge(raw_loaded[s], raw_count(n - s))
                if not (isinstance(n, int) and n < 2):
                    ac.wait_ge(block_done, n - 1)
                nc.scalar.activation(hi[:, s % 2, :], raw[:, s, :], ACT.Copy).then_inc(hi_ready, 1)

            def evacuate(n, s, dst, func=ACT.Copy, width=T):
                ac.wait_ge(block_done, n + 1)
                nc.scalar.activation(dst, bank[s % 2][:, 0:width], func).then_inc(acc_evacuated, 1)

            def normalise(count):
                nc.scalar.activation(xn.rearrange("p k t -> p (k t)"), hT[:, :], ACT.Square).then_inc(sq_ready, 1)
                ac.wait_ge(ss_ready, count)
                nc.scalar.activation(rstd[:, :], bank[7][:, 0:T], ACT.Sqrt, bias=eps, scale=1.0 / D).then_inc(std_ready, 1)
                ac.wait_ge(xn_ready, KT * count)
                nc.scalar.activation(act[:, :, 0:T], xn, ACT.Copy).then_inc(act_hi_ready, 1)

            ac.wait_ge(x_loaded, 16)
            ac.wait_ge(eps_ready, 1)
            normalise(1)
            ac.wait_ge(small_loaded, 64)
            nc.scalar.activation(wg_r[:, :, 0:24], wg, ACT.Copy).then_inc(wg_hi_ready, 1)
            for h in range(NSA_HEADS):
                ac.wait_ge(rows_ready, h + 1)
                nc.scalar.activation(bias[:, h, :], bank[2 + h % 4][:, 0:BIAS_W], ACT.Copy).then_inc(rows_copied, 1)
            ac.wait_ge(act_lo_ready, 1)
            ac.wait_ge(wg_lo_ready, 1)
            for n in range(RAW):
                round_block(n, n)
                if n:
                    evacuate(n - 1, n - 1, tile(n - 1))
            with ac.Fori(1, W_IN_TILES // RAW) as lap:
                i = lap * RAW
                for s in range(RAW):
                    round_block(i + s, s)
                    evacuate(i + (s - 1), s - 1, proj[:, bass.ds(i * T + (s - 1) * T, T)])
            evacuate(W_IN_TILES - 1, W_IN_TILES - 1, tile(W_IN_TILES - 1))
            ac.wait_ge(gate_acc, 1)
            nc.scalar.activation(gate[:, :, :].rearrange("p t n -> p (t n)"),
                                 bank[6][:, 0:48], ACT.Exp, scale=-1.0).then_inc(gate_exp, 1)
            ac.wait_ge(cbias_copied, 1)
            for x in range(6):
                ac.wait_ge(v_turned, x + 1)
                dst = rv_tok[:, x // 2, (x % 2) * 512:(x % 2 + 1) * 512] if x < 4 else v_tok[:, x - 4, :]
                nc.scalar.activation(dst, bank[2 + x][:, :], ACT.Copy).then_inc(v_copied, 1)
            ac.wait_ge(blk_ready, 8)
            nc.scalar.activation(blk_r[:, :, :, 0:30].rearrange("p k l n -> p (k l) n"),
                                 blk.rearrange("p k l n -> p (k l) n"), ACT.Copy).then_inc(blk_hi, 1)

            def gelu_cmp(e):
                ac.wait_ge(block_done, N_CMP + 2 * e + 2)
                nc.scalar.activation(hid[:, e // 2, e % 2, :], bank[e % 2][:, 0:30], ACT.Gelu_apprx_tanh).then_inc(acc_evacuated, 1)

            for b in range(8):
                round_block(N_CMP + b, b % RAW)
                if b >= 3 and b % 2:
                    gelu_cmp((b - 3) // 2)
            gelu_cmp(3)
            ac.wait_ge(kc_acc, 1)
            nc.scalar.activation(kc[:, 0:30], bank[4][:, 0:30], ACT.Copy).then_inc(kc_copied, 1)
            ac.wait_ge(cstep, 5)
            nc.scalar.activation(pc[:, :, :, 0:NCMP].rearrange("p t h c -> p (t h) c"),
                                 pc[:, :, :, 0:NCMP].rearrange("p t h c -> p (t h) c"), ACT.Exp).then_inc(cexp, 1)

            def exps(u):
                ac.wait_ge(s_nmax, u + 1)
                st = stats(u)
                nc.scalar.activation(pw[:, u % 2, 0:P], pw[:, u % 2, 0:P], ACT.Exp, bias=st[:, 2:3], accum_out=st[:, 4:5])
                nc.scalar.activation(pw[:, u % 2, P:3 * P], pw[:, u % 2, P:3 * P], ACT.Exp, bias=st[:, 3:4],
                                     accum_out=st[:, 5:6]).then_inc(p_exp, 1)

            def copy_pT(u):
                ac.wait_ge(pT_acc, u + 1)
                if u >= 2:
                    ac.wait_ge(pv_done, u - 1)
                nc.scalar.activation(ptw[:, u % 2, :], bank[4 + u % 2][:, 0:3 * P], ACT.Copy).then_inc(pT_copied, 1)

            def copy_o(h):
                ac.wait_ge(pv_done, 2 * h + 2)
                nc.scalar.activation(tile(NQ + h), bank[6 + h % 2][:, 0:T], ACT.Copy).then_inc(o_copied, 1)

            exps(0)
            ac.wait_ge(pcT_acc, 1)
            nc.scalar.activation(pcT, bank[7][:, 0:T], ACT.Copy).then_inc(pcT_copied, 1)
            units = 2 * NSA_HEADS
            for u in range(units):
                if u + 1 < units:
                    exps(u + 1)
                copy_pT(u)
                if u % 2 == 0 and u >= 2:
                    copy_o(u // 2 - 1)
            copy_o(NSA_HEADS - 1)
            for h in range(RET_HEADS):
                ac.wait_ge(y_acc, h + 1)
                nc.scalar.activation(tile(RV + h), bank[4 + h % 2][:, 0:T], ACT.Copy).then_inc(y_copied, 1)
            ac.wait_ge(o_copied, NSA_HEADS)
            nc.scalar.activation(tile(KV, 8), tile(NQ, 8), ACT.Square).then_inc(osq_ready, 1)
            nc.scalar.activation(silu_e, tile(RG, 8), ACT.Exp, scale=-1.0).then_inc(silu_exp, 1)
            for c in range(4):
                ac.wait_ge(oss_acc, c + 1)
                nc.scalar.activation(tile(KV + 2 * c, 2), bank[2 + c][:, :], ACT.Sqrt, bias=eps, scale=1.0 / DH).then_inc(ostd, 1)
            for c in range(4):
                ac.wait_ge(yc_acc, c + 1)
                nc.scalar.activation(tile(2 * c, 2), bank[(6 + c) % 8][:, :], ACT.Square).then_inc(ysq_ready, 1)
            for c in range(4):
                ac.wait_ge(yss_acc, c + 1)
                nc.scalar.activation(tile(2 * c, 2), bank[2 + c][:, :], ACT.Sqrt, bias=eps, scale=1.0 / P).then_inc(ystd, 1)
            ac.wait_ge(mixed, 8)
            nc.scalar.activation(act[:, 8:16, 0:T], tile(NQ, 8).rearrange("p (k t) -> p k t", k=8), ACT.Copy).then_inc(act_hi_ready, 1)
            ac.wait_ge(mixed, 16)
            nc.scalar.activation(act[:, 0:8, 0:T], tile(RV, 8).rearrange("p (k t) -> p k t", k=8), ACT.Copy).then_inc(act_hi_ready, 1)

            with ac.Fori(0, KT // RAW) as lap:
                i = lap * RAW
                for s in range(RAW):
                    round_block(N_OUT + i + s, s)
            ac.wait_ge(acc_evacuated, W_IN_TILES + 4 + KT)
            normalise(2)
            round_block(N_WQ, 0)
            for n in range(1, RAW):
                round_block(N_WQ + n, n)
                evacuate(N_WQ + n - 1, n - 1, qT[:, (n - 1) * T:n * T])
            with ac.Fori(1, KT // RAW) as lap:
                i = lap * RAW
                for s in range(RAW):
                    round_block(N_WQ + i + s, s)
                    evacuate(N_WQ + i + (s - 1), s - 1, qT[:, bass.ds(i * T + (s - 1) * T, T)])
            evacuate(N_WQ + KT - 1, KT - 1, qT[:, (KT - 1) * T:KT * T])
            for b in range(8):
                ac.wait_ge(q_scores, b + 1)
                nc.scalar.activation(sc[:, b // 4, 4 * (b % 4):4 * (b % 4) + 4, :].rearrange("p g k -> p (g k)"),
                                     bank[b][:, :], ACT.Copy).then_inc(q_copied, 1)
            ac.wait_ge(route, ROUTE_GATE)
            nc.scalar.activation(choice[:, 2, :, :].rearrange("p t n -> p (t n)"),
                                 choice[:, 2, :, :].rearrange("p t n -> p (t n)"), ACT.Exp).then_inc(route_exp, 1)
            ac.wait_ge(ch_turned, 1)
            nc.scalar.activation(choiceT[:, 0:2, :].rearrange("p s n -> p (s n)"), bank[0][:, :], ACT.Copy).then_inc(ch_copied, 1)
            nc.scalar.activation(choiceT[:, 2, :], bank[1][:, 0:T], ACT.Copy).then_inc(ch_copied, 1)

            def gate_copy(b, r):
                ac.wait_ge(gate_rows, b + 1)
                if r % 2 == 0 and not isinstance(b, int):
                    ac.wait_ge(gate_stored[r // 2], 4 * b - 4 * r)
                for x in range(2):
                    dst = gs[:, r // 2, :].rearrange("p (g t j) -> p t g j", g=NKEYS // GROUP_J, t=16)
                    t0 = 8 * (r % 2) + 4 * x
                    last = nc.scalar.activation(dst[:, t0:t0 + 4, :, :],
                                                bank[2 * (r % 2) + x][:, :].rearrange("p (t g j) -> p t g j", t=4, j=GROUP_J), ACT.Copy)
                last.then_inc(gate_evac, 1)

            for b in range(4):
                gate_copy(b, b)
            with ac.Fori(1, (T // 8) // 4) as lap:
                i = lap * 4
                for r in range(4):
                    gate_copy(i + r, r)

            for half in range(2):
                n0 = n_u(half)
                round_block(n0, 0)
                for s in range(1, RAW):
                    round_block(n0 + s, s)
                    evacuate(n0 + s - 1, s - 1, arena[:, (s - 1) * T:s * T], ACT.Gelu_apprx_tanh)
                with ac.Fori(1, HALF // RAW) as lap:
                    i = lap * RAW
                    for s in range(RAW):
                        round_block(n0 + i + s, s)
                        evacuate(n0 + i + (s - 1), s - 1, arena[:, bass.ds(i * T + (s - 1) * T, T)], ACT.Gelu_apprx_tanh)
                evacuate(n0 + HALF - 1, HALF - 1, arena[:, (HALF - 1) * T:HALF * T], ACT.Gelu_apprx_tanh)
                with ac.Fori(0, HALF // RAW) as lap:
                    i = lap * RAW
                    for s in range(RAW):
                        round_block(n_v(half) + i + s, s)
                        ac.wait_ge(gated, i + (HALF * half + s + 1))
                        nc.scalar.activation(wm[:, s % 2, 0, :], wmt[:, s % 2, :], ACT.Copy).then_inc(wm_hi, 1)
                ac.wait_ge(block_done, n_v(half) + HALF)
                for b in range(8):
                    if half == 0:
                        nc.scalar.activation(hT[:, b * 512:(b + 1) * 512], bank[b][:, :], ACT.Copy).then_inc(half_kept, 1)
                    else:
                        nc.scalar.activation(arena[:, 8192 + b * 512:8704 + b * 512], bank[b][:, :], ACT.Square,
                                             accum_out=small[:, b:b + 1]).then_inc(fin_sq, 1)
            ac.wait_ge(fin_rstd, 1)
            nc.scalar.activation(small[:, 10:12], small[:, 8:10], ACT.Sqrt, bias=eps, scale=1.0 / D).then_inc(fin_std, 1)

        @block.vector
        def _(dv):
            def rest_block(n, s):
                dv.wait_ge(hi_ready, n + 1)
                nc.vector.tensor_tensor(lo[:, s % 2, :], raw[:, s, :], hi[:, s % 2, :].bitcast(F32), ALU.subtract).then_inc(lo_ready, 1)

            def normalise(count, gain):
                dv.wait_ge(std_ready, count)
                nc.vector.reciprocal(rstd[:, :], rstd[:, :]).then_inc(rstd_ready, 1)
                dv.wait_ge(rstd_ready, count)
                for k in range(KT):
                    nc.vector.scalar_tensor_tensor(out=xn[:, k, :], in0=hT[:, k * T:(k + 1) * T], scalar=gain[:, k:k + 1],
                                                   in1=rstd[:, :], op0=ALU.mult, op1=ALU.mult).then_inc(xn_ready, 1)

            def rest_act(count, k0, k1, src):
                dv.wait_ge(act_hi_ready, count)
                nc.vector.tensor_tensor(act[:, k0:k1, T:2 * T], src, act[:, k0:k1, 0:T].bitcast(F32),
                                        ALU.subtract).then_inc(act_lo_ready, 1)

            nc.vector.memset(eps, EPS).then_inc(eps_ready, 1)
            nc.vector.memset(rb[N_BUCKETS:N_BUCKETS + 1, :], NEG).then_inc(rb_ready, 1)
            dv.wait_ge(rb_ready, 1)
            dv.wait_ge(small_loaded, 64)
            nc.vector.tensor_copy(rb_wide[0:N_BUCKETS + 1, :, :],
                                  rb[0:N_BUCKETS + 1, :].unsqueeze(2).to_broadcast([N_BUCKETS + 1, 8, P])).then_inc(rb_wide_ready, 1)
            normalise(1, g1)
            rest_act(1, 0, KT, xn)
            dv.wait_ge(wg_hi_ready, 1)
            nc.vector.tensor_tensor(wg_r[:, :, 24:48], wg, wg_r[:, :, 0:24].bitcast(F32), ALU.subtract).then_inc(wg_lo_ready, 1)
            dv.wait_ge(cbias_ready, 1)
            nc.vector.tensor_copy(cbias[:, :, 0:NCMP, :], bank[6][:, 0:256].rearrange("p (t c h) -> p t c h", t=2, c=CPAD)[:, :, 0:NCMP, :]
                                  ).then_inc(cbias_copied, 1)
            for n in range(RAW):
                rest_block(n, n)
            with dv.Fori(1, W_IN_TILES // RAW) as lap:
                i = lap * RAW
                for s in range(RAW):
                    rest_block(i + s, s)
            dv.wait_ge(gate_exp, 1)
            nc.vector.tensor_scalar(gate[:, :, :], gate[:, :, :], 1.0, None, ALU.add).then_inc(gate_step, 1)
            dv.wait_ge(gate_step, 1)
            nc.vector.reciprocal(gate[:, :, :], gate[:, :, :]).then_inc(gate_ready, 1)
            dv.wait_ge(mid_loaded, 48)
            dv.wait_ge(v_turned, 6)
            nc.vector.memset(hid_wide, 0.0).then_inc(wide_zero, 1)
            nc.vector.memset(pc, 0.0).then_inc(wide_zero, 1)
            pe_cols = wmt[:, :, :].rearrange("p a n -> p (a n)")[:, 0:2 * CMP_LEN]
            for kind in range(2):
                for g in range(GROUPS):
                    rows_of = tile((KC, VC)[kind] + g).rearrange("p (c l) -> p l c", l=CMP_STRIDE)
                    for lh in range(2):
                        ls = slice(16 * lh, 16 * lh + 16)
                        nc.vector.tensor_tensor(blk[:, kind, ls, g * NCMP:(g + 1) * NCMP], rows_of[:, :, lh:lh + NCMP],
                                                pe_cols[:, kind * CMP_LEN + 16 * lh:kind * CMP_LEN + 16 * lh + 16]
                                                .unsqueeze(2).to_broadcast([P, 16, NCMP]), ALU.add).then_inc(blk_ready, 1)
            dv.wait_ge(blk_hi, 1)
            nc.vector.tensor_tensor(blk_r[:, :, :, 30:60].rearrange("p k l n -> p (k l) n"), blk.rearrange("p k l n -> p (k l) n"),
                                    blk_r[:, :, :, 0:30].bitcast(F32).rearrange("p k l n -> p (k l) n"), ALU.subtract).then_inc(blk_lo, 1)
            for b in range(8):
                rest_block(N_CMP + b, b % RAW)
            for i in range(4):
                dv.wait_ge(swapped, i + 1)
                tmp = (pw, ptw)[i % 2].rearrange("p s n -> p (s n)")[:, 0:2 * T].rearrange("p (f t) -> p f t", f=2)
                qk = tile(2 * i, 2).rearrange("p (f t) -> p f t", f=2)
                nc.vector.tensor_tensor(tmp, bank[2 + i][:, :].rearrange("p (f t) -> p f t", f=2),
                                        sin.unsqueeze(1).to_broadcast([P, 2, T]), ALU.mult).then_inc(rot_sin, 1)
                nc.vector.tensor_tensor(qk, qk, cos.unsqueeze(1).to_broadcast([P, 2, T]), ALU.mult).then_inc(rot_cos, 1)
                dv.wait_ge(rot_sin, i + 1)
                dv.wait_ge(rot_cos, i + 1)
                nc.vector.tensor_tensor(qk, qk, tmp, ALU.add).then_inc(rotated, 1)
            dv.wait_ge(acc_evacuated, W_IN_TILES + 4)
            dv.wait_ge(wide_zero, 2)
            for f in range(2):
                nc.vector.tensor_copy(hid_wide[:, f, :].rearrange("p (g h c) -> p g h c", g=2, c=CPAD)[:, :, :, 0:NCMP],
                                      hid[:, 1, f, :].rearrange("p (g c) -> p g c", g=2).unsqueeze(2).to_broadcast([P, 2, HPG, NCMP])
                                      ).then_inc(wide_ready, 1)
            dv.wait_ge(vc_acc, 1)
            for h in range(NSA_HEADS):
                nc.vector.tensor_scalar(vch[:, h, :], bank[5][:, 0:DH], head_mask[:, h:h + 1], None, ALU.mult).then_inc(vch_ready, 1)
            dv.wait_ge(cs_acc, 1)
            pcv = pc[:, :, :, 0:NCMP]
            pcf = pcv.rearrange("p t h c -> p (t h) c")
            mx, sm = small[:, 0:16], small[:, 16:32]
            for tt in range(2):
                nc.vector.scalar_tensor_tensor(out=pcv[:, tt], in0=bank[6][:, tt * P:(tt + 1) * P].rearrange("p (h c) -> p h c", h=8)[:, :, 0:NCMP],
                                               scalar=SCALE, in1=cbias[:, tt, 0:NCMP, :].rearrange("p c h -> p h c"),
                                               op0=ALU.mult, op1=ALU.add).then_inc(cstep, 1)
            dv.wait_ge(cstep, 2)
            nc.vector.tensor_reduce(mx, pcf, AX.X, ALU.max).then_inc(cstep, 1)
            dv.wait_ge(cstep, 3)
            nc.vector.tensor_scalar(sm, mx, -1.0, None, ALU.mult).then_inc(cstep, 1)
            dv.wait_ge(cstep, 4)
            nc.vector.tensor_tensor(pcf, pcf, sm.unsqueeze(2).to_broadcast([P, 16, NCMP]), ALU.add).then_inc(cstep, 1)
            dv.wait_ge(cexp, 1)
            nc.vector.tensor_tensor(pcv, pcv, seen[:, :, 0:NCMP].unsqueeze(2).to_broadcast([P, 2, 8, NCMP]), ALU.mult).then_inc(cstep, 1)
            dv.wait_ge(cstep, 6)
            nc.vector.tensor_reduce(sm, pcf, AX.X, ALU.add).then_inc(cstep, 1)
            dv.wait_ge(cstep, 7)
            nc.vector.tensor_scalar(sm, sm, 1e-30, None, ALU.max).then_inc(cstep, 1)
            dv.wait_ge(cstep, 8)
            nc.vector.reciprocal(sm, sm).then_inc(cstep, 1)
            dv.wait_ge(cstep, 9)
            dv.wait_ge(gate_ready, 1)
            nc.vector.tensor_tensor(sm.rearrange("p (t h) -> p t h", t=2), sm.rearrange("p (t h) -> p t h", t=2),
                                    gate[:, :, :].rearrange("p t (h b) -> p t h b", b=3)[:, :, :, 0], ALU.mult).then_inc(cstep, 1)
            dv.wait_ge(cstep, 10)
            nc.vector.tensor_tensor(pcf, pcf, sm.unsqueeze(2).to_broadcast([P, 16, NCMP]), ALU.mult).then_inc(pc_ready, 1)

            dv.wait_ge(bias_loaded, 32)

            def soft_in(u):
                h, st = u // 2, stats(u)
                dv.wait_ge(s_acc, u + 1)
                if u >= 2:
                    dv.wait_ge(pT_acc, u - 1)
                nc.vector.scalar_tensor_tensor(out=pw[:, u % 2, :], in0=bank[2 + u % 2][:, 0:3 * P], scalar=SCALE,
                                               in1=bias[:, h, :], op0=ALU.mult, op1=ALU.add).then_inc(s_biased, 1)
                dv.wait_ge(s_biased, u + 1)
                nc.vector.tensor_reduce(st[:, 0:1], pw[:, u % 2, 0:P], AX.X, ALU.max)
                nc.vector.tensor_reduce(st[:, 1:2], pw[:, u % 2, P:3 * P], AX.X, ALU.max).then_inc(s_max, 1)
                dv.wait_ge(s_max, u + 1)
                nc.vector.tensor_scalar(st[:, 2:4], st[:, 0:2], -1.0, None, ALU.mult).then_inc(s_nmax, 1)

            def soft_out(u):
                h, branch, st = u // 2, u % 2, stats(u)
                dv.wait_ge(p_exp, u + 1)
                nc.vector.reciprocal(st[:, 4:6], st[:, 4:6]).then_inc(p_rec, 1)
                dv.wait_ge(p_rec, u + 1)
                nc.vector.tensor_tensor(st[:, 6:8], st[:, 4:6], gate[:, :, 3 * h + branch + 1], ALU.mult).then_inc(p_coef, 1)
                dv.wait_ge(p_coef, u + 1)
                nc.vector.tensor_scalar(pw[:, u % 2, 0:P], pw[:, u % 2, 0:P], st[:, 6:7], None, ALU.mult)
                nc.vector.tensor_scalar(pw[:, u % 2, P:3 * P], pw[:, u % 2, P:3 * P], st[:, 7:8], None, ALU.mult).then_inc(p_ready, 1)

            units = 2 * NSA_HEADS
            dv.wait_ge(rotated, 4)
            soft_in(0)
            for u in range(units):
                if u + 1 < units:
                    soft_in(u + 1)
                soft_out(u)

            dv.wait_ge(decay_loaded, 16)
            dv.wait_ge(pT_acc, units)
            for h in range(RET_HEADS):
                dv.wait_ge(r_acc, h + 1)
                if h >= 2:
                    dv.wait_ge(y_acc, h - 1)
                nc.vector.tensor_tensor(pw[:, h % 2, 0:T], bank[2 + h % 2][:, 0:T], decay[:, h * T:(h + 1) * T], ALU.mult)
                nc.vector.tensor_tensor(pw[:, h % 2, T:3 * P], bank[2 + h % 2][:, T:3 * P], decay[:, h * T:h * T + P],
                                        ALU.mult).then_inc(r_decayed, 1)
            for c in range(4):
                dv.wait_ge(ostd, c + 1)
                nc.vector.reciprocal(tile(KV + 2 * c, 2), tile(KV + 2 * c, 2)).then_inc(orstd, 1)
            dv.wait_ge(orstd, 4)
            for h in range(NSA_HEADS):
                nc.vector.scalar_tensor_tensor(out=tile(NQ + h), in0=tile(NQ + h), scalar=out_g[:, h:h + 1], in1=tile(KV + h),
                                               op0=ALU.mult, op1=ALU.mult).then_inc(mixed, 1)
            dv.wait_ge(silu_exp, 1)
            nc.vector.tensor_scalar(silu_e, silu_e, 1.0, None, ALU.add).then_inc(silu_step, 1)
            dv.wait_ge(silu_step, 1)
            nc.vector.reciprocal(silu_e, silu_e).then_inc(silu_step, 1)
            dv.wait_ge(silu_step, 2)
            nc.vector.tensor_tensor(tile(RG, 8), tile(RG, 8), silu_e, ALU.mult).then_inc(silu_step, 1)
            for c in range(4):
                dv.wait_ge(ystd, c + 1)
                nc.vector.reciprocal(tile(2 * c, 2), tile(2 * c, 2)).then_inc(yrstd, 1)
            dv.wait_ge(yrstd, 4)
            for f in range(RET_HEADS):
                nc.vector.scalar_tensor_tensor(out=tile(RV + f), in0=bank[(6 + f // 2) % 8][:, (f % 2) * T:(f % 2 + 1) * T],
                                               scalar=gn_g[:, f:f + 1], in1=tile(f), op0=ALU.mult, op1=ALU.mult).then_inc(ynorm, 1)
            dv.wait_ge(silu_step, 3)
            for f in range(RET_HEADS):
                dv.wait_ge(ynorm, f + 1)
                nc.vector.tensor_tensor(tile(RV + f), tile(RV + f), tile(RG + f), ALU.mult).then_inc(mixed, 1)
            rest_act(2, 8, 16, tile(NQ, 8).rearrange("p (k t) -> p k t", k=8))
            rest_act(3, 0, 8, tile(RV, 8).rearrange("p (k t) -> p k t", k=8))

            def add_residual(n, s, where):
                dv.wait_ge(block_done, n + 1)
                nc.vector.tensor_tensor(where, bank[s % 2][:, 0:T], where, ALU.add).then_inc(acc_evacuated, 1)

            for n in range(RAW):
                rest_block(N_OUT + n, n)
                if n == 1:
                    dv.wait_ge(xres_loaded, 16)
                if n:
                    add_residual(N_OUT + n - 1, n - 1, hT[:, (n - 1) * T:n * T])
            with dv.Fori(1, KT // RAW) as lap:
                i = lap * RAW
                for s in range(RAW):
                    rest_block(N_OUT + i + s, s)
                    add_residual(N_OUT + i + (s - 1), s - 1, hT[:, bass.ds(i * T + (s - 1) * T, T)])
            add_residual(N_OUT + KT - 1, KT - 1, hT[:, (KT - 1) * T:KT * T])
            normalise(2, g2)
            rest_act(4, 0, KT, xn)
            with dv.Fori(0, KT // RAW) as lap:
                i = lap * RAW
                for s in range(RAW):
                    rest_block(N_WQ + i + s, s)

            steps = [0]

            def step(ins):
                steps[0] += 1
                ins.then_inc(route, 1)

            def best16(vals, idx, src):
                for v, s_ in zip(vals, src):
                    step(nc.vector.max(v[:, 0:8], s_))
                dv.wait_ge(route, steps[0])
                for v, x, s_ in zip(vals, idx, src):
                    step(nc.vector.max_index(x[:, 0:8], v[:, 0:8], s_))
                dv.wait_ge(route, steps[0])
                for v, s_ in zip(vals, src):
                    step(nc.vector.match_replace(s_, v[:, 0:8], s_, LOWEST))
                dv.wait_ge(route, steps[0])
                for v, s_ in zip(vals, src):
                    step(nc.vector.max(v[:, 8:16], s_))
                dv.wait_ge(route, steps[0])
                for v, x, s_ in zip(vals, idx, src):
                    step(nc.vector.max_index(x[:, 8:16], v[:, 8:16], s_))
                dv.wait_ge(route, steps[0])

            dv.wait_ge(q_copied, 8)
            both = [(tt, g) for tt in range(2) for g in range(2 * PH)]
            best16([top[:, tt, g, :] for tt, g in both], [top_i[:, tt, g, :] for tt, g in both], [sc[:, tt, g, :] for tt, g in both])
            for tt in range(2):
                tv = top[:, tt].rearrange("p (h s) k -> p h s k", s=2)
                step(nc.vector.tensor_tensor(cand[:, tt], tv[:, :, 0, :].unsqueeze(3).to_broadcast([P, PH, PK, PK]),
                                             tv[:, :, 1, :].unsqueeze(2).to_broadcast([P, PH, PK, PK]), ALU.add))
            step(nc.vector.tensor_copy(top_f.rearrange("p t h s k -> p (t h s k)"), top_i.rearrange("p t g k -> p (t g k)")))
            dv.wait_ge(route, steps[0])
            heads = [(tt, h) for tt in range(2) for h in range(PH)]
            ci4 = ci.rearrange("p (t h k) -> p t h k", t=2, h=PH)
            best16([cs[:, tt, h, :] for tt, h in heads], [ci4[:, tt, h, :] for tt, h in heads],
                   [cand[:, tt, h].rearrange("p a b -> p (a b)") for tt, h in heads])
            cs_f = cs.rearrange("p t h k -> p (t h) k")
            gates = choice[:, 2].rearrange("p t (h k) -> p (t h) k", h=PH)
            step(nc.vector.tensor_tensor(gates, cs_f, cs_f[:, :, 0:1].to_broadcast([P, 2 * PH, PK]), ALU.subtract))
            assert steps[0] == ROUTE_GATE
            step(nc.vector.tensor_scalar(cab_u[:, 0], ci, 4, None, ALU.logical_shift_right))
            step(nc.vector.tensor_scalar(cab_u[:, 1], ci, 15, None, ALU.bitwise_and))
            dv.wait_ge(route, steps[0])
            step(nc.vector.tensor_copy(cab.rearrange("p s n -> p (s n)"), cab_u.rearrange("p s n -> p (s n)")))
            dv.wait_ge(route, steps[0])
            for side in range(2):
                for tt in range(2):
                    step(nc.vector.tensor_tensor(pick[:, tt], cab[:, side, tt * P:(tt + 1) * P].unsqueeze(2).to_broadcast([P, P, PK]),
                                                 iota[:, 0:PK].unsqueeze(1).to_broadcast([P, P, PK]), ALU.is_equal))
                dv.wait_ge(route, steps[0])
                for tt in range(2):
                    pv = pick[:, tt].rearrange("p (h k) a -> p h k a", h=PH)
                    step(nc.vector.tensor_tensor(pv, pv, top_f[:, tt, :, side, :].unsqueeze(2).to_broadcast([P, PH, PK, PK]), ALU.mult))
                dv.wait_ge(route, steps[0])
                for tt in range(2):
                    last = nc.vector.tensor_reduce(choice[:, side, tt], pick[:, tt], AX.X, ALU.add)
                    step(last)
                dv.wait_ge(route, steps[0])
            dv.wait_ge(route_exp, 1)
            step(nc.vector.tensor_reduce(small[:, 0:16], gates, AX.X, ALU.add))
            dv.wait_ge(route, steps[0])
            step(nc.vector.reciprocal(small[:, 0:16], small[:, 0:16]))
            dv.wait_ge(route, steps[0])
            nc.vector.tensor_tensor(gates, gates, small[:, 0:16].unsqueeze(2).to_broadcast([P, 2 * PH, PK]), ALU.mult).then_inc(choices_ready, 3)

            dv.wait_ge(ch_copied, 2)

            def onehots_batch(b, r):
                if not (isinstance(b, int) and b < 2):
                    dv.wait_ge(gate_rows, b - 1)
                for t in range(8):
                    at = bass.ds(b * 8 + t, 1)
                    nc.vector.tensor_scalar(onehot[:, r % 2, 0, t, :], iota, choiceT[:, 0, at], None, ALU.is_equal)
                    last = nc.vector.tensor_scalar(onehot[:, r % 2, 1, t, :], iota, choiceT[:, 1, at], choiceT[:, 2, at],
                                                   ALU.is_equal, ALU.mult)
                last.then_inc(onehot_ready, 1)

            for b in range(4):
                onehots_batch(b, b)
            with dv.Fori(1, (T // 8) // 4) as lap:
                i = lap * 4
                for r in range(4):
                    onehots_batch(i + r, r)

            for half in range(2):
                with dv.Fori(0, HALF // RAW) as lap:
                    i = lap * RAW
                    for s in range(RAW):
                        rest_block(n_u(half) + i + s, s)
                dv.wait_ge(acc_evacuated, W_IN_TILES + 4 + 2 * KT + HALF * (half + 1))
                with dv.Fori(0, HALF // (2 * GROUP_J)) as lap:
                    i = lap * (2 * GROUP_J)
                    for r in range(2 * GROUP_J):
                        m = HALF * half + r
                        if r % GROUP_J == 0:
                            dv.wait_ge(gate_loaded[r // GROUP_J], i + (HALF * half + 16))
                        nc.vector.tensor_tensor(wmt[:, r % 2, :], arena[:, bass.ds(i * T + r * T, T)],
                                                gs[:, r // GROUP_J, :].rearrange("p (t j) -> p t j", j=GROUP_J)[:, :, r % GROUP_J],
                                                ALU.mult).then_inc(gated, 1)
                        rest_block(n_v(half) + i + r, r % RAW)
                        dv.wait_ge(wm_hi, i + (m + 1))
                        nc.vector.tensor_tensor(wm[:, r % 2, 1, :], wmt[:, r % 2, :], wm[:, r % 2, 0, :].bitcast(F32),
                                                ALU.subtract).then_inc(wm_lo, 1)
            dv.wait_ge(fin_sq, 8)
            nc.vector.tensor_reduce(small[:, 8:10], small[:, 0:8].rearrange("p (t c) -> p t c", t=2), AX.X, ALU.add).then_inc(fin_rstd, 1)
            dv.wait_ge(fin_std, 1)
            nc.vector.reciprocal(small[:, 12:14], small[:, 10:12]).then_inc(fin_rstd, 1)
            dv.wait_ge(fin_rstd, 2)
            dv.wait_ge(gf_loaded, 16)
            for b in range(8):
                nc.vector.scalar_tensor_tensor(out=arena[:, b * 512:(b + 1) * 512], in0=bank[b][:, :], scalar=small[:, 12 + b // 4:13 + b // 4],
                                               in1=hT[:, (b % 4) * 512:(b % 4 + 1) * 512], op0=ALU.mult, op1=ALU.mult).then_inc(fin_ready, 1)


def kernel(x, norm1_g, w_in, rel_bias, ret_gn_g, cmp_pe, cmp_w1, cmp_w2, nsa_out_g, w_out, norm2_g, peer_wq,
           peer_subkeys, peer_u, peer_v, norm_f_g):
    import numpy as _np
    import concourse.bacc as _bacc
    from concourse.bass_utils import run_bass_kernel_spmd as _run

    c = _np.ascontiguousarray

    def blocks(w):
        k, n = w.shape
        return c(_np.asarray(w).reshape(k // P, P, n // P, P).transpose(2, 1, 0, 3).reshape(n // P, P, k))

    def cols(g):
        return _np.asarray(g).reshape(-1, P).T

    x, w_in = _np.asarray(x), _np.asarray(w_in)[0]
    base, mid, decay, onehots = constants()
    cmp_pe, cmp_w1, cmp_w2 = (_np.asarray(v)[0] for v in (cmp_pe, cmp_w1, cmp_w2))
    wide = W_IN_TILES * P
    arrays = {
        "xT": c(x[0].reshape(T, KT, P).transpose(2, 1, 0).reshape(P, KT * T)),
        "base": base, "mid": mid, "decay": decay, "onehots": onehots,
        "gains": c(_np.concatenate([cols(norm1_g), cols(norm2_g), cols(ret_gn_g), cols(nsa_out_g)], 1)),
        "w_gate": c(w_in[:, wide:].reshape(KT, P, -1).transpose(1, 0, 2)),
        "rel_bias": c(rel_bias),
        "subkeys": c(_np.asarray(peer_subkeys)[0].transpose(2, 0, 1)),
        "w_in": blocks(w_in[:, :wide]),
        "cmp_w2": c(cmp_w2.reshape(2, 2, P, DH).transpose(2, 0, 1, 3).reshape(P, 4 * DH)),
        "cmp_pe": c(cmp_pe.transpose(2, 0, 1).reshape(P, 2 * CMP_LEN)),
        "cmp_w1": c(cmp_w1.reshape(2, 2, 16, P, 2, P).transpose(0, 4, 1, 3, 2, 5).reshape(8, P, D)),
        "w_out": blocks(_np.asarray(w_out)[0]),
        "wq": blocks(_np.asarray(peer_wq)[0]),
        "u": c(_np.asarray(peer_u)[0].reshape(NKEYS, NKEYS, KT, P).transpose(1, 3, 2, 0).reshape(NKEYS, P, D)),
        "v": c(_np.asarray(peer_v)[0].reshape(NKEYS, NKEYS, D)),
        "norm_f": c(_np.broadcast_to(_np.asarray(norm_f_g)[None, :], (P, D))),
    }
    nc = _bacc.Bacc("TRN2", target_bir_lowering=False, num_devices=1)
    aps = {k: nc.dram_tensor(f"in_{k}", v.shape, mybir.dt.from_np(v.dtype), kind="ExternalInput").ap() for k, v in arrays.items()}
    out = nc.dram_tensor("out", (T, D), F32, kind="ExternalOutput").ap()
    build(nc, aps, out)
    r = _run(nc, [{f"in_{k}": v for k, v in arrays.items()}], core_ids=[0])
    return r.results[0]["out"].reshape(1, T, D)
```

```python
import math
from contextlib import ExitStack

import concourse.bass as bass
import numpy as np
from concourse import mybir

F32 = mybir.dt.float32
F32R = mybir.dt.float32r
U32 = mybir.dt.uint32
ALU = mybir.AluOpType
ACT = mybir.ActivationFunctionType
AX = mybir.AxisListType

P = 128
T = 256
D = 2048
KT = D // P
EPS = 1e-6
RET_HEADS, RET_DK = 8, 64
NSA_HEADS, GROUPS, DH = 8, 2, 128
HPG = NSA_HEADS // GROUPS
CMP_LEN, CMP_STRIDE = 32, 16
NCMP = (T - CMP_LEN) // CMP_STRIDE + 1
CPAD = 16
N_BUCKETS, MAX_DISTANCE = 32, 128
NEG = -1e30
PH, PK, NKEYS = 8, 16, 128
GROUP_J = 8

KC, VC, VS, VW, NQ, KS, KW, RQ, RK, RV, RG = 0, 2, 4, 6, 8, 16, 18, 20, 24, 28, 36
W_IN_TILES = 44
TILE_ORDER = [32, 33, 34, 35, 38, 39, 42, 43, *range(24, 32), 36, 37, 40, 41, *range(24)]

RAW = 4
PAIRS = 8
M_OUT1, M_OUT2, M_WQ, M_PEER = 44, 52, 60, 76
HALF = NKEYS // 2
def m_u(half): return M_PEER + 2 * HALF * half
def m_v(half): return m_u(half) + HALF
def raw_at(m): return m + 8 if not isinstance(m, int) or m >= PAIRS + 8 else m if m < PAIRS else PAIRS + 2 * (m - PAIRS)

ROUTED = 40
GATE_BLOCKS, BATCHES = HALF - ROUTED, T // 8
def batches_after(r): return range(-(-BATCHES * r // GATE_BLOCKS), -(-BATCHES * (r + 1) // GATE_BLOCKS))

BIAS_W = 384
ONEHOT_F = 512
SCALE = float(DH) ** -0.5
LOWEST = -3.4e38
ROUTE_GATE = 5 * 32 + 3 + 5 * 16 + 1


def buckets(dist):
    d = np.maximum(dist, 0)
    exact = N_BUCKETS // 2
    ratio = np.log(np.maximum(d, 1).astype(np.float32) / np.float32(exact)) / np.float32(math.log(MAX_DISTANCE / exact))
    large = np.minimum(exact + (ratio * np.float32(N_BUCKETS - exact)).astype(np.int32), N_BUCKETS - 1)
    return np.where(d < exact, d, large)


def onehot_of(dist):
    out = np.zeros((N_BUCKETS + 1, len(dist)), np.float32)
    out[np.where(dist >= 0, buckets(dist), N_BUCKETS), np.arange(len(dist))] = 1.0
    return out


def constants():
    eye = np.eye(P, dtype=np.float32)
    base = np.concatenate([eye, np.ones((P, P), np.float32), np.tile(np.arange(P, dtype=np.float32), (P, 1))], 1)
    center = eye - 1.0 / P
    swap = np.zeros((P, P), np.float32)
    half = RET_DK // 2
    for m in range(P):
        if m % RET_DK < half:
            swap[m + half, m] = -1.0
        else:
            swap[m - half, m] = 1.0
    inv = (1.0 / (np.float32(10000.0) ** (np.arange(half, dtype=np.float32) / np.float32(half)))).astype(np.float32)
    ang = np.arange(T, dtype=np.float32)[None, :] * inv[np.arange(P) % half][:, None]
    hm = np.zeros((P, NSA_HEADS), np.float32)
    for p in range(P):
        if p % CPAD < NCMP:
            hm[p, p // CPAD] = 1.0
    t = np.arange(T).reshape(2, P)
    seen = np.zeros((P, 2, CPAD), np.float32)
    for c in range(NCMP):
        seen[:, :, c] = (t >= c * CMP_STRIDE + CMP_LEN - 1).T
    mid = np.concatenate([center, swap, np.cos(ang), np.sin(ang), hm, seen.reshape(P, 2 * CPAD)], 1).astype(np.float32)
    log_g = np.log(1.0 - 2.0 ** (-5.0 - np.arange(RET_HEADS, dtype=np.float64)))
    diff = np.arange(T)[None, :] - np.arange(P)[:, None]
    decay = np.where(diff >= 0, np.exp(log_g[:, None, None] * np.maximum(diff, 0)), 0.0) * RET_DK ** -0.5
    decay = decay.transpose(1, 0, 2).reshape(P, RET_HEADS * T).astype(np.float32)
    onehots = np.concatenate([onehot_of(T - 1 - np.arange(BIAS_W)), onehot_of(np.arange(ONEHOT_F) - 256)], 1)
    return base, mid, decay, onehots


MID_W = 2 * P + 2 * T + NSA_HEADS + 2 * CPAD


def build(nc, a, out):
    with ExitStack() as ctx:
        def sb(name, shape, dt=F32):
            return ctx.enter_context(nc.sbuf_tensor(name, shape, dt))

        def sem(name):
            return ctx.enter_context(nc.semaphore(name))

        bank = [ctx.enter_context(nc.psum_tensor(f"bank{b}", [P, 512], F32)) for b in range(8)]

        raw = sb("raw", [P, RAW, D])
        hi = sb("hi", [P, 2, D], F32R)
        lo = sb("lo", [P, 2, D], F32R)
        act = sb("act", [P, KT, 2 * T], F32R)
        hT = sb("hT", [P, 4096])
        arena = sb("arena", [P, 16384])
        gs = sb("gs", [P, 2, 2048])
        wm = sb("wm", [P, 2, 2, T], F32R)
        wmt = sb("wmt", [P, 2, T])
        choiceT = sb("choiceT", [P, 3, T])
        base = sb("base", [P, 3 * P])
        subk = sb("subk", [P, 2, NKEYS])
        gains = sb("gains", [P, 2 * KT + 16])
        gate = sb("gate", [P, 2, 3 * NSA_HEADS])
        small = sb("small", [P, 72])
        rstd = sb("rstd", [P, T])
        ident, ones, iota = base[:, 0:P], base[:, P:2 * P], base[:, 2 * P:3 * P]
        g1, g2 = gains[:, 0:KT], gains[:, KT:2 * KT]
        gn_g, out_g = gains[:, 2 * KT:2 * KT + 8], gains[:, 2 * KT + 8:2 * KT + 16]
        eps, rb, nrs = small[:, 32:33], small[:, 40:48], small[:, 34:36]

        proj = arena[:, 0:W_IN_TILES * T]
        def tile(f, n=1): return proj[:, f * T:(f + n) * T]
        rv_tok = arena[:, 11264:13312].rearrange("p (t n) -> p t n", t=2)
        v_tok = arena[:, 13312:14336].rearrange("p (t n) -> p t n", t=2)
        decay = arena[:, 14336:16384]
        sq = arena[:, 4096:8192].rearrange("p (k t) -> p k t", k=KT)
        onehots = arena[:, 11264:11264 + BIAS_W + ONEHOT_F]
        rb_wide = arena[:, 12288:13312].rearrange("p (h m) -> p h m", h=NSA_HEADS)
        wg = arena[:, 8192:8192 + KT * 24].rearrange("p (k n) -> p k n", k=KT)
        wg_r = wm[:, :, :, :].rearrange("p a b n -> p (a b n)")[:, 0:KT * 48].rearrange("p (k n) -> p k n", k=KT)
        blk_flat = arena[:, RG * T:RG * T + 2 * CMP_LEN * 30]
        blk = blk_flat.rearrange("p (k l n) -> p k l n", k=2, l=CMP_LEN)
        gs_flat = gs[:, :, :].rearrange("p a n -> p (a n)")
        wmt_flat = wmt[:, :, :].rearrange("p a n -> p (a n)")
        bias = gs_flat[:, 0:8 * BIAS_W].rearrange("p (h n) -> p h n", h=8)
        vch = gs_flat[:, 3072:4096].rearrange("p (h n) -> p h n", h=8)
        mid = hT[:, 0:MID_W]
        center, swap = mid[:, 0:P], mid[:, P:2 * P]
        cos, sin = mid[:, 2 * P:2 * P + T], mid[:, 2 * P + T:2 * P + 2 * T]
        head_mask = mid[:, 2 * P + 2 * T:2 * P + 2 * T + 8]
        seen = mid[:, MID_W - 2 * CPAD:MID_W].rearrange("p (t c) -> p t c", t=2)
        w2 = hT[:, 832:1344].rearrange("p (k f n) -> p k f n", k=2, f=2)
        hid = hT[:, 1344:1472].rearrange("p (k f n) -> p k f n", k=2, f=2)
        hid_wide = hT[:, 1472:1728].rearrange("p (f n) -> p f n", f=2)
        cbias = hT[:, 1728:1984].rearrange("p (t c h) -> p t c h", t=2, c=CPAD)
        pc = hT[:, 1984:2240].rearrange("p (t h c) -> p t h c", t=2, h=8)
        pcT = hT[:, 2240:2496]
        kc = hT[:, 2496:2528]
        pw = hT[:, 2560:3328].rearrange("p (s n) -> p s n", s=2)
        ptw = hT[:, 3328:4096].rearrange("p (s n) -> p s n", s=2)
        pe_cols = wmt_flat[:, 0:2 * CMP_LEN]
        res = arena[:, 0:4096]
        ysq = arena[:, 4096:5120]

        xn = hT[:, :].rearrange("p (k t) -> p k t", k=KT)
        qT = arena[:, 4096:8192]
        sc = arena[:, 8192:12288].rearrange("p (t g k) -> p t g k", t=2, g=2 * PH)
        cand = gs_flat.rearrange("p (t h a b) -> p t h a b", t=2, h=PH, a=PK)
        pick = gs_flat.rearrange("p (t n a) -> p t n a", t=2, a=PK)
        top = arena[:, 12288:12800].rearrange("p (t g k) -> p t g k", t=2, g=2 * PH)
        top_i = arena[:, 12800:13312].bitcast(U32).rearrange("p (t g k) -> p t g k", t=2, g=2 * PH)
        top_f = arena[:, 13312:13824].rearrange("p (t h s k) -> p t h s k", t=2, h=PH, s=2)
        cs = arena[:, 13824:14080].rearrange("p (t h k) -> p t h k", t=2, h=PH)
        ci = arena[:, 14080:14336].bitcast(U32)
        cab = arena[:, 14336:14848].rearrange("p (s n) -> p s n", s=2)
        cab_u = arena[:, 14336:14848].bitcast(U32).rearrange("p (s n) -> p s n", s=2)
        choice = arena[:, 14848:15616].rearrange("p (s t n) -> p s t n", s=3, t=2)
        onehot = hT[:, :].rearrange("p (b s n j) -> p b s n j", b=2, s=2, n=8)

        rows_dram = nc.dram_tensor("bias_rows", (NSA_HEADS, P, BIAS_W), F32, kind="Internal").ap()
        res_dram = nc.dram_tensor("residual", (P, 4096), F32, kind="Internal").ap()
        gate_dram = nc.dram_tensor("gate_matrix", (NKEYS // GROUP_J, P, T, GROUP_J), F32, kind="Internal").ap()

        raw_loaded = [sem(f"raw_loaded{s}") for s in range(RAW)]
        hi_ready, lo_ready, block_done, cmp_done, acc_evacuated = (
            sem(s) for s in ("hi_ready", "lo_ready", "block_done", "cmp_done", "acc_evacuated"))
        x_loaded, base_loaded, small_loaded, onehots_loaded, mid_loaded, decay_loaded, xres_loaded = (
            sem(s) for s in ("x_loaded", "base_loaded", "small_loaded", "onehots_loaded", "mid_loaded", "decay_loaded", "xres_loaded"))
        consts_ready, act_hi_ready, act_lo_ready, sq_ready, ss_ready, log_ready, rstd_ready, xn_ready = (
            sem(s) for s in ("consts_ready", "act_hi_ready", "act_lo_ready", "sq_ready", "ss_ready", "log_ready", "rstd_ready", "xn_ready"))
        rb_wide_ready, rows_ready, rows_copied, rows_stored, bias_loaded, cbias_ready, cbias_copied = (
            sem(s) for s in ("rb_wide_ready", "rows_ready", "rows_copied", "rows_stored", "bias_loaded", "cbias_ready", "cbias_copied"))
        wg_hi_ready, wg_lo_ready, rstd_turned, nrs_ready, gate_acc, gate_exp, gate_step, gate_ready = (
            sem(s) for s in ("wg_hi_ready", "wg_lo_ready", "rstd_turned", "nrs_ready", "gate_acc", "gate_exp", "gate_step", "gate_ready"))
        blk_ready, hid_ready, kc_acc, kc_copied, zeroed, wide_ready, vc_acc, vch_ready, v_turned, v_copied = (
            sem(s) for s in ("blk_ready", "hid_ready", "kc_acc", "kc_copied", "zeroed", "wide_ready", "vc_acc", "vch_ready",
                             "v_turned", "v_copied"))
        cs_acc, cstep, cexp, pc_ready, pcT_acc, pcT_copied = (
            sem(s) for s in ("cs_acc", "cstep", "cexp", "pc_ready", "pcT_acc", "pcT_copied"))
        s_acc, s_biased, s_max, s_nmax, p_exp, p_rec, p_coef, p_ready, pT_acc, pT_copied, pv_done, o_copied = (
            sem(s) for s in ("s_acc", "s_biased", "s_max", "s_nmax", "p_exp", "p_rec", "p_coef", "p_ready", "pT_acc",
                             "pT_copied", "pv_done", "o_copied"))
        swapped, rot_sin, rot_cos, rotated, rv_turned, rv_copied = (
            sem(s) for s in ("swapped", "rot_sin", "rot_cos", "rotated", "rv_turned", "rv_copied"))
        osq_ready, oss_acc, olog, orstd, mixed = (sem(s) for s in ("osq_ready", "oss_acc", "olog", "orstd", "mixed"))
        r_acc, r_decayed, y_acc, y_copied, yc_acc, yc_copied, ysq_ready, yss_acc, ylog, yrstd, silu_ready, ynorm = (
            sem(s) for s in ("r_acc", "r_decayed", "y_acc", "y_copied", "yc_acc", "yc_copied", "ysq_ready", "yss_acc", "ylog",
                             "yrstd", "silu_ready", "ynorm"))
        res_stored, q_scores, q_copied, route, route_exp, choices_ready, ch_turned, ch_copied = (
            sem(s) for s in ("res_stored", "q_scores", "q_copied", "route", "route_exp", "choices_ready", "ch_turned", "ch_copied"))
        onehots_ready, gate_rows, gate_evac, res_loaded = (
            sem(s) for s in ("onehots_ready", "gate_rows", "gate_evac", "res_loaded"))
        gate_stored = [sem(f"gate_stored{s}") for s in range(2)]
        gate_loaded = [sem(f"gate_loaded{s}") for s in range(2)]
        gated, wm_hi, wm_lo, half_kept, sums_done, fin_sq, fin_sum, fin_log, fin_rstd, fin_ready, gf_loaded, out_stored = (
            sem(s) for s in ("gated", "wm_hi", "wm_lo", "half_kept", "sums_done", "fin_sq", "fin_sum", "fin_log", "fin_rstd",
                             "fin_ready", "gf_loaded", "out_stored"))

        def stats(u):
            return small[:, 48 + 8 * (u % 2):56 + 8 * (u % 2)]

        units = 2 * NSA_HEADS
        UNIT0, ROT, TURN_V, RET0 = 20, 36, 38, 41

        block = ctx.enter_context(nc.Block())

        @block.sync
        def _(sp):
            sp.dma_start(hT[:, :], a["xT"]).then_inc(x_loaded, 16)
            sp.dma_start(gains[:, :], a["gains"]).then_inc(small_loaded, 16)
            sp.dma_start(rb[0:N_BUCKETS, :], a["rel_bias"]).then_inc(small_loaded, 16)
            sp.dma_start(wg, a["w_gate"]).then_inc(small_loaded, 16)
            sp.dma_start(base[:, :], a["base"]).then_inc(base_loaded, 16)

            def load(src, n):
                sp.dma_start(raw[:, n % RAW, :], src).then_inc(raw_loaded[n % RAW], 16)

            def load_after(src, m, s):
                sp.wait_ge(hi_ready, m + 1)
                sp.wait_ge(lo_ready, m + 1)
                sp.dma_start(raw[:, s, :], src).then_inc(raw_loaded[s], 16)

            for n in range(RAW):
                load(a["w_in"][n], n)
            sp.dma_start(onehots[0:N_BUCKETS + 1, :], a["onehots"]).then_inc(onehots_loaded, 16)
            sp.wait_ge(act_lo_ready, KT)
            sp.wait_ge(sq_ready, 1)
            sp.dma_start(mid, a["mid"]).then_inc(mid_loaded, 16)
            sp.dma_start(hT[:, 832:1344], a["cmp_w2"]).then_inc(mid_loaded, 16)
            sp.dma_start(pe_cols, a["cmp_pe"]).then_inc(mid_loaded, 16)
            for m in range(RAW, PAIRS):
                load_after(a["w_in"][m], m - RAW, m % RAW)
            sp.dma_start(decay, a["decay"]).then_inc(decay_loaded, 16)
            sp.dma_start(subk[:, :, :], a["subkeys"]).then_inc(decay_loaded, 16)
            sp.wait_ge(rows_copied, NSA_HEADS)
            sp.dma_start(rows_dram.rearrange("h p n -> p h n"), bias).then_inc(rows_stored, 16)
            for r in range(2):
                load_after(a["w_in"][PAIRS + r], PAIRS - RAW + 2 * r, 2 * r)
                load_after(a["cmp_w1"][r], PAIRS - RAW + 2 * r + 1, 2 * r + 1)
            sp.wait_ge(rows_stored, 16)
            for part in range(2):
                first = P * (1 - part)
                skew = bass.AP(tensor=rows_dram.tensor, offset=P - 1 + first,
                               ap=[[BIAS_W - 1, P], [P * BIAS_W, NSA_HEADS], [1, P * (part + 1)]])
                sp.dma_start(bias[:, :, P * part:P * part + P * (part + 1)], skew).then_inc(bias_loaded, 16)
            with sp.Fori(1, 4) as lap:
                for r in range(2):
                    load_after(a["w_in"][2 * lap + (PAIRS + r)], 2 * lap + (PAIRS - 2 + r), 2 * r)
                    sp.wait_ge(cmp_done, 2 * lap + (r - 1))
                    sp.dma_start(raw[:, 2 * r + 1, :], a["cmp_w1"][2 * lap + r]).then_inc(raw_loaded[2 * r + 1], 16)
            for s in range(RAW):
                if s % 2:
                    sp.wait_ge(cmp_done, 7 + s // 2)
                    sp.dma_start(raw[:, s, :], a["w_in"][16 + s]).then_inc(raw_loaded[s], 16)
                else:
                    load_after(a["w_in"][16 + s], 14 + s // 2, s)
            with sp.Fori(5, W_IN_TILES // RAW) as lap:
                for s in range(RAW):
                    load_after(a["w_in"][RAW * lap + s], RAW * lap + (s - RAW), s)
            for s in range(RAW):
                if s == 2:
                    sp.wait_ge(act_lo_ready, KT + 4)
                    sp.dma_start(res, a["xT"]).then_inc(xres_loaded, 16)
                load_after(a["w_out"][s], M_OUT1 - RAW + s, s)
            with sp.Fori(1, KT // RAW) as lap:
                for s in range(RAW):
                    load_after(a["w_out"][RAW * lap + s], RAW * lap + (M_OUT1 - RAW + s), s)
            with sp.Fori(0, KT // RAW) as lap:
                for s in range(RAW):
                    load_after(a["wq"][RAW * lap + s], RAW * lap + (M_WQ - RAW + s), s)
            for half in range(2):
                with sp.Fori(0, HALF // RAW) as lap:
                    for s in range(RAW):
                        load_after(a["u"][RAW * lap + (HALF * half + s)], RAW * lap + (m_u(half) - RAW + s), s)

                def load_v(mv, s):
                    load_after(a["v"][:, mv + HALF * half, :], mv + (m_v(half) - RAW), s)

                def load_gates(q, g):
                    sp.dma_start(gs[:, g, :], gate_dram[q + (HALF // GROUP_J * half)].rearrange("i t j -> i (t j)")
                                 ).then_inc(gate_loaded[g], 16)

                if half == 0:
                    for s in range(RAW):
                        load_v(s, s)
                    for s in range(2):
                        sp.wait_ge(gate_stored[s], 16 * (T // 32))
                    load_gates(0, 0)
                    load_gates(1, 1)
                    sp.wait_ge(gate_rows, BATCHES)
                    sp.wait_ge(res_stored, 16)
                    sp.dma_start(hT[:, :], res_dram).then_inc(res_loaded, 16)
                    for mv in range(RAW, 2 * GROUP_J):
                        load_v(mv, mv % RAW)
                with sp.Fori(1 if half == 0 else 0, HALF // GROUP_J // 2) as lap:
                    for g in range(2):
                        sp.wait_ge(gated, 2 * GROUP_J * lap + (GROUP_J * (g - 1) + HALF * half))
                        load_gates(2 * lap + g, g)
                        for r in range(GROUP_J):
                            load_v(2 * GROUP_J * lap + (GROUP_J * g + r), r % RAW)
            sp.wait_ge(block_done, m_v(1) + 8)
            sp.dma_start(hT[:, 0:D], a["norm_f"]).then_inc(gf_loaded, 16)
            for tt in range(2):
                sp.wait_ge(fin_ready, 4 * (tt + 1))
                sp.dma_start(out[tt * P:(tt + 1) * P, :], arena[:, tt * D:(tt + 1) * D]).then_inc(out_stored, 16)
            sp.wait_ge(out_stored, 32)

        @block.gpsimd
        def _(pool):
            pool.wait_ge(acc_evacuated, M_WQ)
            pool.dma_start(res_dram, res).then_inc(res_stored, 16)
            with pool.Fori(0, T // 32) as lap:
                for s in range(2):
                    pool.wait_ge(gate_evac, 4 * lap + (2 * s + 2))
                    pool.dma_start(gate_dram.rearrange("g i t j -> i g (t j)")[:, :, bass.ds((32 * lap + 16 * s) * GROUP_J, 16 * GROUP_J)],
                                   gs[:, s, :].rearrange("p (g n) -> p g n", g=NKEYS // GROUP_J)).then_inc(gate_stored[s], 16)

        @block.tensor
        def _(pe):
            mm = nc.tensor.matmul

            def product(dst, wh, wl, mh, ml, first, last):
                mm(dst, wh, mh, start=first, stop=False)
                mm(dst, wh, ml, start=False, stop=False)
                return mm(dst, wl, mh, start=False, stop=last)

            def weights_block(m, s, others=0):
                pe.wait_ge(hi_ready, m + 1)
                pe.wait_ge(lo_ready, m + 1)
                if not (isinstance(m, int) and m < 2):
                    pe.wait_ge(acc_evacuated, m - (others + 1))
                for k in range(KT):
                    w = slice(k * P, (k + 1) * P)
                    last = product(bank[s % 2][:, 0:T], hi[:, s % 2, w], lo[:, s % 2, w], act[:, k, 0:T], act[:, k, T:2 * T],
                                   k == 0, k == KT - 1)
                last.then_inc(block_done, 1)

            def w_out_block(m, s, k0, act_count=0):
                pe.wait_ge(hi_ready, m + 1)
                pe.wait_ge(lo_ready, m + 1)
                pe.wait_ge(acc_evacuated, m - 1)
                for f in range(2):
                    for k in range(8):
                        if act_count and f == 0 and k % 2 == 0:
                            pe.wait_ge(act_hi_ready, act_count + k // 2)
                            pe.wait_ge(act_lo_ready, act_count + k // 2)
                        w = slice((8 * f + k) * P, (8 * f + k + 1) * P)
                        last = product(bank[s % 2][:, f * T:(f + 1) * T], hi[:, s % 2, w], lo[:, s % 2, w],
                                       act[:, k0 + k, 0:T], act[:, k0 + k, T:2 * T], k == 0, k == 7)
                last.then_inc(block_done, 1)

            rows = N_BUCKETS + 1
            pe.wait_ge(base_loaded, 16)
            pe.wait_ge(act_hi_ready, KT)
            pe.wait_ge(act_lo_ready, KT)
            weights_block(0, 0)
            pe.wait_ge(sq_ready, 1)
            for k in range(KT):
                last = mm(bank[7][:, 0:T], ones, sq[:, k, :], start=(k == 0), stop=(k == KT - 1))
            last.then_inc(ss_ready, 1)
            for part in range(2):
                weights_block(1 + part, 1 + part)
                pe.wait_ge(rb_wide_ready, 1)
                pe.wait_ge(onehots_loaded, 16)
                for h in range(4 * part, 4 * part + 4):
                    if h >= 4:
                        pe.wait_ge(rows_copied, h - 3)
                    mm(bank[2 + h % 4][:, 0:BIAS_W], rb_wide[0:rows, h, :], onehots[0:rows, 0:BIAS_W],
                       start=True, stop=True).then_inc(rows_ready, 1)
            weights_block(3, 3)
            for tt in range(2):
                for c in range(NCMP):
                    z = BIAS_W + 256 + tt * P - CMP_STRIDE * c - (CMP_LEN - 1)
                    at = (tt * CPAD + c) * 8
                    last = mm(bank[6][:, at:at + 8], onehots[0:rows, z:z + P], rb[0:rows, :], start=True, stop=True)
            last.then_inc(cbias_ready, 1)
            weights_block(4, 4)
            pe.wait_ge(rstd_ready, 1)
            pe.wait_ge(cbias_copied, 1)
            for tt in range(2):
                last = nc.tensor.transpose(bank[6][:, T + tt * P:T + (tt + 1) * P], rstd[:, tt * P:(tt + 1) * P], ident)
            last.then_inc(rstd_turned, 1)
            pe.wait_ge(wg_hi_ready, 1)
            pe.wait_ge(wg_lo_ready, 1)
            for tt in range(2):
                dst = bank[7][:, T + tt * 24:T + (tt + 1) * 24]
                for k in range(KT):
                    xh, xl = act[:, k, tt * P:(tt + 1) * P], act[:, k, T + tt * P:T + (tt + 1) * P]
                    mm(dst, xh, wg_r[:, k, 0:24], start=(k == 0), stop=False)
                    mm(dst, xh, wg_r[:, k, 24:48], start=False, stop=False)
                    last = mm(dst, xl, wg_r[:, k, 0:24], start=False, stop=(k == KT - 1))
            last.then_inc(gate_acc, 1)
            for m in range(5, PAIRS):
                weights_block(m, m)
            pe.wait_ge(blk_ready, 8)
            pe.wait_ge(gate_exp, 2)
            with pe.Fori(0, 2) as kind:
                for f in range(2):
                    for r in range(2):
                        weights_block(4 * kind + (PAIRS + 2 * f + r), r)
                        pe.wait_ge(raw_loaded[2 * r + 1], 32 * kind + (16 * f + 16 * (PAIRS // RAW + 1)))
                        for k in range(16):
                            last = mm(bank[7][:, bass.ds(64 * kind + 32 * f, 30)], raw[:, 2 * r + 1, k * P:(k + 1) * P],
                                      blk_flat[:, bass.ds(CMP_LEN * 30 * kind + (16 * r + k) * 30, 30)],
                                      start=(r == 0 and k == 0), stop=(r == 1 and k == 15))
                        last.then_inc(cmp_done, 1)
            weights_block(16, 16)
            pe.wait_ge(rows_copied, NSA_HEADS)
            for tt in range(2):
                for j, f in enumerate((VS, VS + 1, VW, VW + 1)):
                    last = nc.tensor.transpose(bank[2 + tt][:, j * P:(j + 1) * P], tile(f)[:, tt * P:(tt + 1) * P], ident)
                last.then_inc(v_turned, 1)
            pe.wait_ge(mid_loaded, 48)
            pe.wait_ge(hid_ready, 1)
            for f in range(2):
                last = mm(bank[4][:, 0:30], w2[:, 0, f, :], hid[:, 0, f, 0:30], start=(f == 0), stop=(f == 1))
            last.then_inc(kc_acc, 1)
            pe.wait_ge(wide_ready, 2)
            for f in range(2):
                last = mm(bank[5][:, 0:DH], hid_wide[:, f, :], w2[:, 1, f, :], start=(f == 0), stop=(f == 1))
            last.then_inc(vc_acc, 1)
            weights_block(17, 17)
            pe.wait_ge(kc_copied, 1)
            pe.wait_ge(nrs_ready, 1)
            for tt in range(2):
                for h in range(NSA_HEADS):
                    at, g = (tt * 8 + h) * CPAD, h // HPG
                    last = mm(bank[6][:, at:at + NCMP], tile(NQ + h)[:, tt * P:(tt + 1) * P],
                              kc[:, g * NCMP:(g + 1) * NCMP], start=True, stop=True)
            last.then_inc(cs_acc, 1)
            weights_block(18, 18)
            weights_block(19, 19)
            pe.wait_ge(pc_ready, 1)
            for tt in range(2):
                last = nc.tensor.transpose(bank[7][:, tt * P:(tt + 1) * P], pc[:, tt, :, :].rearrange("p h c -> p (h c)"), ident)
            last.then_inc(pcT_acc, 1)

            def scores(u):
                h, kt = u // 2, (KS, KW)[u % 2] + u // 2 // HPG
                if u >= 2:
                    pe.wait_ge(s_biased, u - 1)
                q, dst = tile(NQ + h), bank[2 + u % 2]
                mm(dst[:, 0:P], q[:, 0:P], tile(kt)[:, 0:P], start=True, stop=True)
                mm(dst[:, P:3 * P], q[:, P:T], tile(kt), start=True, stop=True).then_inc(s_acc, 1)

            def turn(u):
                pe.wait_ge(p_ready, u + 1)
                if u >= 2:
                    pe.wait_ge(pT_copied, u - 1)
                for j in range(3):
                    last = nc.tensor.transpose(bank[4 + u % 2][:, j * P:(j + 1) * P], pw[:, u % 2, j * P:(j + 1) * P], ident)
                last.then_inc(pT_acc, 1)

            def weigh(u):
                h, branch = u // 2, u % 2
                g, dst = h // HPG, bank[6 + h % 2]
                at = branch * T + g * DH
                if branch == 0:
                    if h >= 2:
                        pe.wait_ge(o_copied, h - 1)
                    mm(dst[:, 0:T], vch[:, h, :], pcT, start=True, stop=False)
                pe.wait_ge(pT_copied, u + 1)
                mm(dst[:, 0:T], v_tok[:, 0, at:at + DH], ptw[:, u % 2, 0:T], start=False, stop=False)
                mm(dst[:, P:T], v_tok[:, 1, at:at + DH], ptw[:, u % 2, T:3 * P],
                   start=False, stop=(branch == 1)).then_inc(pv_done, 1)

            def r_scores(h):
                part = slice(RET_DK * (h % 2), RET_DK * (h % 2 + 1))
                q, k, dst = tile(RQ + h // 2)[part, :], tile(RK + h // 2)[part, :], bank[2 + h % 2]
                if h >= 2:
                    pe.wait_ge(r_decayed, h - 1)
                mm(dst[:, 0:T], k[:, 0:P], q, start=True, stop=True)
                mm(dst[:, T:3 * P], k[:, P:T], q[:, P:T], start=True, stop=True).then_inc(r_acc, 1)

            def r_weigh(h):
                pe.wait_ge(r_decayed, h + 1)
                if h >= 2:
                    pe.wait_ge(y_copied, h - 1)
                dst = bank[4 + h % 2]
                mm(dst[:, 0:T], rv_tok[:, 0, h * P:(h + 1) * P], pw[:, h % 2, 0:T], start=True, stop=False)
                mm(dst[:, P:T], rv_tok[:, 1, h * P:(h + 1) * P], pw[:, h % 2, T:3 * P],
                   start=False, stop=True).then_inc(y_acc, 1)

            for m in range(UNIT0, M_OUT2):
                if m < M_OUT1:
                    weights_block(m, m)
                else:
                    w_out_block(m, m, 8, KT + 1 if m == M_OUT1 else 0)
                u = m - UNIT0
                if u < units:
                    if u == 0:
                        pe.wait_ge(v_copied, 2)
                    scores(u)
                if 1 <= u <= units:
                    if u == 1:
                        pe.wait_ge(kc_copied, 1)
                        pe.wait_ge(vch_ready, NSA_HEADS)
                    turn(u - 1)
                if 2 <= u <= units + 1:
                    if u == 2:
                        pe.wait_ge(pcT_copied, 1)
                    weigh(u - 2)
                if ROT <= m < ROT + 2:
                    for i in range(2 * (m - ROT), 2 * (m - ROT) + 2):
                        if i < 2:
                            pe.wait_ge(s_biased, units - 1 + i)
                        else:
                            pe.wait_ge(rot_sin, i - 1)
                        mm(bank[2 + i % 2][:, :], swap, tile(RQ + 2 * i, 2), start=True, stop=True).then_inc(swapped, 1)
                if TURN_V <= m < TURN_V + 2:
                    tt = m - TURN_V
                    for half in range(2):
                        if tt == 0:
                            pe.wait_ge(pT_copied, units - 1 + half)
                        else:
                            pe.wait_ge(rv_copied, half + 1)
                        for j in range(4):
                            last = nc.tensor.transpose(bank[4 + half][:, j * P:(j + 1) * P],
                                                       tile(RV + 4 * half + j)[:, tt * P:(tt + 1) * P], ident)
                        last.then_inc(rv_turned, 1)
                if m == TURN_V + 1:
                    pe.wait_ge(osq_ready, 1)
                    pe.wait_ge(o_copied, NSA_HEADS)
                    pe.wait_ge(rot_sin, 4)
                    for c in range(4):
                        mm(bank[(2, 3, 6, 7)[c]][:, :], ones, tile(2 * c, 2), start=True, stop=True).then_inc(oss_acc, 1)
                i = m - RET0
                if 0 <= i < 4:
                    if i == 0:
                        pe.wait_ge(rotated, 4)
                        pe.wait_ge(olog, 4)
                        pe.wait_ge(rv_copied, 4)
                    r_scores(2 * i)
                    r_scores(2 * i + 1)
                if 1 <= i <= 4:
                    r_weigh(2 * i - 2)
                    r_weigh(2 * i - 1)
                if 2 <= i <= 5:
                    c = i - 2
                    pe.wait_ge(y_copied, 2 * c + 2)
                    if c:
                        pe.wait_ge(yc_copied, c)
                    mm(bank[6][:, :], center, tile(RV + 2 * c, 2), start=True, stop=True).then_inc(yc_acc, 1)
                if 3 <= i <= 6:
                    c = i - 3
                    pe.wait_ge(ysq_ready, c + 1)
                    if c:
                        pe.wait_ge(ylog, c)
                    mm(bank[7][:, :], ones, ysq[:, (c % 2) * 512:(c % 2 + 1) * 512], start=True, stop=True).then_inc(yss_acc, 1)

            pe.wait_ge(act_hi_ready, KT + 5)
            pe.wait_ge(act_lo_ready, KT + 5)
            pe.wait_ge(ylog, 4)

            def squares(c):
                pe.wait_ge(sq_ready, c + 2)
                for k in range(2 * c, 2 * c + 2):
                    last = mm(bank[7][:, 0:T], ones, xn[:, k, :], start=(k == 0), stop=(k == KT - 1))
                return last

            for c in range(8):
                w_out_block(M_OUT2 + c, c, 0)
                if c:
                    squares(c - 1)
            squares(7).then_inc(ss_ready, 1)

            pe.wait_ge(act_hi_ready, KT + 9)
            pe.wait_ge(act_lo_ready, KT + 9)
            with pe.Fori(0, KT // RAW) as lap:
                for s in range(RAW):
                    weights_block(RAW * lap + (M_WQ + s), s)
            for j in range(RAW):
                weights_block(M_PEER + j, j)
                if j == 0:
                    pe.wait_ge(decay_loaded, 32)
                    pe.wait_ge(acc_evacuated, M_PEER)
                    for x in range(8):
                        tt, g0 = x // 4, 4 * (x % 4)
                        if x >= 6:
                            pe.wait_ge(q_copied, x - 5)
                        for g in range(g0, g0 + 4):
                            last = mm(bank[2 + x % 6][:, (g % 4) * P:(g % 4 + 1) * P],
                                      qT[:, g * T + tt * P:g * T + (tt + 1) * P], subk[:, g % 2, :], start=True, stop=True)
                        last.then_inc(q_scores, 1)
            with pe.Fori(1, ROUTED // RAW) as lap:
                for s in range(RAW):
                    weights_block(RAW * lap + (M_PEER + s), s)
            pe.wait_ge(choices_ready, 1)
            pe.wait_ge(q_copied, 8)
            for x in range(6):
                last = nc.tensor.transpose(bank[2 + x // 4][:, (x % 4) * P:(x % 4 + 1) * P], choice[:, x // 2, x % 2, :], ident)
            last.then_inc(ch_turned, 1)

            def gate_batch(b):
                pe.wait_ge(onehots_ready, b + 1)
                if b >= 2:
                    pe.wait_ge(gate_evac, b - 1)
                for t in range(8):
                    last = mm(bank[4 + 2 * (b % 2) + t // 4][:, (t % 4) * P:(t % 4 + 1) * P],
                              onehot[:, b % 2, 0, t, :], onehot[:, b % 2, 1, t, :], start=True, stop=True)
                last.then_inc(gate_rows, 1)

            for r in range(GATE_BLOCKS):
                weights_block(M_PEER + ROUTED + r, r)
                for b in batches_after(r):
                    gate_batch(b)

            for half in range(2):
                if half:
                    pe.wait_ge(half_kept, 2)
                    with pe.Fori(0, HALF // RAW) as lap:
                        for s in range(RAW):
                            weights_block(RAW * lap + (m_u(1) + s), s, HALF)
                    pe.wait_ge(half_kept, 8)
                else:
                    pe.wait_ge(gate_evac, BATCHES)

                def v_block(mv, s, opening=False, closing=False):
                    pe.wait_ge(hi_ready, mv + (m_v(half) + 1))
                    pe.wait_ge(lo_ready, mv + (m_v(half) + 1))
                    pe.wait_ge(wm_hi, mv + (HALF * half + 1))
                    pe.wait_ge(wm_lo, mv + (HALF * half + 1))
                    w, vh, vl = wm[:, s % 2, :, :], hi[:, s % 2, :], lo[:, s % 2, :]
                    for tt in range(2):
                        for x, (part, moving) in enumerate(((0, vl), (0, vh), (1, vh))):
                            for dc in range(4):
                                last = mm(bank[tt * 4 + dc][:, :], w[:, part, tt * P:(tt + 1) * P],
                                          moving[:, dc * 512:(dc + 1) * 512], start=opening and x == 0,
                                          stop=closing and x == 2, skip_group_check=True)
                        if closing and tt == 0:
                            last.then_inc(sums_done, 1)
                    last.then_inc(block_done, 1)

                pe.wait_ge(acc_evacuated, M_PEER + HALF * (half + 1))
                for s in range(RAW):
                    v_block(s, s, opening=(s == 0))
                if half == 0:
                    pe.wait_ge(res_loaded, 16)
                for b in range(8):
                    tt, dc = b // 4, b % 4
                    if half == 0:
                        for j in range(4):
                            mm(bank[b][:, j * P:(j + 1) * P], hT[:, (4 * dc + j) * T + tt * P:(4 * dc + j) * T + (tt + 1) * P],
                               ident, start=False, stop=False, skip_group_check=True)
                    else:
                        mm(bank[b][:, :], ident, hT[:, tt * D + dc * 512:tt * D + (dc + 1) * 512],
                           start=False, stop=False, skip_group_check=True)
                with pe.Fori(1, HALF // RAW - 1) as lap:
                    for s in range(RAW):
                        v_block(RAW * lap + s, s)
                for s in range(RAW):
                    v_block(HALF - RAW + s, s, closing=(s == RAW - 1))

        @block.scalar
        def _(ac):
            do = nc.scalar.activation

            def round_block(m, s, raw_slot, laps):
                ac.wait_ge(raw_loaded[raw_slot], 16 * laps)
                if not (isinstance(m, int) and m < 2):
                    ac.wait_ge(block_done, m - 1)
                do(hi[:, s % 2, :], raw[:, raw_slot, :], ACT.Copy).then_inc(hi_ready, 1)

            def round_static(m):
                n = raw_at(m)
                round_block(m, m, n % RAW, n // RAW + 1)

            def round_lap(m, lap, s, base_lap):
                ac.wait_ge(raw_loaded[s], 16 * lap + 16 * base_lap)
                ac.wait_ge(block_done, m - 1)
                do(hi[:, s % 2, :], raw[:, s, :], ACT.Copy).then_inc(hi_ready, 1)

            def rsqrt(src, dst, width, logged, ready, count):
                do(dst, src, ACT.Ln, bias=eps, scale=1.0 / width).then_inc(logged, 1)
                ac.wait_ge(logged, count)
                do(dst, dst, ACT.Exp, scale=-0.5).then_inc(ready, 1)

            ac.wait_ge(small_loaded, 48)
            ac.wait_ge(x_loaded, 16)
            for k in range(KT):
                do(act[:, k, 0:T], hT[:, k * T:(k + 1) * T], ACT.Copy, scale=g1[:, k:k + 1]).then_inc(act_hi_ready, 1)
            do(sq.rearrange("p k t -> p (k t)"), hT[:, :], ACT.Square).then_inc(sq_ready, 1)
            round_static(0)
            do(wg_r[:, :, 0:24], wg, ACT.Copy).then_inc(wg_hi_ready, 1)
            ac.wait_ge(consts_ready, 1)
            for m in range(1, PAIRS):
                round_static(m)
                if m == 1:
                    ac.wait_ge(ss_ready, 1)
                    rsqrt(bank[7][:, 0:T], rstd[:, :], D, log_ready, rstd_ready, 1)
                if m in (2, 3):
                    for h in range(4 * (m - 2), 4 * (m - 2) + 4):
                        ac.wait_ge(rows_ready, h + 1)
                        do(bias[:, h, :], bank[2 + h % 4][:, 0:BIAS_W], ACT.Copy).then_inc(rows_copied, 1)
                if m == 5:
                    ac.wait_ge(gate_acc, 1)
                    ac.wait_ge(nrs_ready, 1)
                    for tt in range(2):
                        do(gate[:, tt, :], bank[7][:, T + tt * 24:T + (tt + 1) * 24], ACT.Exp,
                           scale=nrs[:, tt:tt + 1]).then_inc(gate_exp, 1)
            with ac.Fori(0, 4) as lap:
                for r in range(2):
                    ac.wait_ge(raw_loaded[2 * r], 16 * lap + 16 * (PAIRS // RAW + 1))
                    ac.wait_ge(block_done, 2 * lap + (PAIRS + r - 1))
                    do(hi[:, r, :], raw[:, 2 * r, :], ACT.Copy).then_inc(hi_ready, 1)
            round_static(16)
            ac.wait_ge(cmp_done, 8)
            ac.wait_ge(mid_loaded, 48)
            do(hid[:, :, :, :].rearrange("p k f n -> p (k f) n")[:, :, 0:30],
               bank[7][:, 0:P].rearrange("p (e n) -> p e n", e=4)[:, :, 0:30], ACT.Gelu_apprx_tanh).then_inc(hid_ready, 1)
            round_static(17)
            ac.wait_ge(kc_acc, 1)
            do(kc[:, 0:30], bank[4][:, 0:30], ACT.Copy).then_inc(kc_copied, 1)
            ac.wait_ge(cbias_copied, 1)
            for tt in range(2):
                ac.wait_ge(v_turned, tt + 1)
                do(v_tok[:, tt, :], bank[2 + tt][:, :], ACT.Copy).then_inc(v_copied, 1)
            round_static(18)
            ac.wait_ge(cstep, 5)
            pcf = pc[:, :, :, 0:NCMP].rearrange("p t h c -> p (t h) c")
            do(pcf, pcf, ACT.Exp).then_inc(cexp, 1)
            round_static(19)

            def exps(u):
                ac.wait_ge(s_nmax, u + 1)
                st = stats(u)
                do(pw[:, u % 2, 0:P], pw[:, u % 2, 0:P], ACT.Exp, bias=st[:, 2:3], accum_out=st[:, 4:5])
                do(pw[:, u % 2, P:3 * P], pw[:, u % 2, P:3 * P], ACT.Exp, bias=st[:, 3:4],
                   accum_out=st[:, 5:6]).then_inc(p_exp, 1)

            def copy_pT(u):
                ac.wait_ge(pT_acc, u + 1)
                if u >= 2:
                    ac.wait_ge(pv_done, u - 1)
                do(ptw[:, u % 2, :], bank[4 + u % 2][:, 0:3 * P], ACT.Copy).then_inc(pT_copied, 1)

            def copy_o(h):
                ac.wait_ge(pv_done, 2 * h + 2)
                do(tile(NQ + h), bank[6 + h % 2][:, 0:T], ACT.Copy).then_inc(o_copied, 1)

            for m in range(UNIT0, M_OUT2):
                round_static(m)
                if m == M_OUT1:
                    ac.wait_ge(mixed, 8)
                    ac.wait_ge(block_done, W_IN_TILES)
                    for k in range(0, 8, 2):
                        do(act[:, 8 + k:10 + k, 0:T], tile(NQ + k, 2).rearrange("p (k t) -> p k t", k=2), ACT.Copy).then_inc(act_hi_ready, 1)
                if m == UNIT0:
                    ac.wait_ge(pcT_acc, 1)
                    do(pcT, bank[7][:, 0:T], ACT.Copy).then_inc(pcT_copied, 1)
                u = m - UNIT0 - 1
                if 1 <= u <= units:
                    copy_pT(u - 1)
                if 0 <= u < units:
                    exps(u)
                if u >= 3 and u % 2 and (u - 3) // 2 < NSA_HEADS:
                    copy_o((u - 3) // 2)
                if m == TURN_V:
                    ac.wait_ge(o_copied, NSA_HEADS)
                    do(tile(0, 8), tile(NQ, 8), ACT.Square).then_inc(osq_ready, 1)
                if m in (TURN_V + 1, TURN_V + 2):
                    for half in range(2):
                        tt = m - TURN_V - 1
                        ac.wait_ge(rv_turned, 2 * tt + half + 1)
                        do(rv_tok[:, tt, half * 512:(half + 1) * 512], bank[4 + half][:, :], ACT.Copy).then_inc(rv_copied, 1)
                if m == TURN_V + 2:
                    for c in range(4):
                        ac.wait_ge(oss_acc, c + 1)
                        rsqrt(bank[(2, 3, 6, 7)[c]][:, :], tile(2 * c, 2), DH, olog, orstd, c + 1)
                i = m - RET0 - 2
                if 0 <= i < 4:
                    for h in (2 * i, 2 * i + 1):
                        ac.wait_ge(y_acc, h + 1)
                        do(tile(RV + h), bank[4 + h % 2][:, 0:T], ACT.Copy).then_inc(y_copied, 1)
                if 1 <= i <= 4:
                    c = i - 1
                    ac.wait_ge(yc_copied, c + 1)
                    if c >= 2:
                        ac.wait_ge(ynorm, 4 * c - 4)
                    do(ysq[:, (c % 2) * 512:(c % 2 + 1) * 512], tile(RV + 2 * c, 2), ACT.Square).then_inc(ysq_ready, 1)
                if i == 1:
                    ac.wait_ge(acc_evacuated, W_IN_TILES)
                    do(tile(RG, 8), tile(RG, 8), ACT.Silu).then_inc(silu_ready, 1)
                if 2 <= i <= 5:
                    c = i - 2
                    ac.wait_ge(yss_acc, c + 1)
                    rsqrt(bank[7][:, :], ysq[:, (c % 2) * 512:(c % 2 + 1) * 512], P, ylog, yrstd, c + 1)
                if i == 6:
                    ac.wait_ge(ynorm, 16)
                    do(act[:, 0:8, 0:T], tile(RV, 8).rearrange("p (k t) -> p k t", k=8), ACT.Copy).then_inc(act_hi_ready, 1)

            for c in range(9):
                round_static(M_OUT2 + c)
                if c:
                    ac.wait_ge(acc_evacuated, M_OUT2 + c)
                    do(hT[:, (c - 1) * 512:c * 512], res[:, (c - 1) * 512:c * 512], ACT.Square).then_inc(sq_ready, 1)
            ac.wait_ge(ss_ready, 2)
            rsqrt(bank[7][:, 0:T], rstd[:, :], D, log_ready, rstd_ready, 2)
            for c in range(4):
                ac.wait_ge(xn_ready, 4 * c + 4)
                do(act[:, 4 * c:4 * c + 4, 0:T], xn[:, 4 * c:4 * c + 4, :], ACT.Copy).then_inc(act_hi_ready, 1)

            def evacuate(m, s, dst, func):
                ac.wait_ge(block_done, m + 1)
                do(dst, bank[s % 2][:, 0:T], func).then_inc(acc_evacuated, 1)

            for s in range(1, RAW):
                round_static(M_WQ + s)
                evacuate(M_WQ + s - 1, s - 1, qT[:, (s - 1) * T:s * T], ACT.Copy)
            with ac.Fori(1, KT // RAW) as lap:
                for s in range(RAW):
                    m = RAW * lap + (M_WQ + s)
                    round_lap(m, lap, s, (M_WQ + 8) // RAW + 1)
                    evacuate(RAW * lap + (M_WQ + s - 1), s - 1, qT[:, bass.ds(RAW * T * lap + (s - 1) * T, T)], ACT.Copy)
            round_static(M_PEER)
            evacuate(M_PEER - 1, 1, qT[:, (KT - 1) * T:KT * T], ACT.Copy)
            ac.wait_ge(res_stored, 16)
            for j in range(1, RAW):
                round_static(M_PEER + j)
                evacuate(M_PEER + j - 1, j - 1, arena[:, (j - 1) * T:j * T], ACT.Gelu_apprx_tanh)
                if j == 1:
                    for x in range(8):
                        ac.wait_ge(q_scores, x + 1)
                        do(sc[:, x // 4, 4 * (x % 4):4 * (x % 4) + 4, :].rearrange("p g k -> p (g k)"),
                           bank[2 + x % 6][:, :], ACT.Copy).then_inc(q_copied, 1)

            def hidden_lap(lap, half):
                for s in range(RAW):
                    m = RAW * lap + (m_u(half) + s)
                    round_lap(m, lap, s, (m_u(half) + 8) // RAW + 1)
                    ac.wait_ge(block_done, RAW * lap + (m_u(half) + s))
                    do(arena[:, bass.ds(RAW * T * lap + (s - 1) * T, T)], bank[(s - 1) % 2][:, 0:T],
                       ACT.Gelu_apprx_tanh).then_inc(acc_evacuated, 1)

            with ac.Fori(1, ROUTED // RAW - 1) as lap:
                hidden_lap(lap, 0)
            ac.wait_ge(route, ROUTE_GATE)
            do(choice[:, 2], choice[:, 2], ACT.Exp).then_inc(route_exp, 1)
            hidden_lap(ROUTED // RAW - 1, 0)
            m0 = M_PEER + ROUTED
            round_static(m0)
            evacuate(m0 - 1, 1, arena[:, (ROUTED - 1) * T:ROUTED * T], ACT.Gelu_apprx_tanh)
            ac.wait_ge(ch_turned, 1)
            for part in range(3):
                do(choiceT[:, part, :], bank[2 + part // 2][:, (part % 2) * T:(part % 2 + 1) * T], ACT.Copy).then_inc(ch_copied, 1)

            def gate_copy(b):
                ac.wait_ge(gate_rows, b + 1)
                if b % 2 == 0 and b >= 4:
                    ac.wait_ge(gate_stored[b // 2 % 2], 16 * (b // 4))
                for x in range(2):
                    dst = gs[:, b // 2 % 2, :].rearrange("p (g t j) -> p t g j", g=NKEYS // GROUP_J, t=16)
                    t0 = 8 * (b % 2) + 4 * x
                    last = do(dst[:, t0:t0 + 4, :, :], bank[4 + 2 * (b % 2) + x][:, :].rearrange("p (t g j) -> p t g j", t=4, j=GROUP_J),
                              ACT.Copy)
                last.then_inc(gate_evac, 1)

            for r in range(GATE_BLOCKS):
                if r:
                    round_static(m0 + r)
                    evacuate(m0 + r - 1, r - 1, arena[:, (ROUTED + r - 1) * T:(ROUTED + r) * T], ACT.Gelu_apprx_tanh)
                for b in batches_after(r):
                    if b:
                        gate_copy(b - 1)

            for half in range(2):
                if half:
                    for s in range(1, RAW):
                        round_static(m_u(1) + s)
                        evacuate(m_u(1) + s - 1, s - 1, arena[:, (s - 1) * T:s * T], ACT.Gelu_apprx_tanh)
                    with ac.Fori(1, HALF // RAW) as lap:
                        hidden_lap(lap, 1)
                round_static(m_v(half))
                evacuate(m_v(half) - 1, 1, arena[:, (HALF - 1) * T:HALF * T], ACT.Gelu_apprx_tanh)
                if half == 0:
                    gate_copy(BATCHES - 1)

                def round_gated(mv, s):
                    ac.wait_ge(gated, mv + (HALF * half + 1))
                    do(wm[:, s % 2, 0, :], wmt[:, s % 2, :], ACT.Copy).then_inc(wm_hi, 1)

                round_gated(0, 0)
                for s in range(1, RAW):
                    round_static(m_v(half) + s)
                    round_gated(s, s)
                with ac.Fori(1, HALF // RAW) as lap:
                    for s in range(RAW):
                        round_lap(RAW * lap + (m_v(half) + s), lap, s, (m_v(half) + 8) // RAW + 1)
                        round_gated(RAW * lap + s, s)
                if half == 0:
                    round_static(m_u(1))
                    ac.wait_ge(sums_done, 1)
                    for b in range(8):
                        if b == 4:
                            ac.wait_ge(block_done, m_v(0) + HALF)
                        do(hT[:, b * 512:(b + 1) * 512], bank[b][:, :], ACT.Copy).then_inc(half_kept, 1)
            for b in range(8):
                if b == 0:
                    ac.wait_ge(sums_done, 2)
                if b == 4:
                    ac.wait_ge(block_done, m_v(1) + HALF)
                do(arena[:, 8192 + b * 512:8704 + b * 512], bank[b][:, :], ACT.Square, accum_out=small[:, b:b + 1]).then_inc(fin_sq, 1)
                if b % 4 == 3:
                    tt = b // 4
                    ac.wait_ge(fin_sum, tt + 1)
                    rsqrt(small[:, 8 + tt:9 + tt], small[:, 10 + tt:11 + tt], D, fin_log, fin_rstd, tt + 1)

        @block.vector
        def _(dv):
            vec = nc.vector

            def rest_block(m, s, raw_slot):
                dv.wait_ge(hi_ready, m + 1)
                vec.tensor_tensor(lo[:, s % 2, :], raw[:, raw_slot, :], hi[:, s % 2, :].bitcast(F32), ALU.subtract).then_inc(lo_ready, 1)

            def rest_static(m):
                rest_block(m, m, raw_at(m) % RAW)

            def rest_act(hi_count, k0, k1, src):
                dv.wait_ge(act_hi_ready, hi_count)
                vec.tensor_tensor(act[:, k0:k1, T:2 * T], src, act[:, k0:k1, 0:T].bitcast(F32), ALU.subtract).then_inc(act_lo_ready, 1)

            def scaled(m, s, dst):
                dv.wait_ge(block_done, m + 1)
                vec.tensor_tensor(dst, bank[s % 2][:, 0:T], rstd[:, :], ALU.mult).then_inc(acc_evacuated, 1)

            vec.memset(eps, EPS).then_inc(consts_ready, 1)
            vec.memset(rb[N_BUCKETS:N_BUCKETS + 1, :], NEG).then_inc(consts_ready, 1)
            dv.wait_ge(small_loaded, 48)
            dv.wait_ge(x_loaded, 16)
            for k in range(KT):
                dv.wait_ge(act_hi_ready, k + 1)
                vec.scalar_tensor_tensor(out=act[:, k, T:2 * T], in0=hT[:, k * T:(k + 1) * T], scalar=g1[:, k:k + 1],
                                         in1=act[:, k, 0:T].bitcast(F32), op0=ALU.mult, op1=ALU.subtract).then_inc(act_lo_ready, 1)
            rest_static(0)
            dv.wait_ge(consts_ready, 2)
            vec.tensor_copy(rb_wide[0:N_BUCKETS + 1, :, :],
                            rb[0:N_BUCKETS + 1, :].unsqueeze(2).to_broadcast([N_BUCKETS + 1, 8, P])).then_inc(rb_wide_ready, 1)
            dv.wait_ge(wg_hi_ready, 1)
            vec.tensor_tensor(wg_r[:, :, 24:48], wg, wg_r[:, :, 0:24].bitcast(F32), ALU.subtract).then_inc(wg_lo_ready, 1)
            for m in range(1, PAIRS):
                rest_static(m)
                if m == 1:
                    dv.wait_ge(rstd_ready, 1)
                scaled(m - 1, m - 1, tile(m - 1))
                if m == 4:
                    dv.wait_ge(cbias_ready, 1)
                    dv.wait_ge(act_lo_ready, KT)
                    vec.tensor_copy(cbias[:, :, 0:NCMP, :], bank[6][:, 0:T].rearrange("p (t c h) -> p t c h", t=2, c=CPAD)[:, :, 0:NCMP, :]
                                    ).then_inc(cbias_copied, 1)
                if m == 5:
                    dv.wait_ge(rstd_turned, 1)
                    vec.tensor_scalar(nrs, bank[6][:, T:2 * T].rearrange("p (t n) -> p t n", t=2)[:, :, 0], -1.0, None, ALU.mult
                                      ).then_inc(nrs_ready, 1)
                    vec.memset(hid_wide, 0.0).then_inc(zeroed, 1)
                    vec.memset(pc, 0.0).then_inc(zeroed, 1)
                if m == 6:
                    dv.wait_ge(gate_exp, 2)
                    vec.tensor_scalar(gate[:, :, :], gate[:, :, :], 1.0, None, ALU.add).then_inc(gate_step, 1)
                    dv.wait_ge(gate_step, 1)
                    vec.reciprocal(gate[:, :, :], gate[:, :, :]).then_inc(gate_ready, 1)
                if m == 7:
                    dv.wait_ge(mid_loaded, 48)
                    for kind in range(2):
                        for g in range(GROUPS):
                            dv.wait_ge(acc_evacuated, (KC, VC)[kind] + g + 1)
                            rows_of = tile((KC, VC)[kind] + g).rearrange("p (c l) -> p l c", l=CMP_STRIDE)
                            for lh in range(2):
                                ls = slice(16 * lh, 16 * lh + 16)
                                vec.tensor_tensor(blk[:, kind, ls, g * NCMP:(g + 1) * NCMP], rows_of[:, :, lh:lh + NCMP],
                                                  pe_cols[:, kind * CMP_LEN + 16 * lh:kind * CMP_LEN + 16 * lh + 16]
                                                  .unsqueeze(2).to_broadcast([P, 16, NCMP]), ALU.add).then_inc(blk_ready, 1)
            with dv.Fori(0, 4) as lap:
                for r in range(2):
                    rest_block(2 * lap + (PAIRS + r), r, 2 * r)
                    scaled(2 * lap + (PAIRS + r - 1), r - 1, proj[:, bass.ds(2 * T * lap + (PAIRS + r - 1) * T, T)])
            rest_static(16)
            scaled(15, 15, tile(15))
            dv.wait_ge(hid_ready, 1)
            dv.wait_ge(zeroed, 2)
            for f in range(2):
                vec.tensor_copy(hid_wide[:, f, :].rearrange("p (g h c) -> p g h c", g=2, c=CPAD)[:, :, :, 0:NCMP],
                                hid[:, 1, f, 0:30].rearrange("p (g c) -> p g c", g=2).unsqueeze(2).to_broadcast([P, 2, HPG, NCMP])
                                ).then_inc(wide_ready, 1)
            rest_static(17)
            scaled(16, 16, tile(16))
            dv.wait_ge(vc_acc, 1)
            for h in range(NSA_HEADS):
                vec.tensor_scalar(vch[:, h, :], bank[5][:, 0:DH], head_mask[:, h:h + 1], None, ALU.mult).then_inc(vch_ready, 1)
            rest_static(18)
            scaled(17, 17, tile(17))
            dv.wait_ge(cs_acc, 1)
            dv.wait_ge(cbias_copied, 1)
            pcv = pc[:, :, :, 0:NCMP]
            pcf = pcv.rearrange("p t h c -> p (t h) c")
            mx, sm = small[:, 0:16], small[:, 16:32]
            for tt in range(2):
                vec.scalar_tensor_tensor(out=pcv[:, tt], in0=bank[6][:, tt * P:(tt + 1) * P].rearrange("p (h c) -> p h c", h=8)[:, :, 0:NCMP],
                                         scalar=SCALE, in1=cbias[:, tt, 0:NCMP, :].rearrange("p c h -> p h c"),
                                         op0=ALU.mult, op1=ALU.add).then_inc(cstep, 1)
            dv.wait_ge(cstep, 2)
            vec.tensor_reduce(mx, pcf, AX.X, ALU.max).then_inc(cstep, 1)
            dv.wait_ge(cstep, 3)
            vec.tensor_scalar(sm, mx, -1.0, None, ALU.mult).then_inc(cstep, 1)
            dv.wait_ge(cstep, 4)
            vec.tensor_tensor(pcf, pcf, sm.unsqueeze(2).to_broadcast([P, 16, NCMP]), ALU.add).then_inc(cstep, 1)
            rest_static(19)
            scaled(18, 18, tile(18))
            dv.wait_ge(cexp, 1)
            vec.tensor_tensor(pcv, pcv, seen[:, :, 0:NCMP].unsqueeze(2).to_broadcast([P, 2, 8, NCMP]), ALU.mult).then_inc(cstep, 1)
            dv.wait_ge(cstep, 6)
            vec.tensor_reduce(sm, pcf, AX.X, ALU.add).then_inc(cstep, 1)
            dv.wait_ge(cstep, 7)
            vec.tensor_scalar(sm, sm, 1e-30, None, ALU.max).then_inc(cstep, 1)
            dv.wait_ge(cstep, 8)
            vec.reciprocal(sm, sm).then_inc(cstep, 1)
            dv.wait_ge(cstep, 9)
            dv.wait_ge(gate_ready, 1)
            vec.tensor_tensor(sm.rearrange("p (t h) -> p t h", t=2), sm.rearrange("p (t h) -> p t h", t=2),
                              gate[:, :, :].rearrange("p t (h b) -> p t h b", b=3)[:, :, :, 0], ALU.mult).then_inc(cstep, 1)
            dv.wait_ge(cstep, 10)
            vec.tensor_tensor(pcf, pcf, sm.unsqueeze(2).to_broadcast([P, 16, NCMP]), ALU.mult).then_inc(pc_ready, 1)

            def soft_in(u):
                h, st = u // 2, stats(u)
                dv.wait_ge(s_acc, u + 1)
                if u >= 2:
                    dv.wait_ge(pT_acc, u - 1)
                vec.scalar_tensor_tensor(out=pw[:, u % 2, :], in0=bank[2 + u % 2][:, 0:3 * P], scalar=SCALE,
                                         in1=bias[:, h, :], op0=ALU.mult, op1=ALU.add).then_inc(s_biased, 1)
                dv.wait_ge(s_biased, u + 1)
                vec.tensor_reduce(st[:, 0:1], pw[:, u % 2, 0:P], AX.X, ALU.max)
                vec.tensor_reduce(st[:, 1:2], pw[:, u % 2, P:3 * P], AX.X, ALU.max).then_inc(s_max, 1)
                dv.wait_ge(s_max, u + 1)
                vec.tensor_scalar(st[:, 2:4], st[:, 0:2], -1.0, None, ALU.mult).then_inc(s_nmax, 1)

            def soft_out(u):
                h, branch, st = u // 2, u % 2, stats(u)
                dv.wait_ge(p_exp, u + 1)
                vec.reciprocal(st[:, 4:6], st[:, 4:6]).then_inc(p_rec, 1)
                dv.wait_ge(p_rec, u + 1)
                vec.tensor_tensor(st[:, 6:8], st[:, 4:6], gate[:, :, 3 * h + branch + 1], ALU.mult).then_inc(p_coef, 1)
                dv.wait_ge(p_coef, u + 1)
                vec.tensor_scalar(pw[:, u % 2, 0:P], pw[:, u % 2, 0:P], st[:, 6:7], None, ALU.mult)
                vec.tensor_scalar(pw[:, u % 2, P:3 * P], pw[:, u % 2, P:3 * P], st[:, 7:8], None, ALU.mult).then_inc(p_ready, 1)

            def rotate(i):
                dv.wait_ge(swapped, i + 1)
                if i:
                    dv.wait_ge(rotated, i)
                tmp = wmt_flat.rearrange("p (f t) -> p f t", f=2)
                qk = tile(RQ + 2 * i, 2).rearrange("p (f t) -> p f t", f=2)
                vec.tensor_tensor(tmp, bank[2 + i % 2][:, :].rearrange("p (f t) -> p f t", f=2),
                                  sin.unsqueeze(1).to_broadcast([P, 2, T]), ALU.mult).then_inc(rot_sin, 1)
                vec.tensor_tensor(qk, qk, cos.unsqueeze(1).to_broadcast([P, 2, T]), ALU.mult).then_inc(rot_cos, 1)
                dv.wait_ge(rot_sin, i + 1)
                dv.wait_ge(rot_cos, i + 1)
                vec.tensor_tensor(qk, qk, tmp, ALU.add).then_inc(rotated, 1)

            def add_residual(m, s, where):
                dv.wait_ge(block_done, m + 1)
                vec.tensor_tensor(where, bank[s % 2][:, :], where, ALU.add).then_inc(acc_evacuated, 1)

            for m in range(UNIT0, M_OUT2):
                rest_static(m)
                if m <= M_OUT1:
                    scaled(m - 1, m - 1, tile(m - 1))
                    if m == M_OUT1:
                        for k in range(0, 8, 2):
                            rest_act(KT + 1 + k // 2, 8 + k, 10 + k, tile(NQ + k, 2).rearrange("p (k t) -> p k t", k=2))
                else:
                    if m == M_OUT1 + 1:
                        dv.wait_ge(xres_loaded, 16)
                    add_residual(m - 1, m - 1, res[:, (m - 1 - M_OUT1) * 512:(m - M_OUT1) * 512])
                u = m - UNIT0 - 1
                if 0 <= u < units:
                    if u == 0:
                        dv.wait_ge(bias_loaded, 32)
                    soft_in(u)
                    soft_out(u)
                if ROT < m <= ROT + 2:
                    rotate(2 * (m - ROT) - 2)
                    rotate(2 * (m - ROT) - 1)
                if m == TURN_V + 3:
                    dv.wait_ge(orstd, 4)
                    for h in range(NSA_HEADS):
                        vec.scalar_tensor_tensor(out=tile(NQ + h), in0=tile(NQ + h), scalar=out_g[:, h:h + 1], in1=tile(h),
                                                 op0=ALU.mult, op1=ALU.mult).then_inc(mixed, 1)
                i = m - RET0 - 1
                if 0 <= i < 4:
                    dv.wait_ge(decay_loaded, 32)
                    if i == 0:
                        dv.wait_ge(pT_acc, units)
                    for h in (2 * i, 2 * i + 1):
                        dv.wait_ge(r_acc, h + 1)
                        if h >= 2:
                            dv.wait_ge(y_acc, h - 1)
                        vec.tensor_tensor(pw[:, h % 2, 0:T], bank[2 + h % 2][:, 0:T], decay[:, h * T:(h + 1) * T], ALU.mult)
                        vec.tensor_tensor(pw[:, h % 2, T:3 * P], bank[2 + h % 2][:, T:3 * P], decay[:, h * T:h * T + P],
                                          ALU.mult).then_inc(r_decayed, 1)
                if 2 <= i <= 5:
                    c = i - 2
                    dv.wait_ge(yc_acc, c + 1)
                    vec.tensor_copy(tile(RV + 2 * c, 2), bank[6][:, :]).then_inc(yc_copied, 1)
                if 3 <= i <= 6:
                    c = i - 3
                    dv.wait_ge(yrstd, c + 1)
                    dv.wait_ge(yc_copied, c + 1)
                    dv.wait_ge(silu_ready, 1)
                    for f in (2 * c, 2 * c + 1):
                        rs = ysq[:, (c % 2) * 512 + (f % 2) * T:(c % 2) * 512 + (f % 2 + 1) * T]
                        vec.scalar_tensor_tensor(out=tile(RV + f), in0=tile(RV + f), scalar=gn_g[:, f:f + 1], in1=rs,
                                                 op0=ALU.mult, op1=ALU.mult).then_inc(ynorm, 1)
                    dv.wait_ge(ynorm, 4 * c + 2)
                    for f in (2 * c, 2 * c + 1):
                        vec.tensor_tensor(tile(RV + f), tile(RV + f), tile(RG + f), ALU.mult).then_inc(ynorm, 1)
                if i == 7:
                    rest_act(KT + 5, 0, 8, tile(RV, 8).rearrange("p (k t) -> p k t", k=8))

            for c in range(9):
                rest_static(M_OUT2 + c)
                x = (c + 7) % 8
                add_residual(M_OUT2 + c - 1, c - 1, res[:, x * 512:(x + 1) * 512])
            dv.wait_ge(rstd_ready, 2)
            dv.wait_ge(acc_evacuated, M_WQ)
            for k in range(KT):
                vec.scalar_tensor_tensor(out=xn[:, k, :], in0=res[:, k * T:(k + 1) * T], scalar=g2[:, k:k + 1],
                                         in1=rstd[:, :], op0=ALU.mult, op1=ALU.mult).then_inc(xn_ready, 1)
            for c in range(4):
                rest_act(KT + 6 + c, 4 * c, 4 * c + 4, xn[:, 4 * c:4 * c + 4, :])
            for s in range(1, RAW):
                rest_static(M_WQ + s)
            with dv.Fori(1, KT // RAW) as lap:
                for s in range(RAW):
                    rest_block(RAW * lap + (M_WQ + s), s, s)

            done = {"route": 0, "u": 0}

            def step(ins):
                done["route"] += 1
                ins.then_inc(route, 1)

            def routed():
                dv.wait_ge(route, done["route"])

            def u_rest():
                if done["u"] < ROUTED:
                    rest_static(M_PEER + done["u"])
                    done["u"] += 1

            def best16(vals, idx, src):
                for v, l in zip(vals, src):
                    step(vec.max(v[:, 0:8], l))
                routed()
                for v, x, l in zip(vals, idx, src):
                    step(vec.max_index(x[:, 0:8], v[:, 0:8], l))
                routed()
                for v, l in zip(vals, src):
                    step(vec.match_replace(l, v[:, 0:8], l, LOWEST))
                routed()
                for v, l in zip(vals, src):
                    step(vec.max(v[:, 8:16], l))
                routed()
                for v, x, l in zip(vals, idx, src):
                    step(vec.max_index(x[:, 8:16], v[:, 8:16], l))
                routed()

            u_rest()
            u_rest()
            for pair in range(2 * PH):
                tt, g = pair // PH, 2 * (pair % PH)
                dv.wait_ge(q_copied, pair // 2 + 1)
                best16([top[:, tt, g + s, :] for s in range(2)], [top_i[:, tt, g + s, :] for s in range(2)],
                       [sc[:, tt, g + s, :] for s in range(2)])
                u_rest()
            step(vec.tensor_copy(top_f.rearrange("p t h s k -> p (t h s k)"), top_i.rearrange("p t g k -> p (t g k)")))
            for tt in range(2):
                tv = top[:, tt].rearrange("p (h s) k -> p h s k", s=2)
                step(vec.tensor_tensor(cand[:, tt], tv[:, :, 0, :].unsqueeze(3).to_broadcast([P, PH, PK, PK]),
                                       tv[:, :, 1, :].unsqueeze(2).to_broadcast([P, PH, PK, PK]), ALU.add))
                u_rest()
            routed()
            ci4 = ci.rearrange("p (t h k) -> p t h k", t=2, h=PH)
            for pair in range(PH):
                tt, h = pair // 4, 2 * (pair % 4)
                best16([cs[:, tt, h + x, :] for x in range(2)], [ci4[:, tt, h + x, :] for x in range(2)],
                       [cand[:, tt, h + x].rearrange("p a b -> p (a b)") for x in range(2)])
                u_rest()
            cs_f = cs.rearrange("p t h k -> p (t h) k")
            gates = choice[:, 2].rearrange("p t (h k) -> p (t h) k", h=PH)
            step(vec.tensor_tensor(gates, cs_f, cs_f[:, :, 0:1].to_broadcast([P, 2 * PH, PK]), ALU.subtract))
            assert done["route"] == ROUTE_GATE
            step(vec.tensor_scalar(cab_u[:, 0], ci, 4, None, ALU.logical_shift_right))
            step(vec.tensor_scalar(cab_u[:, 1], ci, 15, None, ALU.bitwise_and))
            routed()
            step(vec.tensor_copy(cab.rearrange("p s n -> p (s n)"), cab_u.rearrange("p s n -> p (s n)")))
            routed()
            for side in range(2):
                for tt in range(2):
                    step(vec.tensor_tensor(pick[:, tt], cab[:, side, tt * P:(tt + 1) * P].unsqueeze(2).to_broadcast([P, P, PK]),
                                           iota[:, 0:PK].unsqueeze(1).to_broadcast([P, P, PK]), ALU.is_equal))
                    u_rest()
                    routed()
                    pv = pick[:, tt].rearrange("p (h k) a -> p h k a", h=PH)
                    step(vec.tensor_tensor(pv, pv, top_f[:, tt, :, side, :].unsqueeze(2).to_broadcast([P, PH, PK, PK]), ALU.mult))
                    u_rest()
                    routed()
                    step(vec.tensor_reduce(choice[:, side, tt], pick[:, tt], AX.X, ALU.add))
                    u_rest()
                    routed()
            dv.wait_ge(route_exp, 1)
            step(vec.tensor_reduce(small[:, 0:16], gates, AX.X, ALU.add))
            routed()
            step(vec.reciprocal(small[:, 0:16], small[:, 0:16]))
            routed()
            vec.tensor_tensor(gates, gates, small[:, 0:16].unsqueeze(2).to_broadcast([P, 2 * PH, PK]), ALU.mult).then_inc(choices_ready, 1)
            while done["u"] < ROUTED:
                u_rest()

            rest_static(M_PEER + ROUTED)
            dv.wait_ge(ch_copied, 3)

            def onehots(b):
                if b >= 2:
                    dv.wait_ge(gate_rows, b - 1)
                vec.tensor_tensor(onehot[:, b % 2, 0, :, :], iota.unsqueeze(1).to_broadcast([P, 8, P]),
                                  choiceT[:, 0, 8 * b:8 * b + 8].unsqueeze(2).to_broadcast([P, 8, P]), ALU.is_equal)
                for t in range(8 * b, 8 * b + 8):
                    last = vec.tensor_scalar(onehot[:, b % 2, 1, t % 8, :], iota, choiceT[:, 1, t:t + 1], choiceT[:, 2, t:t + 1],
                                             ALU.is_equal, ALU.mult)
                last.then_inc(onehots_ready, 1)

            onehots(0)
            for r in range(GATE_BLOCKS):
                if r:
                    rest_static(M_PEER + ROUTED + r)
                for b in batches_after(r):
                    if b + 1 < BATCHES:
                        onehots(b + 1)

            for half in range(2):
                if half:
                    with dv.Fori(0, HALF // RAW) as lap:
                        for s in range(RAW):
                            rest_block(RAW * lap + (m_u(1) + s), s, s)

                def gate_hidden(mv, r, arena_at):
                    if r % GROUP_J == 0:
                        dv.wait_ge(gate_loaded[r // GROUP_J], mv + (HALF * half + 16 - r))
                    vec.tensor_tensor(wmt[:, r % 2, :], arena[:, arena_at],
                                      gs[:, r // GROUP_J, :].rearrange("p (t j) -> p t j", j=GROUP_J)[:, :, r % GROUP_J],
                                      ALU.mult).then_inc(gated, 1)

                def split_gated(mv, r):
                    dv.wait_ge(wm_hi, mv + (HALF * half + 1))
                    vec.tensor_tensor(wm[:, r % 2, 1, :], wmt[:, r % 2, :], wm[:, r % 2, 0, :].bitcast(F32),
                                      ALU.subtract).then_inc(wm_lo, 1)

                for r in range(2 * GROUP_J):
                    dv.wait_ge(acc_evacuated, M_PEER + HALF * (half + 1) - (r == 0))
                    gate_hidden(r, r, slice(r * T, (r + 1) * T))
                    rest_static(m_v(half) + r)
                    split_gated(r, r)
                with dv.Fori(1, HALF // (2 * GROUP_J)) as lap:
                    for r in range(2 * GROUP_J):
                        mv = 2 * GROUP_J * lap + r
                        gate_hidden(mv, r, bass.ds(2 * GROUP_J * T * lap + r * T, T))
                        rest_block(2 * GROUP_J * lap + (m_v(half) + r), r, r % RAW)
                        split_gated(mv, r)
            dv.wait_ge(gf_loaded, 16)
            for tt in range(2):
                dv.wait_ge(fin_sq, 4 * tt + 4)
                vec.tensor_reduce(small[:, 8 + tt:9 + tt], small[:, 4 * tt:4 * tt + 4], AX.X, ALU.add).then_inc(fin_sum, 1)
                dv.wait_ge(fin_rstd, tt + 1)
                for b in range(4 * tt, 4 * tt + 4):
                    vec.scalar_tensor_tensor(out=arena[:, b * 512:(b + 1) * 512], in0=bank[b][:, :], scalar=small[:, 10 + tt:11 + tt],
                                             in1=hT[:, (b % 4) * 512:(b % 4 + 1) * 512], op0=ALU.mult, op1=ALU.mult).then_inc(fin_ready, 1)


def kernel(x, norm1_g, w_in, rel_bias, ret_gn_g, cmp_pe, cmp_w1, cmp_w2, nsa_out_g, w_out, norm2_g, peer_wq,
           peer_subkeys, peer_u, peer_v, norm_f_g):
    import numpy as _np
    import concourse.bacc as _bacc
    from concourse.bass_utils import run_bass_kernel_spmd as _run

    c = _np.ascontiguousarray

    def blocks(w):
        k, n = w.shape
        return c(_np.asarray(w).reshape(k // P, P, n // P, P).transpose(2, 1, 0, 3).reshape(n // P, P, k))

    def cols(g):
        return _np.asarray(g).reshape(-1, P).T

    x, w_in = _np.asarray(x), _np.asarray(w_in)[0]
    base, mid, decay, onehots = constants()
    cmp_pe, cmp_w1, cmp_w2 = (_np.asarray(v)[0] for v in (cmp_pe, cmp_w1, cmp_w2))
    wide = W_IN_TILES * P
    arrays = {
        "xT": c(x[0].reshape(T, KT, P).transpose(2, 1, 0).reshape(P, KT * T)),
        "base": base, "mid": mid, "decay": decay, "onehots": onehots,
        "gains": c(_np.concatenate([cols(norm1_g), cols(norm2_g), cols(ret_gn_g), cols(nsa_out_g)], 1)),
        "w_gate": c(w_in[:, wide:].reshape(KT, P, -1).transpose(1, 0, 2)),
        "rel_bias": c(rel_bias),
        "subkeys": c(_np.asarray(peer_subkeys)[0].transpose(2, 0, 1)),
        "w_in": c(blocks(w_in[:, :wide])[TILE_ORDER]),
        "cmp_w2": c(cmp_w2.reshape(2, 2, P, DH).transpose(2, 0, 1, 3).reshape(P, 4 * DH)),
        "cmp_pe": c(cmp_pe.transpose(2, 0, 1).reshape(P, 2 * CMP_LEN)),
        "cmp_w1": c(cmp_w1.reshape(2, 2, 16, P, 2, P).transpose(0, 4, 1, 3, 2, 5).reshape(8, P, D)),
        "w_out": c(_np.asarray(w_out)[0].reshape(2, 8, P, 8, 2, P)[::-1].transpose(0, 3, 2, 4, 1, 5).reshape(KT, P, D)),
        "wq": blocks(_np.asarray(peer_wq)[0]),
        "u": c(_np.asarray(peer_u)[0].reshape(NKEYS, NKEYS, KT, P).transpose(1, 3, 2, 0).reshape(NKEYS, P, D)),
        "v": c(_np.asarray(peer_v)[0].reshape(NKEYS, NKEYS, D)),
        "norm_f": c(_np.broadcast_to(_np.asarray(norm_f_g)[None, :], (P, D))),
    }
    nc = _bacc.Bacc("TRN2", target_bir_lowering=False, num_devices=1)
    aps = {k: nc.dram_tensor(f"in_{k}", v.shape, mybir.dt.from_np(v.dtype), kind="ExternalInput").ap() for k, v in arrays.items()}
    out = nc.dram_tensor("out", (T, D), F32, kind="ExternalOutput").ap()
    build(nc, aps, out)
    r = _run(nc, [{f"in_{k}": v for k, v in arrays.items()}], core_ids=[0])
    return r.results[0]["out"].reshape(1, T, D)
```

```python
import math
from contextlib import ExitStack

import concourse.bass as bass
import numpy as np
from concourse import mybir

F32 = mybir.dt.float32
F32R = mybir.dt.float32r
U32 = mybir.dt.uint32
ALU = mybir.AluOpType
ACT = mybir.ActivationFunctionType
AX = mybir.AxisListType

P = 128
T = 256
D = 2048
KT = D // P
EPS = 1e-6
RET_HEADS, RET_DK = 8, 64
NSA_HEADS, GROUPS, DH = 8, 2, 128
HPG = NSA_HEADS // GROUPS
CMP_LEN, CMP_STRIDE = 32, 16
NCMP = (T - CMP_LEN) // CMP_STRIDE + 1
CPAD = 16
N_BUCKETS, MAX_DISTANCE = 32, 128
NEG = -1e30
PH, PK, NKEYS = 8, 16, 128
GROUP_J = 8

KC, VC, VS, VW, NQ, KS, KW, RQ, RK, RV, RG = 0, 2, 4, 6, 8, 16, 18, 20, 24, 28, 36
W_IN_TILES = 44
TILE_ORDER = [32, 33, 34, 35, 38, 39, 42, 43, *range(24, 32), 36, 37, 40, 41, *range(24)]

RAW = 4
PAIRS = 8
M_OUT1, M_OUT2, M_WQ, M_PEER = 44, 52, 60, 76
HALF = NKEYS // 2
def m_u(half): return M_PEER + 2 * HALF * half
def m_v(half): return m_u(half) + HALF
def raw_at(m): return m + 8 if not isinstance(m, int) or m >= PAIRS + 8 else m if m < PAIRS else PAIRS + 2 * (m - PAIRS)

ROUTED = 44
GATE_BLOCKS, BATCHES = HALF - ROUTED, T // 8
BATCH_BLOCKS = GATE_BLOCKS - 4
def batches_after(r): return range(min(-(-BATCHES * r // BATCH_BLOCKS), BATCHES), min(-(-BATCHES * (r + 1) // BATCH_BLOCKS), BATCHES))

BIAS_W = 384
ONEHOT_F = 512
SCALE = float(DH) ** -0.5
LOWEST = -3.4e38
ROUTE_GATE = 5 * 32 + 3 + 5 * 16 + 1


def buckets(dist):
    d = np.maximum(dist, 0)
    exact = N_BUCKETS // 2
    ratio = np.log(np.maximum(d, 1).astype(np.float32) / np.float32(exact)) / np.float32(math.log(MAX_DISTANCE / exact))
    large = np.minimum(exact + (ratio * np.float32(N_BUCKETS - exact)).astype(np.int32), N_BUCKETS - 1)
    return np.where(d < exact, d, large)


def onehot_of(dist):
    out = np.zeros((N_BUCKETS + 1, len(dist)), np.float32)
    out[np.where(dist >= 0, buckets(dist), N_BUCKETS), np.arange(len(dist))] = 1.0
    return out


def constants():
    eye = np.eye(P, dtype=np.float32)
    base = np.concatenate([eye, np.ones((P, P), np.float32), np.tile(np.arange(P, dtype=np.float32), (P, 1))], 1)
    center = eye - 1.0 / P
    swap = np.zeros((P, P), np.float32)
    half = RET_DK // 2
    for m in range(P):
        if m % RET_DK < half:
            swap[m + half, m] = -1.0
        else:
            swap[m - half, m] = 1.0
    inv = (1.0 / (np.float32(10000.0) ** (np.arange(half, dtype=np.float32) / np.float32(half)))).astype(np.float32)
    ang = np.arange(T, dtype=np.float32)[None, :] * inv[np.arange(P) % half][:, None]
    hm = np.zeros((P, NSA_HEADS), np.float32)
    for p in range(P):
        if p % CPAD < NCMP:
            hm[p, p // CPAD] = 1.0
    t = np.arange(T).reshape(2, P)
    seen = np.zeros((P, 2, CPAD), np.float32)
    for c in range(NCMP):
        seen[:, :, c] = (t >= c * CMP_STRIDE + CMP_LEN - 1).T
    mid = np.concatenate([center, swap, np.cos(ang), np.sin(ang), hm, seen.reshape(P, 2 * CPAD)], 1).astype(np.float32)
    log_g = np.log(1.0 - 2.0 ** (-5.0 - np.arange(RET_HEADS, dtype=np.float64)))
    diff = np.arange(T)[None, :] - np.arange(P)[:, None]
    decay = np.where(diff >= 0, np.exp(log_g[:, None, None] * np.maximum(diff, 0)), 0.0) * RET_DK ** -0.5
    decay = decay.transpose(1, 0, 2).reshape(P, RET_HEADS * T).astype(np.float32)
    onehots = np.concatenate([onehot_of(T - 1 - np.arange(BIAS_W)), onehot_of(np.arange(ONEHOT_F) - 256)], 1)
    return base, mid, decay, onehots


MID_W = 2 * P + 2 * T + NSA_HEADS + 2 * CPAD


def build(nc, a, out):
    with ExitStack() as ctx:
        def sb(name, shape, dt=F32):
            return ctx.enter_context(nc.sbuf_tensor(name, shape, dt))

        def sem(name):
            return ctx.enter_context(nc.semaphore(name))

        bank = [ctx.enter_context(nc.psum_tensor(f"bank{b}", [P, 512], F32)) for b in range(8)]

        raw = sb("raw", [P, RAW, D])
        hi = sb("hi", [P, 2, D], F32R)
        lo = sb("lo", [P, 2, D], F32R)
        act = sb("act", [P, KT, 2 * T], F32R)
        hT = sb("hT", [P, 4096])
        arena = sb("arena", [P, 16384])
        gs = sb("gs", [P, 2, 2048])
        wm = sb("wm", [P, 2, 2, T], F32R)
        wmt = sb("wmt", [P, 2, T])
        choiceT = sb("choiceT", [P, 3, T])
        base = sb("base", [P, 3 * P])
        subk = sb("subk", [P, 2, NKEYS])
        gains = sb("gains", [P, 2 * KT + 16])
        gate = sb("gate", [P, 2, 3 * NSA_HEADS])
        small = sb("small", [P, 72])
        rstd = sb("rstd", [P, T])
        ident, ones, iota = base[:, 0:P], base[:, P:2 * P], base[:, 2 * P:3 * P]
        g1, g2 = gains[:, 0:KT], gains[:, KT:2 * KT]
        gn_g, out_g = gains[:, 2 * KT:2 * KT + 8], gains[:, 2 * KT + 8:2 * KT + 16]
        eps, rb = small[:, 32:33], small[:, 40:48]

        proj = arena[:, 0:W_IN_TILES * T]
        def tile(f, n=1): return proj[:, f * T:(f + n) * T]
        rv_tok = arena[:, 11264:13312].rearrange("p (t n) -> p t n", t=2)
        v_tok = arena[:, 13312:14336].rearrange("p (t n) -> p t n", t=2)
        decay = arena[:, 14336:16384]
        sq = arena[:, 4096:8192].rearrange("p (k t) -> p k t", k=KT)
        sq_sum = wmt[:, :, :].rearrange("p a n -> p (a n)")
        onehots = arena[:, 11264:11264 + BIAS_W + ONEHOT_F]
        rb_wide = arena[:, 12288:13312].rearrange("p (h m) -> p h m", h=NSA_HEADS)
        wg = arena[:, 8192:8192 + KT * 24].rearrange("p (k n) -> p k n", k=KT)
        wg_r = wm[:, :, :, :].rearrange("p a b n -> p (a b n)")[:, 0:KT * 48].rearrange("p (k n) -> p k n", k=KT)
        blk_flat = arena[:, RG * T:RG * T + 2 * CMP_LEN * 30]
        blk = blk_flat.rearrange("p (k l n) -> p k l n", k=2, l=CMP_LEN)
        hid_T = choiceT[:, :, :].rearrange("p a n -> p (a n)")[0:30, 0:4 * P]
        gs_flat = gs[:, :, :].rearrange("p a n -> p (a n)")
        wmt_flat = wmt[:, :, :].rearrange("p a n -> p (a n)")
        bias = gs_flat[:, 0:8 * BIAS_W].rearrange("p (h n) -> p h n", h=8)
        vch = gs_flat[:, 3072:4096].rearrange("p (h n) -> p h n", h=8)
        mid = hT[:, 0:MID_W]
        center, swap = mid[:, 0:P], mid[:, P:2 * P]
        cos, sin = mid[:, 2 * P:2 * P + T], mid[:, 2 * P + T:2 * P + 2 * T]
        head_mask = mid[:, 2 * P + 2 * T:2 * P + 2 * T + 8]
        seen = mid[:, MID_W - 2 * CPAD:MID_W].rearrange("p (t c) -> p t c", t=2)
        w2 = hT[:, 832:1344].rearrange("p (k f n) -> p k f n", k=2, f=2)
        hid = hT[:, 1344:1472].rearrange("p (k f n) -> p k f n", k=2, f=2)
        hid_wide = hT[:, 1472:1728].rearrange("p (f n) -> p f n", f=2)
        cbias = hT[:, 1728:1984].rearrange("p (t c h) -> p t c h", t=2, c=CPAD)
        pc = hT[:, 1984:2240].rearrange("p (t h c) -> p t h c", t=2, h=8)
        pcT = hT[:, 2240:2496]
        kc = hT[:, 2496:2528]
        pw = hT[:, 2560:3328].rearrange("p (s n) -> p s n", s=2)
        ptw = hT[:, 3328:4096].rearrange("p (s n) -> p s n", s=2)
        gate_T = choiceT[0:3 * NSA_HEADS, 0, :]
        pe_cols = wmt_flat[:, 0:2 * CMP_LEN]
        res = arena[:, 0:4096]
        def ysq(c):
            at = (4096, 4608, 13312, 13824)[c]
            return arena[:, at:at + 512]

        xn = hT[:, :].rearrange("p (k t) -> p k t", k=KT)
        qT = arena[:, 4096:8192]
        sc = arena[:, 8192:12288].rearrange("p (t g k) -> p t g k", t=2, g=2 * PH)
        cand = gs_flat.rearrange("p (t h a b) -> p t h a b", t=2, h=PH, a=PK)
        pick = gs_flat.rearrange("p (t n a) -> p t n a", t=2, a=PK)
        top = arena[:, 12288:12800].rearrange("p (t g k) -> p t g k", t=2, g=2 * PH)
        top_i = arena[:, 12800:13312].bitcast(U32).rearrange("p (t g k) -> p t g k", t=2, g=2 * PH)
        top_f = arena[:, 13312:13824].rearrange("p (t h s k) -> p t h s k", t=2, h=PH, s=2)
        cs = arena[:, 13824:14080].rearrange("p (t h k) -> p t h k", t=2, h=PH)
        ci = arena[:, 14080:14336].bitcast(U32)
        cab = arena[:, 14336:14848].rearrange("p (s n) -> p s n", s=2)
        cab_u = arena[:, 14336:14848].bitcast(U32).rearrange("p (s n) -> p s n", s=2)
        choice = arena[:, 14848:15616].rearrange("p (s t n) -> p s t n", s=3, t=2)
        onehot = hT[:, :].rearrange("p (b s n j) -> p b s n j", b=2, s=2, n=8)

        rows_dram = nc.dram_tensor("bias_rows", (NSA_HEADS, P, BIAS_W), F32, kind="Internal").ap()
        res_dram = nc.dram_tensor("residual", (P, 4096), F32, kind="Internal").ap()
        gate_dram = nc.dram_tensor("gate_matrix", (NKEYS // GROUP_J, P, T, GROUP_J), F32, kind="Internal").ap()

        raw_loaded = [sem(f"raw_loaded{s}") for s in range(RAW)]
        hi_ready, lo_ready, block_done, cmp_done, acc_evacuated = (
            sem(s) for s in ("hi_ready", "lo_ready", "block_done", "cmp_done", "acc_evacuated"))
        x_loaded = [sem(f"x_loaded{x}") for x in range(2)]
        bias_in_loaded, gains_loaded, base_loaded, wg_loaded, mid_loaded, decay_loaded, xres_loaded = (
            sem(s) for s in ("bias_in_loaded", "gains_loaded", "base_loaded", "wg_loaded", "mid_loaded", "decay_loaded", "xres_loaded"))
        consts_ready, act_hi_ready, act_lo_ready, sq_ready, ss_ready, log_ready, rstd_ready, xn_ready, sq_summed = (
            sem(s) for s in ("consts_ready", "act_hi_ready", "act_lo_ready", "sq_ready", "ss_ready", "log_ready", "rstd_ready", "xn_ready", "sq_summed"))
        rb_wide_ready, rows_ready, rows_copied, rows_stored, bias_loaded, cbias_ready, cbias_copied = (
            sem(s) for s in ("rb_wide_ready", "rows_ready", "rows_copied", "rows_stored", "bias_loaded", "cbias_ready", "cbias_copied"))
        wg_hi_ready, wg_lo_ready, gate_acc, gate_scaled, gate_turned, gate_exp, gate_step, gate_ready = (
            sem(s) for s in ("wg_hi_ready", "wg_lo_ready", "gate_acc", "gate_scaled", "gate_turned", "gate_exp", "gate_step", "gate_ready"))
        blk_ready, gelu_ready, hid_turned, hid_ready, kc_acc, kc_copied, zeroed, wide_ready, vc_acc, vch_ready, v_turned, v_copied = (
            sem(s) for s in ("blk_ready", "gelu_ready", "hid_turned", "hid_ready", "kc_acc", "kc_copied", "zeroed", "wide_ready", "vc_acc", "vch_ready",
                             "v_turned", "v_copied"))
        cs_acc, cstep, cexp, pc_ready, pcT_acc, pcT_copied = (
            sem(s) for s in ("cs_acc", "cstep", "cexp", "pc_ready", "pcT_acc", "pcT_copied"))
        s_acc, s_biased, s_max, s_nmax, p_exp, p_rec, p_coef, p_ready, pT_acc, pT_copied, pv_done, o_copied = (
            sem(s) for s in ("s_acc", "s_biased", "s_max", "s_nmax", "p_exp", "p_rec", "p_coef", "p_ready", "pT_acc",
                             "pT_copied", "pv_done", "o_copied"))
        swapped, rot_sin, rot_cos, rotated, rv_turned, rv_copied = (
            sem(s) for s in ("swapped", "rot_sin", "rot_cos", "rotated", "rv_turned", "rv_copied"))
        osq_ready, oss_acc, olog, orstd, mixed = (sem(s) for s in ("osq_ready", "oss_acc", "olog", "orstd", "mixed"))
        r_acc, r_decayed, y_acc, y_copied, yc_acc, yc_copied, ysq_ready, yss_acc, ylog, yrstd, silu_ready, ynorm = (
            sem(s) for s in ("r_acc", "r_decayed", "y_acc", "y_copied", "yc_acc", "yc_copied", "ysq_ready", "yss_acc", "ylog",
                             "yrstd", "silu_ready", "ynorm"))
        res_stored, q_scores, q_copied, route, route_exp, choices_ready, ch_turned, ch_copied = (
            sem(s) for s in ("res_stored", "q_scores", "q_copied", "route", "route_exp", "choices_ready", "ch_turned", "ch_copied"))
        onehots_ready, gate_rows, gate_evac, res_loaded = (
            sem(s) for s in ("onehots_ready", "gate_rows", "gate_evac", "res_loaded"))
        gate_stored = [sem(f"gate_stored{s}") for s in range(2)]
        gate_loaded = [sem(f"gate_loaded{s}") for s in range(2)]
        gated, wm_hi, wm_lo, half_kept, sums_done, fin_sq, fin_sum, fin_log, fin_rstd, fin_ready, gf_loaded, out_stored = (
            sem(s) for s in ("gated", "wm_hi", "wm_lo", "half_kept", "sums_done", "fin_sq", "fin_sum", "fin_log", "fin_rstd",
                             "fin_ready", "gf_loaded", "out_stored"))

        def stats(u):
            return small[:, 48 + 8 * (u % 2):56 + 8 * (u % 2)]

        units = 2 * NSA_HEADS
        UNIT0, ROT, TURN_V, RET0 = 20, 36, 38, 41

        block = ctx.enter_context(nc.Block())

        @block.sync
        def _(sp):
            sp.dma_start(rb[0:N_BUCKETS, :], a["rel_bias"]).then_inc(bias_in_loaded, 16)
            sp.dma_start(onehots[0:N_BUCKETS + 1, :], a["onehots"]).then_inc(bias_in_loaded, 16)
            sp.dma_start(gains[:, :], a["gains"]).then_inc(gains_loaded, 16)
            for x in range(2):
                sp.dma_start(hT[:, x * 2048:(x + 1) * 2048], a["xT"][:, x * 2048:(x + 1) * 2048]).then_inc(x_loaded[x], 16)

            def load(src, n):
                sp.dma_start(raw[:, n % RAW, :], src).then_inc(raw_loaded[n % RAW], 16)

            def load_after(src, m, s):
                sp.wait_ge(hi_ready, m + 1)
                sp.wait_ge(lo_ready, m + 1)
                sp.dma_start(raw[:, s, :], src).then_inc(raw_loaded[s], 16)

            sp.dma_start(base[:, :], a["base"]).then_inc(base_loaded, 16)
            load(a["w_in"][0], 0)
            sp.dma_start(wg, a["w_gate"]).then_inc(wg_loaded, 16)
            for n in range(1, RAW):
                load(a["w_in"][n], n)
            sp.wait_ge(act_lo_ready, KT)
            sp.wait_ge(sq_ready, 1)
            sp.wait_ge(ss_ready, 1)
            sp.dma_start(mid, a["mid"]).then_inc(mid_loaded, 16)
            sp.dma_start(hT[:, 832:1344], a["cmp_w2"]).then_inc(mid_loaded, 16)
            sp.dma_start(pe_cols, a["cmp_pe"]).then_inc(mid_loaded, 16)
            for m in range(RAW, PAIRS):
                load_after(a["w_in"][m], m - RAW, m % RAW)
            sp.dma_start(decay, a["decay"]).then_inc(decay_loaded, 16)
            sp.dma_start(subk[:, :, :], a["subkeys"]).then_inc(decay_loaded, 16)
            sp.wait_ge(rows_copied, NSA_HEADS)
            sp.dma_start(rows_dram.rearrange("h p n -> p h n"), bias).then_inc(rows_stored, 16)
            for r in range(2):
                load_after(a["w_in"][PAIRS + r], PAIRS - RAW + 2 * r, 2 * r)
                load_after(a["cmp_w1"][r], PAIRS - RAW + 2 * r + 1, 2 * r + 1)
            sp.wait_ge(rows_stored, 16)
            for part in range(2):
                first = P * (1 - part)
                skew = bass.AP(tensor=rows_dram.tensor, offset=P - 1 + first,
                               ap=[[BIAS_W - 1, P], [P * BIAS_W, NSA_HEADS], [1, P * (part + 1)]])
                sp.dma_start(bias[:, :, P * part:P * part + P * (part + 1)], skew).then_inc(bias_loaded, 16)
            with sp.Fori(1, 4) as lap:
                for r in range(2):
                    load_after(a["w_in"][2 * lap + (PAIRS + r)], 2 * lap + (PAIRS - 2 + r), 2 * r)
                    sp.wait_ge(cmp_done, 2 * lap + (r - 1))
                    sp.dma_start(raw[:, 2 * r + 1, :], a["cmp_w1"][2 * lap + r]).then_inc(raw_loaded[2 * r + 1], 16)
            for s in range(RAW):
                if s % 2:
                    sp.wait_ge(cmp_done, 7 + s // 2)
                    sp.dma_start(raw[:, s, :], a["w_in"][16 + s]).then_inc(raw_loaded[s], 16)
                else:
                    load_after(a["w_in"][16 + s], 14 + s // 2, s)
            with sp.Fori(5, W_IN_TILES // RAW) as lap:
                for s in range(RAW):
                    load_after(a["w_in"][RAW * lap + s], RAW * lap + (s - RAW), s)
            for s in range(RAW):
                if s == 2:
                    sp.wait_ge(act_lo_ready, KT + 4)
                    sp.dma_start(res, a["xT"]).then_inc(xres_loaded, 16)
                load_after(a["w_out"][s], M_OUT1 - RAW + s, s)
            with sp.Fori(1, KT // RAW) as lap:
                for s in range(RAW):
                    load_after(a["w_out"][RAW * lap + s], RAW * lap + (M_OUT1 - RAW + s), s)
            with sp.Fori(0, KT // RAW) as lap:
                for s in range(RAW):
                    load_after(a["wq"][RAW * lap + s], RAW * lap + (M_WQ - RAW + s), s)
            for half in range(2):
                with sp.Fori(0, HALF // RAW) as lap:
                    for s in range(RAW):
                        load_after(a["u"][RAW * lap + (HALF * half + s)], RAW * lap + (m_u(half) - RAW + s), s)

                def load_v(mv, s):
                    load_after(a["v"][:, mv + HALF * half, :], mv + (m_v(half) - RAW), s)

                def load_gates(q, g):
                    sp.dma_start(gs[:, g, :], gate_dram[q + (HALF // GROUP_J * half)].rearrange("i t j -> i (t j)")
                                 ).then_inc(gate_loaded[g], 16)

                if half == 0:
                    load_v(0, 0)
                    load_v(1, 1)
                    for s in range(2):
                        sp.wait_ge(gate_stored[s], 16 * (T // 32))
                    for g in range(2):
                        load_gates(g, g)
                        load_v(2 + g, 2 + g)
                    sp.wait_ge(gate_rows, BATCHES)
                    sp.wait_ge(res_stored, 16)
                    sp.dma_start(hT[:, :], res_dram).then_inc(res_loaded, 16)
                    for mv in range(RAW, 2 * GROUP_J):
                        load_v(mv, mv % RAW)
                with sp.Fori(1 if half == 0 else 0, HALF // GROUP_J // 2) as lap:
                    for g in range(2):
                        sp.wait_ge(gated, 2 * GROUP_J * lap + (GROUP_J * (g - 1) + HALF * half))
                        load_gates(2 * lap + g, g)
                        for r in range(GROUP_J):
                            load_v(2 * GROUP_J * lap + (GROUP_J * g + r), r % RAW)
            sp.wait_ge(block_done, m_v(1) + 8)
            sp.dma_start(hT[:, 0:D], a["norm_f"]).then_inc(gf_loaded, 16)
            for tt in range(2):
                for part in range(2):
                    sp.wait_ge(fin_ready, 4 * tt + 2 * part + 2)
                    cols = slice(part * D // 2, (part + 1) * D // 2)
                    sp.dma_start(out[tt * P:(tt + 1) * P, cols], arena[:, tt * D:(tt + 1) * D][:, cols]).then_inc(out_stored, 16)
            sp.wait_ge(out_stored, 64)

        @block.gpsimd
        def _(pool):
            pool.wait_ge(acc_evacuated, M_WQ)
            pool.dma_start(res_dram, res).then_inc(res_stored, 16)
            with pool.Fori(0, T // 32) as lap:
                for s in range(2):
                    pool.wait_ge(gate_evac, 4 * lap + (2 * s + 2))
                    pool.dma_start(gate_dram.rearrange("g i t j -> i g (t j)")[:, :, bass.ds((32 * lap + 16 * s) * GROUP_J, 16 * GROUP_J)],
                                   gs[:, s, :].rearrange("p (g n) -> p g n", g=NKEYS // GROUP_J)).then_inc(gate_stored[s], 16)

        @block.tensor
        def _(pe):
            mm = nc.tensor.matmul

            def product(dst, wh, wl, mh, ml, first, last):
                mm(dst, wh, mh, start=first, stop=False)
                mm(dst, wh, ml, start=False, stop=False)
                return mm(dst, wl, mh, start=False, stop=last)

            def weights_block(m, s, others=0, act_count=0, act_step=1):
                pe.wait_ge(hi_ready, m + 1)
                pe.wait_ge(lo_ready, m + 1)
                if not (isinstance(m, int) and m < 2):
                    pe.wait_ge(acc_evacuated, m - (others + 1))
                for k in range(KT):
                    if act_count and k % 4 == 0:
                        pe.wait_ge(act_hi_ready, act_count + act_step * (k // 4))
                        pe.wait_ge(act_lo_ready, act_count + act_step * (k // 4))
                    w = slice(k * P, (k + 1) * P)
                    last = product(bank[s % 2][:, 0:T], hi[:, s % 2, w], lo[:, s % 2, w], act[:, k, 0:T], act[:, k, T:2 * T],
                                   k == 0, k == KT - 1)
                last.then_inc(block_done, 1)

            def w_out_block(m, s, k0, act_count=0):
                pe.wait_ge(hi_ready, m + 1)
                pe.wait_ge(lo_ready, m + 1)
                pe.wait_ge(acc_evacuated, m - 1)
                for f in range(2):
                    for k in range(8):
                        if act_count and f == 0 and k % 2 == 0:
                            pe.wait_ge(act_hi_ready, act_count + k // 2)
                            pe.wait_ge(act_lo_ready, act_count + k // 2)
                        w = slice((8 * f + k) * P, (8 * f + k + 1) * P)
                        last = product(bank[s % 2][:, f * T:(f + 1) * T], hi[:, s % 2, w], lo[:, s % 2, w],
                                       act[:, k0 + k, 0:T], act[:, k0 + k, T:2 * T], k == 0, k == 7)
                last.then_inc(block_done, 1)

            rows = N_BUCKETS + 1
            def bias_rows(h):
                mm(bank[2 + h % 4][:, 0:BIAS_W], rb_wide[0:rows, h, :], onehots[0:rows, 0:BIAS_W],
                   start=True, stop=True).then_inc(rows_ready, 1)

            pe.wait_ge(rb_wide_ready, 1)
            pe.wait_ge(bias_in_loaded, 32)
            for h in range(4):
                bias_rows(h)
            for w in range(8 + NCMP):
                z = BIAS_W + 256 - CMP_STRIDE * (w - 8) - (CMP_LEN - 1)
                last = mm(bank[6][:, w * 8:w * 8 + 8], onehots[0:rows, z:z + P], rb[0:rows, :], start=True, stop=True)
            last.then_inc(cbias_ready, 1)
            weights_block(0, 0, act_count=4, act_step=4)
            pe.wait_ge(base_loaded, 16)
            pe.wait_ge(sq_summed, 1)
            mm(bank[7][:, 0:T], ones, sq_sum[:, 0:T], start=True, stop=True).then_inc(ss_ready, 1)
            weights_block(1, 1)
            weights_block(2, 2)
            for h in range(4, 8):
                pe.wait_ge(rows_copied, h - 3)
                bias_rows(h)
            weights_block(3, 3)
            pe.wait_ge(rstd_ready, 1)
            pe.wait_ge(wg_hi_ready, 1)
            pe.wait_ge(wg_lo_ready, 1)
            for k in range(KT):
                last = product(bank[7][0:24, T:2 * T], wg_r[:, k, 0:24], wg_r[:, k, 24:48], act[:, k, 0:T], act[:, k, T:2 * T],
                               k == 0, k == KT - 1)
            last.then_inc(gate_acc, 1)
            weights_block(4, 4)
            pe.wait_ge(gate_scaled, 1)
            for tt in range(2):
                last = nc.tensor.transpose(bank[7][:, T + tt * 24:T + (tt + 1) * 24], gate_T[:, tt * P:(tt + 1) * P], ident[0:24, 0:24])
            last.then_inc(gate_turned, 1)
            for m in range(5, PAIRS):
                weights_block(m, m)
            pe.wait_ge(blk_ready, 8)
            pe.wait_ge(gate_exp, 2)
            for j in range(8):
                kind, q, slot = j // 4, j % 4, 2 * (j % 2) + 1
                weights_block(PAIRS + j, j)
                pe.wait_ge(raw_loaded[slot], 16 * (PAIRS // RAW + 1 + j // 2))
                for l in range(8):
                    at = (CMP_LEN * kind + 8 * q + l) * 30
                    last = mm(bank[7][0:30, 2 * P * kind:2 * P * (kind + 1)], blk_flat[:, at:at + 30],
                              raw[:, slot, l * 2 * P:(l + 1) * 2 * P], start=(q == 0 and l == 0), stop=(q == 3 and l == 7))
                last.then_inc(cmp_done, 1)
            weights_block(16, 16)
            pe.wait_ge(gelu_ready, 1)
            for e in range(4):
                last = nc.tensor.transpose(bank[4][:, e * 32:e * 32 + 30], hid_T[:, e * P:(e + 1) * P], ident[0:30, 0:30])
            last.then_inc(hid_turned, 1)
            pe.wait_ge(rows_copied, NSA_HEADS)
            for tt in range(2):
                for j, f in enumerate((VS, VS + 1, VW, VW + 1)):
                    last = nc.tensor.transpose(bank[2 + tt][:, j * P:(j + 1) * P], tile(f)[:, tt * P:(tt + 1) * P], ident)
                last.then_inc(v_turned, 1)
            pe.wait_ge(mid_loaded, 48)
            pe.wait_ge(hid_ready, 1)
            for f in range(2):
                last = mm(bank[4][:, 0:30], w2[:, 0, f, :], hid[:, 0, f, 0:30], start=(f == 0), stop=(f == 1))
            last.then_inc(kc_acc, 1)
            pe.wait_ge(wide_ready, 2)
            for f in range(2):
                last = mm(bank[5][:, 0:DH], hid_wide[:, f, :], w2[:, 1, f, :], start=(f == 0), stop=(f == 1))
            last.then_inc(vc_acc, 1)
            weights_block(17, 17)
            pe.wait_ge(kc_copied, 1)
            pe.wait_ge(cbias_copied, 2)
            for tt in range(2):
                for h in range(NSA_HEADS):
                    at, g = (tt * 8 + h) * CPAD, h // HPG
                    last = mm(bank[6][:, at:at + NCMP], tile(NQ + h)[:, tt * P:(tt + 1) * P],
                              kc[:, g * NCMP:(g + 1) * NCMP], start=True, stop=True)
            last.then_inc(cs_acc, 1)
            weights_block(18, 18)
            weights_block(19, 19)
            pe.wait_ge(pc_ready, 1)
            for tt in range(2):
                last = nc.tensor.transpose(bank[7][:, tt * P:(tt + 1) * P], pc[:, tt, :, :].rearrange("p h c -> p (h c)"), ident)
            last.then_inc(pcT_acc, 1)

            def scores(u):
                h, kt = u // 2, (KS, KW)[u % 2] + u // 2 // HPG
                if u >= 2:
                    pe.wait_ge(s_biased, u - 1)
                q, dst = tile(NQ + h), bank[2 + u % 2]
                mm(dst[:, 0:P], q[:, 0:P], tile(kt)[:, 0:P], start=True, stop=True)
                mm(dst[:, P:3 * P], q[:, P:T], tile(kt), start=True, stop=True).then_inc(s_acc, 1)

            def turn(u):
                pe.wait_ge(p_ready, u + 1)
                if u >= 2:
                    pe.wait_ge(pT_copied, u - 1)
                for j in range(3):
                    last = nc.tensor.transpose(bank[4 + u % 2][:, j * P:(j + 1) * P], pw[:, u % 2, j * P:(j + 1) * P], ident)
                last.then_inc(pT_acc, 1)

            def weigh(u):
                h, branch = u // 2, u % 2
                g, dst = h // HPG, bank[6 + h % 2]
                at = branch * T + g * DH
                if branch == 0:
                    if h >= 2:
                        pe.wait_ge(o_copied, h - 1)
                    mm(dst[:, 0:T], vch[:, h, :], pcT, start=True, stop=False)
                pe.wait_ge(pT_copied, u + 1)
                mm(dst[:, 0:T], v_tok[:, 0, at:at + DH], ptw[:, u % 2, 0:T], start=False, stop=False)
                mm(dst[:, P:T], v_tok[:, 1, at:at + DH], ptw[:, u % 2, T:3 * P],
                   start=False, stop=(branch == 1)).then_inc(pv_done, 1)

            def r_scores(h):
                part = slice(RET_DK * (h % 2), RET_DK * (h % 2 + 1))
                q, k, dst = tile(RQ + h // 2)[part, :], tile(RK + h // 2)[part, :], bank[2 + h % 2]
                if h >= 2:
                    pe.wait_ge(r_decayed, h - 1)
                mm(dst[:, 0:T], k[:, 0:P], q, start=True, stop=True)
                mm(dst[:, T:3 * P], k[:, P:T], q[:, P:T], start=True, stop=True).then_inc(r_acc, 1)

            def r_weigh(h):
                pe.wait_ge(r_decayed, h + 1)
                if h >= 2:
                    pe.wait_ge(y_copied, h - 1)
                dst = bank[4 + h % 2]
                mm(dst[:, 0:T], rv_tok[:, 0, h * P:(h + 1) * P], pw[:, h % 2, 0:T], start=True, stop=False)
                mm(dst[:, P:T], rv_tok[:, 1, h * P:(h + 1) * P], pw[:, h % 2, T:3 * P],
                   start=False, stop=True).then_inc(y_acc, 1)

            for m in range(UNIT0, M_OUT2):
                if m < M_OUT1:
                    weights_block(m, m)
                else:
                    w_out_block(m, m, 8, KT + 1 if m == M_OUT1 else 0)
                u = m - UNIT0
                if u < units:
                    if u == 0:
                        pe.wait_ge(v_copied, 2)
                    scores(u)
                if 1 <= u <= units:
                    if u == 1:
                        pe.wait_ge(kc_copied, 1)
                        pe.wait_ge(vch_ready, NSA_HEADS)
                    turn(u - 1)
                if 2 <= u <= units + 1:
                    if u == 2:
                        pe.wait_ge(pcT_copied, 1)
                    weigh(u - 2)
                if ROT <= m < ROT + 2:
                    for i in range(2 * (m - ROT), 2 * (m - ROT) + 2):
                        if i < 2:
                            pe.wait_ge(s_biased, units - 1 + i)
                        else:
                            pe.wait_ge(rot_sin, i - 1)
                        mm(bank[2 + i % 2][:, :], swap, tile(RQ + 2 * i, 2), start=True, stop=True).then_inc(swapped, 1)
                if TURN_V <= m < TURN_V + 2:
                    tt = m - TURN_V
                    for half in range(2):
                        if tt == 0:
                            pe.wait_ge(pT_copied, units - 1 + half)
                        else:
                            pe.wait_ge(rv_copied, half + 1)
                        for j in range(4):
                            last = nc.tensor.transpose(bank[4 + half][:, j * P:(j + 1) * P],
                                                       tile(RV + 4 * half + j)[:, tt * P:(tt + 1) * P], ident)
                        last.then_inc(rv_turned, 1)
                if m == TURN_V + 1:
                    pe.wait_ge(osq_ready, 1)
                    pe.wait_ge(o_copied, NSA_HEADS)
                    pe.wait_ge(rot_sin, 4)
                    for c in range(4):
                        mm(bank[(2, 3, 6, 7)[c]][:, :], ones, tile(2 * c, 2), start=True, stop=True).then_inc(oss_acc, 1)
                i = m - RET0
                if 0 <= i < 4:
                    if i == 0:
                        pe.wait_ge(rotated, 4)
                        pe.wait_ge(olog, 4)
                        pe.wait_ge(rv_copied, 4)
                    r_scores(2 * i)
                    r_scores(2 * i + 1)
                if 1 <= i <= 4:
                    r_weigh(2 * i - 2)
                    r_weigh(2 * i - 1)
                if 2 <= i <= 5:
                    c = i - 2
                    pe.wait_ge(y_copied, 2 * c + 2)
                    if c:
                        pe.wait_ge(yc_copied, c)
                    mm(bank[6][:, :], center, tile(RV + 2 * c, 2), start=True, stop=True).then_inc(yc_acc, 1)
                if 3 <= i <= 6:
                    c = i - 3
                    pe.wait_ge(ysq_ready, c + 1)
                    if c:
                        pe.wait_ge(ylog, c)
                    mm(bank[7][:, :], ones, ysq(c), start=True, stop=True).then_inc(yss_acc, 1)

            pe.wait_ge(act_hi_ready, KT + 5)
            pe.wait_ge(act_lo_ready, KT + 5)
            pe.wait_ge(ylog, 4)

            for c in range(8):
                w_out_block(M_OUT2 + c, c, 0)
            pe.wait_ge(sq_summed, 8)
            for f in range(2):
                mm(bank[7][:, 0:T], ones, sq_sum[:, f * T:(f + 1) * T], start=(f == 0), stop=False)
            pe.wait_ge(sq_ready, 9)
            for f in range(2):
                last = mm(bank[7][:, 0:T], ones, xn[:, 14 + f, :], start=False, stop=(f == 1))
            last.then_inc(ss_ready, 1)

            weights_block(M_WQ, 0, act_count=KT + 6)
            for s in range(1, RAW):
                weights_block(M_WQ + s, s)
            with pe.Fori(1, KT // RAW) as lap:
                for s in range(RAW):
                    weights_block(RAW * lap + (M_WQ + s), s)
            for j in range(RAW):
                weights_block(M_PEER + j, j)
                if j == 0:
                    pe.wait_ge(decay_loaded, 32)
                    pe.wait_ge(acc_evacuated, M_PEER)
                    for x in range(8):
                        tt, g0 = x // 4, 4 * (x % 4)
                        if x >= 6:
                            pe.wait_ge(q_copied, x - 5)
                        for g in range(g0, g0 + 4):
                            last = mm(bank[2 + x % 6][:, (g % 4) * P:(g % 4 + 1) * P],
                                      qT[:, g * T + tt * P:g * T + (tt + 1) * P], subk[:, g % 2, :], start=True, stop=True)
                        last.then_inc(q_scores, 1)
            with pe.Fori(1, ROUTED // RAW) as lap:
                for s in range(RAW):
                    weights_block(RAW * lap + (M_PEER + s), s)
            pe.wait_ge(choices_ready, 1)
            pe.wait_ge(q_copied, 8)
            for x in range(6):
                last = nc.tensor.transpose(bank[2 + x // 4][:, (x % 4) * P:(x % 4 + 1) * P], choice[:, x // 2, x % 2, :], ident)
            last.then_inc(ch_turned, 1)

            def gate_batch(b):
                pe.wait_ge(onehots_ready, b + 1)
                if b >= 2:
                    pe.wait_ge(gate_evac, b - 1)
                for t in range(8):
                    last = mm(bank[4 + 2 * (b % 2) + t // 4][:, (t % 4) * P:(t % 4 + 1) * P],
                              onehot[:, b % 2, 0, t, :], onehot[:, b % 2, 1, t, :], start=True, stop=True)
                last.then_inc(gate_rows, 1)

            for r in range(GATE_BLOCKS):
                weights_block(M_PEER + ROUTED + r, r)
                for b in batches_after(r):
                    gate_batch(b)

            for half in range(2):
                if half:
                    pe.wait_ge(half_kept, 2)
                    with pe.Fori(0, HALF // RAW) as lap:
                        for s in range(RAW):
                            weights_block(RAW * lap + (m_u(1) + s), s, HALF)
                    pe.wait_ge(half_kept, 8)
                else:
                    pe.wait_ge(gate_evac, BATCHES)

                def v_block(mv, s, opening=False, closing=False):
                    pe.wait_ge(hi_ready, mv + (m_v(half) + 1))
                    pe.wait_ge(lo_ready, mv + (m_v(half) + 1))
                    pe.wait_ge(wm_hi, mv + (HALF * half + 1))
                    pe.wait_ge(wm_lo, mv + (HALF * half + 1))
                    w, vh, vl = wm[:, s % 2, :, :], hi[:, s % 2, :], lo[:, s % 2, :]
                    parts = ((0, vl), (0, vh), (1, vh))
                    order = [(x, dc) for dc in range(4) for x in range(3)] if closing else [(x, dc) for x in range(3) for dc in range(4)]
                    for tt in range(2):
                        for x, dc in order:
                            part, moving = parts[x]
                            last = mm(bank[tt * 4 + dc][:, :], w[:, part, tt * P:(tt + 1) * P],
                                      moving[:, dc * 512:(dc + 1) * 512], start=opening and x == 0,
                                      stop=closing and x == 2, skip_group_check=True)
                            if closing and x == 2 and (tt, dc) != (1, 3):
                                last.then_inc(sums_done, 1)
                    last.then_inc(block_done, 1)

                pe.wait_ge(acc_evacuated, M_PEER + HALF * (half + 1))
                for s in range(RAW):
                    v_block(s, s, opening=(s == 0))
                if half == 0:
                    pe.wait_ge(res_loaded, 16)
                for b in range(8):
                    tt, dc = b // 4, b % 4
                    if half == 0:
                        for j in range(4):
                            mm(bank[b][:, j * P:(j + 1) * P], hT[:, (4 * dc + j) * T + tt * P:(4 * dc + j) * T + (tt + 1) * P],
                               ident, start=False, stop=False, skip_group_check=True)
                    else:
                        mm(bank[b][:, :], ident, hT[:, tt * D + dc * 512:tt * D + (dc + 1) * 512],
                           start=False, stop=False, skip_group_check=True)
                with pe.Fori(1, HALF // RAW - 1) as lap:
                    for s in range(RAW):
                        v_block(RAW * lap + s, s)
                for s in range(RAW):
                    v_block(HALF - RAW + s, s, closing=(s == RAW - 1))

        @block.scalar
        def _(ac):
            do = nc.scalar.activation

            def round_block(m, s, raw_slot, laps):
                ac.wait_ge(raw_loaded[raw_slot], 16 * laps)
                if not (isinstance(m, int) and m < 2):
                    ac.wait_ge(block_done, m - 1)
                do(hi[:, s % 2, :], raw[:, raw_slot, :], ACT.Copy).then_inc(hi_ready, 1)

            def round_static(m):
                n = raw_at(m)
                round_block(m, m, n % RAW, n // RAW + 1)

            def round_lap(m, lap, s, base_lap):
                ac.wait_ge(raw_loaded[s], 16 * lap + 16 * base_lap)
                ac.wait_ge(block_done, m - 1)
                do(hi[:, s % 2, :], raw[:, s, :], ACT.Copy).then_inc(hi_ready, 1)

            def rsqrt(src, dst, width, logged, ready, count):
                do(dst, src, ACT.Ln, bias=eps, scale=1.0 / width).then_inc(logged, 1)
                ac.wait_ge(logged, count)
                do(dst, dst, ACT.Exp, scale=-0.5).then_inc(ready, 1)

            ac.wait_ge(gains_loaded, 16)
            for k in range(KT):
                if k % 8 == 0:
                    ac.wait_ge(x_loaded[k // 8], 16)
                do(act[:, k, 0:T], hT[:, k * T:(k + 1) * T], ACT.Copy, scale=g1[:, k:k + 1]).then_inc(act_hi_ready, 1)
            round_static(0)
            do(sq.rearrange("p k t -> p (k t)"), hT[:, :], ACT.Square).then_inc(sq_ready, 1)
            ac.wait_ge(consts_ready, 1)
            for m in range(1, PAIRS):
                round_static(m)
                if m == 1:
                    for h in range(4):
                        ac.wait_ge(rows_ready, h + 1)
                        do(bias[:, h, :], bank[2 + h][:, 0:BIAS_W], ACT.Copy).then_inc(rows_copied, 1)
                    ac.wait_ge(ss_ready, 1)
                    rsqrt(bank[7][:, 0:T], rstd[:, :], D, log_ready, rstd_ready, 1)
                if m == 2:
                    ac.wait_ge(wg_loaded, 16)
                    do(wg_r[:, :, 0:24], wg, ACT.Copy).then_inc(wg_hi_ready, 1)
                if m == 3:
                    for h in range(4, 8):
                        ac.wait_ge(rows_ready, h + 1)
                        do(bias[:, h, :], bank[2 + h % 4][:, 0:BIAS_W], ACT.Copy).then_inc(rows_copied, 1)
                if m == 5:
                    ac.wait_ge(gate_turned, 1)
                    for tt in range(2):
                        do(gate[:, tt, :], bank[7][:, T + tt * 24:T + (tt + 1) * 24], ACT.Exp, scale=-1.0).then_inc(gate_exp, 1)
            with ac.Fori(0, 4) as lap:
                for r in range(2):
                    ac.wait_ge(raw_loaded[2 * r], 16 * lap + 16 * (PAIRS // RAW + 1))
                    ac.wait_ge(block_done, 2 * lap + (PAIRS + r - 1))
                    do(hi[:, r, :], raw[:, 2 * r, :], ACT.Copy).then_inc(hi_ready, 1)
            round_static(16)
            ac.wait_ge(cmp_done, 8)
            do(hid_T, bank[7][0:30, :], ACT.Gelu_apprx_tanh).then_inc(gelu_ready, 1)
            round_static(17)
            ac.wait_ge(kc_acc, 1)
            do(kc[:, 0:30], bank[4][:, 0:30], ACT.Copy).then_inc(kc_copied, 1)
            ac.wait_ge(cbias_copied, 2)
            for tt in range(2):
                ac.wait_ge(v_turned, tt + 1)
                do(v_tok[:, tt, :], bank[2 + tt][:, :], ACT.Copy).then_inc(v_copied, 1)
            round_static(18)
            ac.wait_ge(cstep, 5)
            pcf = pc[:, :, :, 0:NCMP].rearrange("p t h c -> p (t h) c")
            do(pcf, pcf, ACT.Exp).then_inc(cexp, 1)
            round_static(19)

            def exps(u):
                ac.wait_ge(s_nmax, u + 1)
                st = stats(u)
                do(pw[:, u % 2, 0:P], pw[:, u % 2, 0:P], ACT.Exp, bias=st[:, 2:3], accum_out=st[:, 4:5])
                do(pw[:, u % 2, P:3 * P], pw[:, u % 2, P:3 * P], ACT.Exp, bias=st[:, 3:4],
                   accum_out=st[:, 5:6]).then_inc(p_exp, 1)

            def copy_pT(u):
                ac.wait_ge(pT_acc, u + 1)
                if u >= 2:
                    ac.wait_ge(pv_done, u - 1)
                do(ptw[:, u % 2, :], bank[4 + u % 2][:, 0:3 * P], ACT.Copy).then_inc(pT_copied, 1)

            def copy_o(h):
                ac.wait_ge(pv_done, 2 * h + 2)
                do(tile(NQ + h), bank[6 + h % 2][:, 0:T], ACT.Copy).then_inc(o_copied, 1)

            for m in range(UNIT0, M_OUT2):
                round_static(m)
                if m == M_OUT1:
                    ac.wait_ge(mixed, 8)
                    ac.wait_ge(block_done, W_IN_TILES)
                    for k in range(0, 8, 2):
                        do(act[:, 8 + k:10 + k, 0:T], tile(NQ + k, 2).rearrange("p (k t) -> p k t", k=2), ACT.Copy).then_inc(act_hi_ready, 1)
                if m == UNIT0:
                    ac.wait_ge(pcT_acc, 1)
                    do(pcT, bank[7][:, 0:T], ACT.Copy).then_inc(pcT_copied, 1)
                u = m - UNIT0 - 1
                if 1 <= u <= units:
                    copy_pT(u - 1)
                if 0 <= u < units:
                    exps(u)
                if u >= 3 and u % 2 and (u - 3) // 2 < NSA_HEADS:
                    copy_o((u - 3) // 2)
                if m == TURN_V:
                    ac.wait_ge(o_copied, NSA_HEADS)
                    do(tile(0, 8), tile(NQ, 8), ACT.Square).then_inc(osq_ready, 1)
                if m in (TURN_V + 1, TURN_V + 2):
                    for half in range(2):
                        tt = m - TURN_V - 1
                        ac.wait_ge(rv_turned, 2 * tt + half + 1)
                        do(rv_tok[:, tt, half * 512:(half + 1) * 512], bank[4 + half][:, :], ACT.Copy).then_inc(rv_copied, 1)
                if m == TURN_V + 2:
                    for c in range(4):
                        ac.wait_ge(oss_acc, c + 1)
                        do(tile(2 * c, 2), bank[(2, 3, 6, 7)[c]][:, :], ACT.Ln, bias=eps, scale=1.0 / DH).then_inc(olog, 1)
                if m == TURN_V + 3:
                    ac.wait_ge(olog, 4)
                    do(tile(0, 8), tile(0, 8), ACT.Exp, scale=-0.5).then_inc(orstd, 1)
                i = m - RET0 - 2
                if 0 <= i < 4:
                    for h in (2 * i, 2 * i + 1):
                        ac.wait_ge(y_acc, h + 1)
                        do(tile(RV + h), bank[4 + h % 2][:, 0:T], ACT.Copy).then_inc(y_copied, 1)
                if 1 <= i <= 4:
                    c = i - 1
                    ac.wait_ge(yc_copied, c + 1)
                    do(ysq(c), tile(RV + 2 * c, 2), ACT.Square).then_inc(ysq_ready, 1)
                if i == 1:
                    ac.wait_ge(acc_evacuated, W_IN_TILES)
                    do(tile(RG, 8), tile(RG, 8), ACT.Silu).then_inc(silu_ready, 1)
                if 2 <= i <= 5:
                    c = i - 2
                    ac.wait_ge(yss_acc, c + 1)
                    do(ysq(c), bank[7][:, :], ACT.Ln, bias=eps, scale=1.0 / P).then_inc(ylog, 1)
                if i == 6:
                    ac.wait_ge(ylog, 4)
                    for c in range(4):
                        do(ysq(c), ysq(c), ACT.Exp, scale=-0.5).then_inc(yrstd, 1)
                if i == 8:
                    ac.wait_ge(ynorm, 16)
                    do(act[:, 0:8, 0:T], tile(RV, 8).rearrange("p (k t) -> p k t", k=8), ACT.Copy).then_inc(act_hi_ready, 1)

            for c in range(9):
                round_static(M_OUT2 + c)
                if c:
                    ac.wait_ge(acc_evacuated, M_OUT2 + c)
                    do(hT[:, (c - 1) * 512:c * 512], res[:, (c - 1) * 512:c * 512], ACT.Square).then_inc(sq_ready, 1)
            ac.wait_ge(ss_ready, 2)
            rsqrt(bank[7][:, 0:T], rstd[:, :], D, log_ready, rstd_ready, 2)
            for c in range(4):
                ac.wait_ge(xn_ready, 4 * c + 4)
                do(act[:, 4 * c:4 * c + 4, 0:T], xn[:, 4 * c:4 * c + 4, :], ACT.Copy).then_inc(act_hi_ready, 1)

            def evacuate(m, s, dst, func):
                ac.wait_ge(block_done, m + 1)
                do(dst, bank[s % 2][:, 0:T], func).then_inc(acc_evacuated, 1)

            for s in range(1, RAW):
                round_static(M_WQ + s)
                evacuate(M_WQ + s - 1, s - 1, qT[:, (s - 1) * T:s * T], ACT.Copy)
            with ac.Fori(1, KT // RAW) as lap:
                for s in range(RAW):
                    m = RAW * lap + (M_WQ + s)
                    round_lap(m, lap, s, (M_WQ + 8) // RAW + 1)
                    evacuate(RAW * lap + (M_WQ + s - 1), s - 1, qT[:, bass.ds(RAW * T * lap + (s - 1) * T, T)], ACT.Copy)
            round_static(M_PEER)
            evacuate(M_PEER - 1, 1, qT[:, (KT - 1) * T:KT * T], ACT.Copy)
            ac.wait_ge(res_stored, 16)
            for j in range(1, RAW):
                round_static(M_PEER + j)
                evacuate(M_PEER + j - 1, j - 1, arena[:, (j - 1) * T:j * T], ACT.Gelu_apprx_tanh)
                if j == 1:
                    for x in range(8):
                        ac.wait_ge(q_scores, x + 1)
                        do(sc[:, x // 4, 4 * (x % 4):4 * (x % 4) + 4, :].rearrange("p g k -> p (g k)"),
                           bank[2 + x % 6][:, :], ACT.Copy).then_inc(q_copied, 1)

            def hidden_lap(lap, half):
                for s in range(RAW):
                    m = RAW * lap + (m_u(half) + s)
                    round_lap(m, lap, s, (m_u(half) + 8) // RAW + 1)
                    ac.wait_ge(block_done, RAW * lap + (m_u(half) + s))
                    do(arena[:, bass.ds(RAW * T * lap + (s - 1) * T, T)], bank[(s - 1) % 2][:, 0:T],
                       ACT.Gelu_apprx_tanh).then_inc(acc_evacuated, 1)

            with ac.Fori(1, ROUTED // RAW - 1) as lap:
                hidden_lap(lap, 0)
            ac.wait_ge(route, ROUTE_GATE)
            do(choice[:, 2], choice[:, 2], ACT.Exp).then_inc(route_exp, 1)
            hidden_lap(ROUTED // RAW - 1, 0)
            m0 = M_PEER + ROUTED
            round_static(m0)
            evacuate(m0 - 1, 1, arena[:, (ROUTED - 1) * T:ROUTED * T], ACT.Gelu_apprx_tanh)
            ac.wait_ge(ch_turned, 1)
            for part in range(3):
                do(choiceT[:, part, :], bank[2 + part // 2][:, (part % 2) * T:(part % 2 + 1) * T], ACT.Copy).then_inc(ch_copied, 1)

            def gate_copy(b):
                ac.wait_ge(gate_rows, b + 1)
                if b % 2 == 0 and b >= 4:
                    ac.wait_ge(gate_stored[b // 2 % 2], 16 * (b // 4))
                for x in range(2):
                    dst = gs[:, b // 2 % 2, :].rearrange("p (g t j) -> p t g j", g=NKEYS // GROUP_J, t=16)
                    t0 = 8 * (b % 2) + 4 * x
                    last = do(dst[:, t0:t0 + 4, :, :], bank[4 + 2 * (b % 2) + x][:, :].rearrange("p (t g j) -> p t g j", t=4, j=GROUP_J),
                              ACT.Copy)
                last.then_inc(gate_evac, 1)

            for r in range(GATE_BLOCKS):
                if r < GATE_BLOCKS - 1:
                    round_static(m0 + r + 1)
                if r:
                    evacuate(m0 + r - 1, r - 1, arena[:, (ROUTED + r - 1) * T:(ROUTED + r) * T], ACT.Gelu_apprx_tanh)
                    for b in batches_after(r - 1):
                        gate_copy(b)

            for half in range(2):
                if half:
                    for s in range(1, RAW):
                        round_static(m_u(1) + s)
                        evacuate(m_u(1) + s - 1, s - 1, arena[:, (s - 1) * T:s * T], ACT.Gelu_apprx_tanh)
                    with ac.Fori(1, HALF // RAW) as lap:
                        hidden_lap(lap, 1)
                round_static(m_v(half))
                evacuate(m_v(half) - 1, 1, arena[:, (HALF - 1) * T:HALF * T], ACT.Gelu_apprx_tanh)

                def round_gated(mv, s):
                    ac.wait_ge(gated, mv + (HALF * half + 1))
                    do(wm[:, s % 2, 0, :], wmt[:, s % 2, :], ACT.Copy).then_inc(wm_hi, 1)

                round_gated(0, 0)
                for s in range(1, RAW):
                    round_static(m_v(half) + s)
                    round_gated(s, s)
                with ac.Fori(1, HALF // RAW) as lap:
                    for s in range(RAW):
                        round_lap(RAW * lap + (m_v(half) + s), lap, s, (m_v(half) + 8) // RAW + 1)
                        round_gated(RAW * lap + s, s)
                if half == 0:
                    round_static(m_u(1))
                    for b in range(8):
                        if b < 7:
                            ac.wait_ge(sums_done, b + 1)
                        else:
                            ac.wait_ge(block_done, m_v(0) + HALF)
                        do(hT[:, b * 512:(b + 1) * 512], bank[b][:, :], ACT.Copy).then_inc(half_kept, 1)
            for b in range(8):
                if b < 7:
                    ac.wait_ge(sums_done, 7 + b + 1)
                else:
                    ac.wait_ge(block_done, m_v(1) + HALF)
                do(arena[:, 8192 + b * 512:8704 + b * 512], bank[b][:, :], ACT.Square, accum_out=small[:, b:b + 1]).then_inc(fin_sq, 1)
                if b % 4 == 3:
                    tt = b // 4
                    ac.wait_ge(fin_sum, tt + 1)
                    rsqrt(small[:, 8 + tt:9 + tt], small[:, 10 + tt:11 + tt], D, fin_log, fin_rstd, tt + 1)

        @block.vector
        def _(dv):
            vec = nc.vector

            def rest_block(m, s, raw_slot):
                dv.wait_ge(hi_ready, m + 1)
                vec.tensor_tensor(lo[:, s % 2, :], raw[:, raw_slot, :], hi[:, s % 2, :].bitcast(F32), ALU.subtract).then_inc(lo_ready, 1)

            def rest_static(m):
                rest_block(m, m, raw_at(m) % RAW)

            def rest_act(hi_count, k0, k1, src):
                dv.wait_ge(act_hi_ready, hi_count)
                vec.tensor_tensor(act[:, k0:k1, T:2 * T], src, act[:, k0:k1, 0:T].bitcast(F32), ALU.subtract).then_inc(act_lo_ready, 1)

            def scaled(m, s, dst):
                dv.wait_ge(block_done, m + 1)
                vec.tensor_tensor(dst, bank[s % 2][:, 0:T], rstd[:, :], ALU.mult).then_inc(acc_evacuated, 1)

            vec.memset(eps, EPS).then_inc(consts_ready, 1)
            vec.memset(rb[N_BUCKETS:N_BUCKETS + 1, :], NEG).then_inc(consts_ready, 1)
            dv.wait_ge(bias_in_loaded, 32)
            dv.wait_ge(consts_ready, 2)
            vec.tensor_copy(rb_wide[0:N_BUCKETS + 1, :, :],
                            rb[0:N_BUCKETS + 1, :].unsqueeze(2).to_broadcast([N_BUCKETS + 1, 8, P])).then_inc(rb_wide_ready, 1)
            dv.wait_ge(gains_loaded, 16)
            for k in range(KT):
                if k % 8 == 0:
                    dv.wait_ge(x_loaded[k // 8], 16)
                dv.wait_ge(act_hi_ready, k + 1)
                vec.scalar_tensor_tensor(out=act[:, k, T:2 * T], in0=hT[:, k * T:(k + 1) * T], scalar=g1[:, k:k + 1],
                                         in1=act[:, k, 0:T].bitcast(F32), op0=ALU.mult, op1=ALU.subtract).then_inc(act_lo_ready, 1)
            rest_static(0)
            for m in range(1, PAIRS):
                rest_static(m)
                if m == 1:
                    dv.wait_ge(sq_ready, 1)
                    vec.tensor_reduce(sq_sum[:, 0:T], sq.rearrange("p k t -> p t k"), AX.X, ALU.add).then_inc(sq_summed, 1)
                    dv.wait_ge(rstd_ready, 1)
                scaled(m - 1, m - 1, tile(m - 1))
                if m == 2:
                    dv.wait_ge(wg_loaded, 16)
                    dv.wait_ge(wg_hi_ready, 1)
                    vec.tensor_tensor(wg_r[:, :, 24:48], wg, wg_r[:, :, 0:24].bitcast(F32), ALU.subtract).then_inc(wg_lo_ready, 1)
                if m == 2:
                    dv.wait_ge(cbias_ready, 1)
                    for tt in range(2):
                        windows = bank[6][:, 64 * (1 - tt):64 * (1 - tt) + 8 * NCMP].rearrange("p (c h) -> p c h", h=8)
                        vec.tensor_copy(cbias[:, tt, 0:NCMP, :], windows).then_inc(cbias_copied, 1)
                if m == 4:
                    dv.wait_ge(gate_acc, 1)
                    vec.tensor_tensor(gate_T, bank[7][0:24, T:2 * T], rstd[0:24, :], ALU.mult).then_inc(gate_scaled, 1)
                if m == 5:
                    vec.memset(hid_wide, 0.0).then_inc(zeroed, 1)
                    vec.memset(pc, 0.0).then_inc(zeroed, 1)
                if m == 6:
                    dv.wait_ge(gate_exp, 2)
                    vec.tensor_scalar(gate[:, :, :], gate[:, :, :], 1.0, None, ALU.add).then_inc(gate_step, 1)
                    dv.wait_ge(gate_step, 1)
                    vec.reciprocal(gate[:, :, :], gate[:, :, :]).then_inc(gate_ready, 1)
                if m == 7:
                    dv.wait_ge(mid_loaded, 48)
                    for kind in range(2):
                        for g in range(GROUPS):
                            dv.wait_ge(acc_evacuated, (KC, VC)[kind] + g + 1)
                            rows_of = tile((KC, VC)[kind] + g).rearrange("p (c l) -> p l c", l=CMP_STRIDE)
                            for lh in range(2):
                                ls = slice(16 * lh, 16 * lh + 16)
                                vec.tensor_tensor(blk[:, kind, ls, g * NCMP:(g + 1) * NCMP], rows_of[:, :, lh:lh + NCMP],
                                                  pe_cols[:, kind * CMP_LEN + 16 * lh:kind * CMP_LEN + 16 * lh + 16]
                                                  .unsqueeze(2).to_broadcast([P, 16, NCMP]), ALU.add).then_inc(blk_ready, 1)
            with dv.Fori(0, 4) as lap:
                for r in range(2):
                    rest_block(2 * lap + (PAIRS + r), r, 2 * r)
                    scaled(2 * lap + (PAIRS + r - 1), r - 1, proj[:, bass.ds(2 * T * lap + (PAIRS + r - 1) * T, T)])
            rest_static(16)
            scaled(15, 15, tile(15))
            dv.wait_ge(hid_turned, 1)
            vec.tensor_copy(hid[:, :, :, :].rearrange("p k f n -> p (k f) n")[:, :, 0:30],
                            bank[4][:, 0:P].rearrange("p (e n) -> p e n", e=4)[:, :, 0:30]).then_inc(hid_ready, 1)
            dv.wait_ge(hid_ready, 1)
            dv.wait_ge(zeroed, 2)
            for f in range(2):
                vec.tensor_copy(hid_wide[:, f, :].rearrange("p (g h c) -> p g h c", g=2, c=CPAD)[:, :, :, 0:NCMP],
                                hid[:, 1, f, 0:30].rearrange("p (g c) -> p g c", g=2).unsqueeze(2).to_broadcast([P, 2, HPG, NCMP])
                                ).then_inc(wide_ready, 1)
            rest_static(17)
            scaled(16, 16, tile(16))
            dv.wait_ge(vc_acc, 1)
            for h in range(NSA_HEADS):
                vec.tensor_scalar(vch[:, h, :], bank[5][:, 0:DH], head_mask[:, h:h + 1], None, ALU.mult).then_inc(vch_ready, 1)
            rest_static(18)
            scaled(17, 17, tile(17))
            dv.wait_ge(cs_acc, 1)
            dv.wait_ge(cbias_copied, 2)
            pcv = pc[:, :, :, 0:NCMP]
            pcf = pcv.rearrange("p t h c -> p (t h) c")
            mx, sm = small[:, 0:16], small[:, 16:32]
            for tt in range(2):
                vec.scalar_tensor_tensor(out=pcv[:, tt], in0=bank[6][:, tt * P:(tt + 1) * P].rearrange("p (h c) -> p h c", h=8)[:, :, 0:NCMP],
                                         scalar=SCALE, in1=cbias[:, tt, 0:NCMP, :].rearrange("p c h -> p h c"),
                                         op0=ALU.mult, op1=ALU.add).then_inc(cstep, 1)
            dv.wait_ge(cstep, 2)
            vec.tensor_reduce(mx, pcf, AX.X, ALU.max).then_inc(cstep, 1)
            dv.wait_ge(cstep, 3)
            vec.tensor_scalar(sm, mx, -1.0, None, ALU.mult).then_inc(cstep, 1)
            dv.wait_ge(cstep, 4)
            vec.tensor_tensor(pcf, pcf, sm.unsqueeze(2).to_broadcast([P, 16, NCMP]), ALU.add).then_inc(cstep, 1)
            rest_static(19)
            scaled(18, 18, tile(18))
            dv.wait_ge(cexp, 1)
            vec.tensor_tensor(pcv, pcv, seen[:, :, 0:NCMP].unsqueeze(2).to_broadcast([P, 2, 8, NCMP]), ALU.mult).then_inc(cstep, 1)
            dv.wait_ge(cstep, 6)
            vec.tensor_reduce(sm, pcf, AX.X, ALU.add).then_inc(cstep, 1)
            dv.wait_ge(cstep, 7)
            vec.tensor_scalar(sm, sm, 1e-30, None, ALU.max).then_inc(cstep, 1)
            dv.wait_ge(cstep, 8)
            vec.reciprocal(sm, sm).then_inc(cstep, 1)
            dv.wait_ge(cstep, 9)
            dv.wait_ge(gate_ready, 1)
            vec.tensor_tensor(sm.rearrange("p (t h) -> p t h", t=2), sm.rearrange("p (t h) -> p t h", t=2),
                              gate[:, :, :].rearrange("p t (h b) -> p t h b", b=3)[:, :, :, 0], ALU.mult).then_inc(cstep, 1)
            dv.wait_ge(cstep, 10)
            vec.tensor_tensor(pcf, pcf, sm.unsqueeze(2).to_broadcast([P, 16, NCMP]), ALU.mult).then_inc(pc_ready, 1)

            def soft_in(u):
                h, st = u // 2, stats(u)
                dv.wait_ge(s_acc, u + 1)
                if u >= 2:
                    dv.wait_ge(pT_acc, u - 1)
                vec.scalar_tensor_tensor(out=pw[:, u % 2, :], in0=bank[2 + u % 2][:, 0:3 * P], scalar=SCALE,
                                         in1=bias[:, h, :], op0=ALU.mult, op1=ALU.add).then_inc(s_biased, 1)
                dv.wait_ge(s_biased, u + 1)
                vec.tensor_reduce(st[:, 0:1], pw[:, u % 2, 0:P], AX.X, ALU.max)
                vec.tensor_reduce(st[:, 1:2], pw[:, u % 2, P:3 * P], AX.X, ALU.max).then_inc(s_max, 1)
                dv.wait_ge(s_max, u + 1)
                vec.tensor_scalar(st[:, 2:4], st[:, 0:2], -1.0, None, ALU.mult).then_inc(s_nmax, 1)

            def soft_out(u):
                h, branch, st = u // 2, u % 2, stats(u)
                dv.wait_ge(p_exp, u + 1)
                vec.reciprocal(st[:, 4:6], st[:, 4:6]).then_inc(p_rec, 1)
                dv.wait_ge(p_rec, u + 1)
                vec.tensor_tensor(st[:, 6:8], st[:, 4:6], gate[:, :, 3 * h + branch + 1], ALU.mult).then_inc(p_coef, 1)
                dv.wait_ge(p_coef, u + 1)
                vec.tensor_scalar(pw[:, u % 2, 0:P], pw[:, u % 2, 0:P], st[:, 6:7], None, ALU.mult)
                vec.tensor_scalar(pw[:, u % 2, P:3 * P], pw[:, u % 2, P:3 * P], st[:, 7:8], None, ALU.mult).then_inc(p_ready, 1)

            def rotate(i):
                dv.wait_ge(swapped, i + 1)
                if i:
                    dv.wait_ge(rotated, i)
                tmp = wmt_flat.rearrange("p (f t) -> p f t", f=2)
                qk = tile(RQ + 2 * i, 2).rearrange("p (f t) -> p f t", f=2)
                vec.tensor_tensor(tmp, bank[2 + i % 2][:, :].rearrange("p (f t) -> p f t", f=2),
                                  sin.unsqueeze(1).to_broadcast([P, 2, T]), ALU.mult).then_inc(rot_sin, 1)
                vec.tensor_tensor(qk, qk, cos.unsqueeze(1).to_broadcast([P, 2, T]), ALU.mult).then_inc(rot_cos, 1)
                dv.wait_ge(rot_sin, i + 1)
                dv.wait_ge(rot_cos, i + 1)
                vec.tensor_tensor(qk, qk, tmp, ALU.add).then_inc(rotated, 1)

            def add_residual(m, s, where):
                dv.wait_ge(block_done, m + 1)
                vec.tensor_tensor(where, bank[s % 2][:, :], where, ALU.add).then_inc(acc_evacuated, 1)

            for m in range(UNIT0, M_OUT2):
                rest_static(m)
                if m <= M_OUT1:
                    scaled(m - 1, m - 1, tile(m - 1))
                    if m == M_OUT1:
                        for k in range(0, 8, 2):
                            rest_act(KT + 1 + k // 2, 8 + k, 10 + k, tile(NQ + k, 2).rearrange("p (k t) -> p k t", k=2))
                else:
                    if m == M_OUT1 + 1:
                        dv.wait_ge(xres_loaded, 16)
                    add_residual(m - 1, m - 1, res[:, (m - 1 - M_OUT1) * 512:(m - M_OUT1) * 512])
                u = m - UNIT0 - 1
                if 0 <= u < units:
                    if u == 0:
                        dv.wait_ge(bias_loaded, 32)
                    soft_in(u)
                    soft_out(u)
                if ROT < m <= ROT + 2:
                    rotate(2 * (m - ROT) - 2)
                    rotate(2 * (m - ROT) - 1)
                if m == TURN_V + 4:
                    dv.wait_ge(orstd, 1)
                    for h in range(NSA_HEADS):
                        vec.scalar_tensor_tensor(out=tile(NQ + h), in0=tile(NQ + h), scalar=out_g[:, h:h + 1], in1=tile(h),
                                                 op0=ALU.mult, op1=ALU.mult).then_inc(mixed, 1)
                i = m - RET0 - 1
                if 0 <= i < 4:
                    dv.wait_ge(decay_loaded, 32)
                    if i == 0:
                        dv.wait_ge(pT_acc, units)
                    for h in (2 * i, 2 * i + 1):
                        dv.wait_ge(r_acc, h + 1)
                        if h >= 2:
                            dv.wait_ge(y_acc, h - 1)
                        vec.tensor_tensor(pw[:, h % 2, 0:T], bank[2 + h % 2][:, 0:T], decay[:, h * T:(h + 1) * T], ALU.mult)
                        vec.tensor_tensor(pw[:, h % 2, T:3 * P], bank[2 + h % 2][:, T:3 * P], decay[:, h * T:h * T + P],
                                          ALU.mult).then_inc(r_decayed, 1)
                if 2 <= i <= 5:
                    c = i - 2
                    dv.wait_ge(yc_acc, c + 1)
                    vec.tensor_copy(tile(RV + 2 * c, 2), bank[6][:, :]).then_inc(yc_copied, 1)
                for c in {7: (0, 1), 8: (2, 3)}.get(i, ()):
                    dv.wait_ge(yrstd, c + 1)
                    dv.wait_ge(yc_copied, c + 1)
                    dv.wait_ge(silu_ready, 1)
                    for f in (2 * c, 2 * c + 1):
                        rs = ysq(c)[:, (f % 2) * T:(f % 2 + 1) * T]
                        vec.scalar_tensor_tensor(out=tile(RV + f), in0=tile(RV + f), scalar=gn_g[:, f:f + 1], in1=rs,
                                                 op0=ALU.mult, op1=ALU.mult).then_inc(ynorm, 1)
                    dv.wait_ge(ynorm, 4 * c + 2)
                    for f in (2 * c, 2 * c + 1):
                        vec.tensor_tensor(tile(RV + f), tile(RV + f), tile(RG + f), ALU.mult).then_inc(ynorm, 1)
                if i == 9:
                    rest_act(KT + 5, 0, 8, tile(RV, 8).rearrange("p (k t) -> p k t", k=8))

            for c in range(9):
                rest_static(M_OUT2 + c)
                x = (c + 7) % 8
                add_residual(M_OUT2 + c - 1, c - 1, res[:, x * 512:(x + 1) * 512])
                if 0 < c < 8:
                    dv.wait_ge(sq_ready, c + 1)
                    if c > 1:
                        dv.wait_ge(sq_summed, c)
                    sq_c = hT[:, (c - 1) * 512:c * 512]
                    if c == 1:
                        vec.tensor_copy(sq_sum, sq_c).then_inc(sq_summed, 1)
                    else:
                        vec.tensor_tensor(sq_sum, sq_sum, sq_c, ALU.add).then_inc(sq_summed, 1)
            dv.wait_ge(rstd_ready, 2)
            dv.wait_ge(acc_evacuated, M_WQ)
            for k in range(KT + 4):
                if k < KT:
                    vec.scalar_tensor_tensor(out=xn[:, k, :], in0=res[:, k * T:(k + 1) * T], scalar=g2[:, k:k + 1],
                                             in1=rstd[:, :], op0=ALU.mult, op1=ALU.mult).then_inc(xn_ready, 1)
                if k % 4 == 3 and k > 4:
                    c = k // 4 - 1
                    rest_act(KT + 6 + c, 4 * c, 4 * c + 4, xn[:, 4 * c:4 * c + 4, :])
            for s in range(1, RAW):
                rest_static(M_WQ + s)
            with dv.Fori(1, KT // RAW) as lap:
                for s in range(RAW):
                    rest_block(RAW * lap + (M_WQ + s), s, s)

            done = {"route": 0, "u": 0}

            def step(ins):
                done["route"] += 1
                ins.then_inc(route, 1)

            def routed():
                dv.wait_ge(route, done["route"])

            def u_rest():
                if done["u"] < ROUTED:
                    rest_static(M_PEER + done["u"])
                    done["u"] += 1

            def best16(vals, idx, src, rest_within=False):
                for v, l in zip(vals, src):
                    step(vec.max(v[:, 0:8], l))
                routed()
                for v, x, l in zip(vals, idx, src):
                    step(vec.max_index(x[:, 0:8], v[:, 0:8], l))
                routed()
                for v, l in zip(vals, src):
                    step(vec.match_replace(l, v[:, 0:8], l, LOWEST))
                if rest_within:
                    u_rest()
                routed()
                for v, l in zip(vals, src):
                    step(vec.max(v[:, 8:16], l))
                routed()
                for v, x, l in zip(vals, idx, src):
                    step(vec.max_index(x[:, 8:16], v[:, 8:16], l))
                routed()

            u_rest()
            u_rest()
            for pair in range(2 * PH):
                tt, g = pair // PH, 2 * (pair % PH)
                dv.wait_ge(q_copied, pair // 2 + 1)
                best16([top[:, tt, g + s, :] for s in range(2)], [top_i[:, tt, g + s, :] for s in range(2)],
                       [sc[:, tt, g + s, :] for s in range(2)])
                u_rest()
            step(vec.tensor_copy(top_f.rearrange("p t h s k -> p (t h s k)"), top_i.rearrange("p t g k -> p (t g k)")))
            for tt in range(2):
                tv = top[:, tt].rearrange("p (h s) k -> p h s k", s=2)
                step(vec.tensor_tensor(cand[:, tt], tv[:, :, 0, :].unsqueeze(3).to_broadcast([P, PH, PK, PK]),
                                       tv[:, :, 1, :].unsqueeze(2).to_broadcast([P, PH, PK, PK]), ALU.add))
                u_rest()
            routed()
            ci4 = ci.rearrange("p (t h k) -> p t h k", t=2, h=PH)
            for pair in range(PH):
                tt, h = pair // 4, 2 * (pair % 4)
                best16([cs[:, tt, h + x, :] for x in range(2)], [ci4[:, tt, h + x, :] for x in range(2)],
                       [cand[:, tt, h + x].rearrange("p a b -> p (a b)") for x in range(2)], rest_within=pair % 2 == 0)
                u_rest()
            cs_f = cs.rearrange("p t h k -> p (t h) k")
            gates = choice[:, 2].rearrange("p t (h k) -> p (t h) k", h=PH)
            step(vec.tensor_tensor(gates, cs_f, cs_f[:, :, 0:1].to_broadcast([P, 2 * PH, PK]), ALU.subtract))
            assert done["route"] == ROUTE_GATE
            step(vec.tensor_scalar(cab_u[:, 0], ci, 4, None, ALU.logical_shift_right))
            step(vec.tensor_scalar(cab_u[:, 1], ci, 15, None, ALU.bitwise_and))
            routed()
            step(vec.tensor_copy(cab.rearrange("p s n -> p (s n)"), cab_u.rearrange("p s n -> p (s n)")))
            routed()
            for side in range(2):
                for tt in range(2):
                    step(vec.tensor_tensor(pick[:, tt], cab[:, side, tt * P:(tt + 1) * P].unsqueeze(2).to_broadcast([P, P, PK]),
                                           iota[:, 0:PK].unsqueeze(1).to_broadcast([P, P, PK]), ALU.is_equal))
                    u_rest()
                    routed()
                    pv = pick[:, tt].rearrange("p (h k) a -> p h k a", h=PH)
                    step(vec.tensor_tensor(pv, pv, top_f[:, tt, :, side, :].unsqueeze(2).to_broadcast([P, PH, PK, PK]), ALU.mult))
                    u_rest()
                    routed()
                    step(vec.tensor_reduce(choice[:, side, tt], pick[:, tt], AX.X, ALU.add))
                    u_rest()
                    routed()
            dv.wait_ge(route_exp, 1)
            step(vec.tensor_reduce(small[:, 0:16], gates, AX.X, ALU.add))
            routed()
            step(vec.reciprocal(small[:, 0:16], small[:, 0:16]))
            routed()
            vec.tensor_tensor(gates, gates, small[:, 0:16].unsqueeze(2).to_broadcast([P, 2 * PH, PK]), ALU.mult).then_inc(choices_ready, 1)
            while done["u"] < ROUTED:
                u_rest()

            rest_static(M_PEER + ROUTED)
            dv.wait_ge(ch_copied, 3)

            def onehots(b):
                if b >= 2:
                    dv.wait_ge(gate_rows, b - 1)
                vec.tensor_tensor(onehot[:, b % 2, 0, :, :], iota.unsqueeze(1).to_broadcast([P, 8, P]),
                                  choiceT[:, 0, 8 * b:8 * b + 8].unsqueeze(2).to_broadcast([P, 8, P]), ALU.is_equal)
                for t in range(8 * b, 8 * b + 8):
                    last = vec.tensor_scalar(onehot[:, b % 2, 1, t % 8, :], iota, choiceT[:, 1, t:t + 1], choiceT[:, 2, t:t + 1],
                                             ALU.is_equal, ALU.mult)
                last.then_inc(onehots_ready, 1)

            onehots(0)
            for r in range(GATE_BLOCKS):
                if r < GATE_BLOCKS - 1:
                    rest_static(M_PEER + ROUTED + r + 1)
                for b in batches_after(r):
                    if b + 1 < BATCHES:
                        onehots(b + 1)

            for half in range(2):
                if half:
                    with dv.Fori(0, HALF // RAW) as lap:
                        for s in range(RAW):
                            rest_block(RAW * lap + (m_u(1) + s), s, s)

                def gate_hidden(mv, r, arena_at):
                    if r % GROUP_J == 0:
                        dv.wait_ge(gate_loaded[r // GROUP_J], mv + (HALF * half + 16 - r))
                    vec.tensor_tensor(wmt[:, r % 2, :], arena[:, arena_at],
                                      gs[:, r // GROUP_J, :].rearrange("p (t j) -> p t j", j=GROUP_J)[:, :, r % GROUP_J],
                                      ALU.mult).then_inc(gated, 1)

                def split_gated(mv, r):
                    dv.wait_ge(wm_hi, mv + (HALF * half + 1))
                    vec.tensor_tensor(wm[:, r % 2, 1, :], wmt[:, r % 2, :], wm[:, r % 2, 0, :].bitcast(F32),
                                      ALU.subtract).then_inc(wm_lo, 1)

                for r in range(2 * GROUP_J):
                    dv.wait_ge(acc_evacuated, M_PEER + HALF * (half + 1) - (r == 0))
                    gate_hidden(r, r, slice(r * T, (r + 1) * T))
                    rest_static(m_v(half) + r)
                    split_gated(r, r)
                with dv.Fori(1, HALF // (2 * GROUP_J)) as lap:
                    for r in range(2 * GROUP_J):
                        mv = 2 * GROUP_J * lap + r
                        gate_hidden(mv, r, bass.ds(2 * GROUP_J * T * lap + r * T, T))
                        rest_block(2 * GROUP_J * lap + (m_v(half) + r), r, r % RAW)
                        split_gated(mv, r)
            dv.wait_ge(gf_loaded, 16)
            for tt in range(2):
                dv.wait_ge(fin_sq, 4 * tt + 4)
                vec.tensor_reduce(small[:, 8 + tt:9 + tt], small[:, 4 * tt:4 * tt + 4], AX.X, ALU.add).then_inc(fin_sum, 1)
                dv.wait_ge(fin_rstd, tt + 1)
                for b in range(4 * tt, 4 * tt + 4):
                    vec.scalar_tensor_tensor(out=arena[:, b * 512:(b + 1) * 512], in0=bank[b][:, :], scalar=small[:, 10 + tt:11 + tt],
                                             in1=hT[:, (b % 4) * 512:(b % 4 + 1) * 512], op0=ALU.mult, op1=ALU.mult).then_inc(fin_ready, 1)


def kernel(x, norm1_g, w_in, rel_bias, ret_gn_g, cmp_pe, cmp_w1, cmp_w2, nsa_out_g, w_out, norm2_g, peer_wq,
           peer_subkeys, peer_u, peer_v, norm_f_g):
    import numpy as _np
    import concourse.bacc as _bacc
    from concourse.bass_utils import run_bass_kernel_spmd as _run

    c = _np.ascontiguousarray

    def blocks(w):
        k, n = w.shape
        return c(_np.asarray(w).reshape(k // P, P, n // P, P).transpose(2, 1, 0, 3).reshape(n // P, P, k))

    def cols(g):
        return _np.asarray(g).reshape(-1, P).T

    x, w_in = _np.asarray(x), _np.asarray(w_in)[0]
    base, mid, decay, onehots = constants()
    cmp_pe, cmp_w1, cmp_w2 = (_np.asarray(v)[0] for v in (cmp_pe, cmp_w1, cmp_w2))
    wide = W_IN_TILES * P
    arrays = {
        "xT": c(x[0].reshape(T, KT, P).transpose(2, 1, 0).reshape(P, KT * T)),
        "base": base, "mid": mid, "decay": decay, "onehots": onehots,
        "gains": c(_np.concatenate([cols(norm1_g), cols(norm2_g), cols(ret_gn_g), cols(nsa_out_g)], 1)),
        "w_gate": c(w_in[:, wide:].reshape(KT, P, -1).transpose(1, 0, 2)),
        "rel_bias": c(rel_bias),
        "subkeys": c(_np.asarray(peer_subkeys)[0].transpose(2, 0, 1)),
        "w_in": c(blocks(w_in[:, :wide])[TILE_ORDER]),
        "cmp_w2": c(cmp_w2.reshape(2, 2, P, DH).transpose(2, 0, 1, 3).reshape(P, 4 * DH)),
        "cmp_pe": c(cmp_pe.transpose(2, 0, 1).reshape(P, 2 * CMP_LEN)),
        "cmp_w1": c(cmp_w1.reshape(2, 4, 8, P, 2 * P).transpose(0, 1, 3, 2, 4).reshape(8, P, D)),
        "w_out": c(_np.asarray(w_out)[0].reshape(2, 8, P, 8, 2, P)[::-1].transpose(0, 3, 2, 4, 1, 5).reshape(KT, P, D)),
        "wq": blocks(_np.asarray(peer_wq)[0]),
        "u": c(_np.asarray(peer_u)[0].reshape(NKEYS, NKEYS, KT, P).transpose(1, 3, 2, 0).reshape(NKEYS, P, D)),
        "v": c(_np.asarray(peer_v)[0].reshape(NKEYS, NKEYS, D)),
        "norm_f": c(_np.broadcast_to(_np.asarray(norm_f_g)[None, :], (P, D))),
    }
    nc = _bacc.Bacc("TRN2", target_bir_lowering=False, num_devices=1)
    aps = {k: nc.dram_tensor(f"in_{k}", v.shape, mybir.dt.from_np(v.dtype), kind="ExternalInput").ap() for k, v in arrays.items()}
    out = nc.dram_tensor("out", (T, D), F32, kind="ExternalOutput").ap()
    build(nc, aps, out)
    r = _run(nc, [{f"in_{k}": v for k, v in arrays.items()}], core_ids=[0])
    return r.results[0]["out"].reshape(1, T, D)
```
